# Optimizing a Trainium2 kernel written in Bass

```python
import jax, jax.numpy as jnp
from jax import lax
import numpy as np

D_MODEL = 1024
BATCH = 1
SEQ = 512
DEPTH = 1
DEC_BATCH = 8
DEC_SEQ = 8
PAST_LEN = 2048
PAGE_SIZE = 128

N_HEADS = 8
N_KV = 2
HPG = N_HEADS // N_KV
HEAD_DIM = 64
ATTN_WIDTH = N_HEADS * HEAD_DIM
POOL_WIDTH = D_MODEL - ATTN_WIDTH
POOL_WINDOWS = (2, 4, 8, 16)
N_POOL_GROUPS = len(POOL_WINDOWS)
POOL_GROUP = POOL_WIDTH // N_POOL_GROUPS
POOL_HIST = max(POOL_WINDOWS) - 1
BLK = 64
N_SELECT = 16
WINDOW = 512
CMP_HIDDEN = 2 * HEAD_DIM
D_FF = 4 * D_MODEL
Q_BLOCK = 128
KV_WIDTH = N_KV * 2 * HEAD_DIM
PROJ_WIDTH = ATTN_WIDTH + 3 * KV_WIDTH + 3 * N_HEADS + POOL_WIDTH
SPLITS = (ATTN_WIDTH, ATTN_WIDTH + KV_WIDTH, ATTN_WIDTH + 2 * KV_WIDTH,
          ATTN_WIDTH + 3 * KV_WIDTH, ATTN_WIDTH + 3 * KV_WIDTH + 3 * N_HEADS)
BLOCKS_PER_PAGE = PAGE_SIZE // BLK
SCALE = HEAD_DIM ** -0.5
FORCE_SCORE = float(HPG + 1)
NORM_EPS = 1e-6
NEG = -1e30

kernel_name = "hymba_nsa_poolformer_decoder_step"

def rms_norm(x, g):
    xf = x.astype(jnp.float32)
    y = xf * lax.rsqrt(jnp.mean(xf * xf, axis=-1, keepdims=True) + NORM_EPS)
    return (y * g.astype(jnp.float32)).astype(x.dtype)

def alibi_slopes():
    h = jnp.arange(N_HEADS, dtype=jnp.float32) + 1.0
    return jnp.exp2(-8.0 * h / N_HEADS).reshape(N_KV, HPG)

def masked_softmax(s, mask):
    s = jnp.where(mask, s, NEG)
    m = jnp.max(s, axis=-1, keepdims=True)
    p = jnp.where(mask, jnp.exp(s - m), 0.0)
    return p / jnp.maximum(jnp.sum(p, axis=-1, keepdims=True), 1e-30)

def split_proj(hp):
    B, T, _ = hp.shape
    q, kc, ks, kw, gl, u = jnp.split(hp, list(SPLITS), axis=-1)
    kvs = lambda a: a.reshape(B, T, N_KV, 2, HEAD_DIM)
    gates = jax.nn.sigmoid(gl.astype(jnp.float32)).reshape(B, T, 3, N_KV, HPG)
    return q.reshape(B, T, N_KV, HPG, HEAD_DIM), kvs(kc), kvs(ks), kvs(kw), gates, u

def compress_blocks(kv, pe, w1, w2):
    B, L = kv.shape[:2]
    blocks = kv.reshape(B, L // BLK, BLK, N_KV, 2, HEAD_DIM) + pe[:, None]
    hid = jax.nn.gelu(jnp.einsum('bnlgcd,cldh->bngch', blocks, w1))
    return jnp.einsum('bngch,chd->bngcd', hid, w2)

def cmp_attend(q, pos_q, comp, slopes):
    nb = comp.shape[1]
    end = (jnp.arange(nb) + 1) * BLK - 1
    dist = (pos_q[:, None] - end[None, :]).astype(jnp.float32)
    s = jnp.einsum('btgpd,bngd->btgpn', q, comp[..., 0, :]).astype(jnp.float32) * SCALE
    s = s - slopes[None, None, :, :, None] * dist[None, :, None, None, :]
    p = masked_softmax(s, (dist >= 0)[None, :, None, None, :])
    o = jnp.einsum('btgpn,bngd->btgpd', p.astype(comp.dtype), comp[..., 1, :])
    return o, p

def select_blocks(imp, pos_q, nb):
    jj = jnp.arange(nb)[None, :]
    cur = (pos_q // BLK)[:, None]
    forced = (jj == 0) | (jj == cur) | (jj == cur - 1)
    score = jnp.where(forced[None, :, None, :], FORCE_SCORE, imp)
    score = jnp.where((jj > cur)[None, :, None, :], -1.0, score)
    _, idx = lax.top_k(score, min(N_SELECT, nb))
    return idx

def gather_local_blocks(blocks, idx):
    B = blocks.shape[0]
    return blocks[jnp.arange(B)[:, None, None, None], jnp.arange(N_KV)[None, None, :, None], idx]

def slc_attend(q, pos_q, kv_sel, idx, slopes):
    B, Tq, G, n = idx.shape
    S = n * BLK
    k = kv_sel[..., 0, :].reshape(B, Tq, G, S, HEAD_DIM)
    v = kv_sel[..., 1, :].reshape(B, Tq, G, S, HEAD_DIM)
    pos_k = (idx[..., None] * BLK + jnp.arange(BLK)).reshape(B, Tq, G, S)
    dist = (pos_q[None, :, None, None] - pos_k).astype(jnp.float32)
    s = jnp.einsum('btgpd,btgsd->btgps', q, k).astype(jnp.float32) * SCALE
    s = s - slopes[None, None, :, :, None] * dist[:, :, :, None, :]
    p = masked_softmax(s, (dist >= 0)[:, :, :, None, :])
    return jnp.einsum('btgps,btgsd->btgpd', p.astype(v.dtype), v)

def win_attend(q, pos_q, kv, pos_k, slopes):
    dist_i = pos_q[:, None] - pos_k[None, :]
    mask = (dist_i >= 0) & (dist_i < WINDOW) & (pos_k >= 0)[None, :]
    dist = dist_i.astype(jnp.float32)
    s = jnp.einsum('btgpd,bsgd->btgps', q, kv[..., 0, :]).astype(jnp.float32) * SCALE
    s = s - slopes[None, None, :, :, None] * dist[None, :, None, None, :]
    p = masked_softmax(s, mask[None, :, None, None, :])
    return jnp.einsum('btgps,bsgd->btgpd', p.astype(kv.dtype), kv[..., 1, :])

def nsa_heads(q, pos_q, comp, gather_sel, kv_win, pos_win, gates, slopes):
    o_c, p_c = cmp_attend(q, pos_q, comp, slopes)
    idx = select_blocks(jnp.sum(p_c, axis=3), pos_q, comp.shape[1])
    o_s = slc_attend(q, pos_q, gather_sel(idx), idx, slopes)
    o_w = win_attend(q, pos_q, kv_win, pos_win, slopes)
    o = (gates[:, :, 0, :, :, None] * o_c + gates[:, :, 1, :, :, None] * o_s
         + gates[:, :, 2, :, :, None] * o_w)
    return o.astype(q.dtype)

def pool_mix(u_ext, pos, w_pool, pool_scale):
    B, L, _ = u_ext.shape
    T = pos.shape[0]
    uf = u_ext.astype(jnp.float32)
    c = jnp.pad(jnp.cumsum(uf, axis=1), ((0, 0), (1, 0), (0, 0)))
    own = uf[:, L - T:]
    outs = []
    for gi, w in enumerate(POOL_WINDOWS):
        sl = slice(gi * POOL_GROUP, (gi + 1) * POOL_GROUP)
        hi = c[:, L - T + 1:, sl]
        lo = c[:, L - T + 1 - w: L + 1 - w, sl]
        cnt = jnp.minimum(w, pos + 1).astype(jnp.float32)[None, :, None]
        outs.append((hi - lo) / cnt - own[..., sl])
    d = jnp.stack(outs, axis=2).astype(u_ext.dtype)
    y = jnp.einsum('btgc,gcd->btgd', d, w_pool).reshape(B, T, POOL_WIDTH)
    return y * pool_scale

def merge_and_mlp(x, o, pool_out, w_out, g_mlp, w_up, w_down):
    B, T, _ = x.shape
    mix = jnp.concatenate([o.reshape(B, T, ATTN_WIDTH).astype(x.dtype),
                           pool_out.astype(x.dtype)], axis=-1)
    h = x + mix @ w_out
    a = jnp.square(jax.nn.relu(rms_norm(h, g_mlp) @ w_up))
    return h + a @ w_down

def prompt_layer(x, g_attn, w_in, cmp_pe, cmp_w1, cmp_w2, w_pool, pool_scale,
                 w_out, g_mlp, w_up, w_down, slopes):
    B, T, _ = x.shape
    q, kv_c, kv_s, kv_w, gates, u = split_proj(rms_norm(x, g_attn) @ w_in)
    comp = compress_blocks(kv_c, cmp_pe, cmp_w1, cmp_w2)
    blocks_s = kv_s.reshape(B, T // BLK, BLK, N_KV, 2, HEAD_DIM).transpose(0, 3, 1, 2, 4, 5)
    kv_w_pad = jnp.pad(kv_w, ((0, 0), (WINDOW, 0), (0, 0), (0, 0), (0, 0)))
    nqb = T // Q_BLOCK
    to_blocks = lambda a: a.reshape((B, nqb, Q_BLOCK) + a.shape[2:]).swapaxes(0, 1)

    def per_block(args):
        i, qb, gb = args
        start = i * Q_BLOCK
        pos_b = start + jnp.arange(Q_BLOCK)
        kvw = lax.dynamic_slice_in_dim(kv_w_pad, start, Q_BLOCK + WINDOW, axis=1)
        pos_w = start - WINDOW + jnp.arange(Q_BLOCK + WINDOW)
        return nsa_heads(qb, pos_b, comp, lambda idx: gather_local_blocks(blocks_s, idx),
                         kvw, pos_w, gb, slopes)

    o = lax.map(per_block, (jnp.arange(nqb), to_blocks(q), to_blocks(gates)))
    o = o.swapaxes(0, 1).reshape(B, T, N_KV, HPG, HEAD_DIM)
    pos = jnp.arange(T)
    p = pool_mix(jnp.pad(u, ((0, 0), (POOL_HIST, 0), (0, 0))), pos, w_pool, pool_scale)
    h = merge_and_mlp(x, o, p, w_out, g_mlp, w_up, w_down)
    wk = min(WINDOW, T)
    return h, (kv_c, kv_s, kv_w[:, T - wk:], u[:, T - POOL_HIST:])

def sample_layer(x, cache_cmp, cache_slc, state_win, state_pool, page_table,
                 g_attn, w_in, cmp_pe, cmp_w1, cmp_w2, w_pool, pool_scale,
                 w_out, g_mlp, w_up, w_down, slopes):
    B, T, _ = x.shape
    past = page_table.shape[1] * PAGE_SIZE
    nb_past = past // BLK
    nb_new = -(-T // BLK)
    pos = past + jnp.arange(T)
    q, kv_c, kv_s, kv_w, gates, u = split_proj(rms_norm(x, g_attn) @ w_in)
    pad_new = ((0, 0), (0, nb_new * BLK - T), (0, 0), (0, 0), (0, 0))
    past_c = cache_cmp[page_table].reshape(B, past, N_KV, 2, HEAD_DIM)
    comp = jnp.concatenate([compress_blocks(past_c, cmp_pe, cmp_w1, cmp_w2),
                            compress_blocks(jnp.pad(kv_c, pad_new), cmp_pe, cmp_w1, cmp_w2)], axis=1)
    new_blocks = jnp.pad(kv_s, pad_new).reshape(B, nb_new, BLK, N_KV, 2, HEAD_DIM).transpose(0, 3, 1, 2, 4, 5)

    def gather_sel(idx):
        in_past = idx < nb_past
        jp = jnp.minimum(idx, nb_past - 1)
        phys = page_table[jnp.arange(B)[:, None, None, None], jp // BLOCKS_PER_PAGE]
        offs = ((jp % BLOCKS_PER_PAGE) * BLK)[..., None] + jnp.arange(BLK)
        rows_past = cache_slc[phys[..., None], offs, jnp.arange(N_KV)[None, None, :, None, None]]
        rows_new = gather_local_blocks(new_blocks, jnp.clip(idx - nb_past, 0, nb_new - 1))
        return jnp.where(in_past[..., None, None, None], rows_past, rows_new)

    wk = state_win.shape[1]
    kv_wext = jnp.concatenate([state_win, kv_w], axis=1)
    pos_w = past - wk + jnp.arange(wk + T)
    o = nsa_heads(q, pos, comp, gather_sel, kv_wext, pos_w, gates, slopes)
    u_ext = jnp.concatenate([state_pool, u], axis=1)
    p = pool_mix(u_ext, pos, w_pool, pool_scale)
    h = merge_and_mlp(x, o, p, w_out, g_mlp, w_up, w_down)
    return h, (kv_c, kv_s, kv_wext[:, T:], u_ext[:, T:])

def setup_inputs(seed: int = 0) -> dict:
    key = jax.random.key(seed)
    ks = jax.random.split(key, 20)
    n_pages = PAST_LEN // PAGE_SIZE
    n_used = DEC_BATCH * n_pages
    n_pool = n_used + n_used // 4
    wk = min(WINDOW, PAST_LEN)
    nrm = lambda k, shape, scale=1.0: scale * jax.random.normal(k, shape, jnp.float32)
    page_table = jax.random.permutation(ks[0], n_pool)[:n_used].reshape(DEC_BATCH, n_pages).astype(jnp.int32)
    return {
        "x_prompt": nrm(ks[1], (BATCH, SEQ, D_MODEL)),
        "x_sample": nrm(ks[2], (DEC_BATCH, DEC_SEQ, D_MODEL)),
        "cache_cmp": nrm(ks[3], (DEPTH, n_pool, PAGE_SIZE, N_KV, 2, HEAD_DIM)),
        "cache_slc": nrm(ks[4], (DEPTH, n_pool, PAGE_SIZE, N_KV, 2, HEAD_DIM)),
        "state_win": nrm(ks[5], (DEPTH, DEC_BATCH, wk, N_KV, 2, HEAD_DIM)),
        "state_pool": nrm(ks[6], (DEPTH, DEC_BATCH, POOL_HIST, POOL_WIDTH)),
        "page_table": page_table,
        "g_attn": 1.0 + nrm(ks[7], (DEPTH, D_MODEL), 0.05),
        "w_in": nrm(ks[8], (DEPTH, D_MODEL, PROJ_WIDTH), D_MODEL ** -0.5),
        "cmp_pe": nrm(ks[9], (DEPTH, BLK, 2, HEAD_DIM), 0.1),
        "cmp_w1": nrm(ks[10], (DEPTH, 2, BLK, HEAD_DIM, CMP_HIDDEN), (BLK * HEAD_DIM) ** -0.5),
        "cmp_w2": nrm(ks[11], (DEPTH, 2, CMP_HIDDEN, HEAD_DIM), (2.0 / CMP_HIDDEN) ** 0.5),
        "w_pool": nrm(ks[12], (DEPTH, N_POOL_GROUPS, POOL_GROUP, POOL_GROUP), POOL_GROUP ** -0.5),
        "pool_scale": 1.0 + nrm(ks[13], (DEPTH, POOL_WIDTH), 0.1),
        "w_out": nrm(ks[14], (DEPTH, D_MODEL, D_MODEL), D_MODEL ** -0.5),
        "g_mlp": 1.0 + nrm(ks[15], (DEPTH, D_MODEL), 0.05),
        "w_up": nrm(ks[16], (DEPTH, D_MODEL, D_FF), D_MODEL ** -0.5),
        "w_down": nrm(ks[17], (DEPTH, D_FF, D_MODEL), D_FF ** -0.5),
        "g_final": 1.0 + nrm(ks[18], (D_MODEL,), 0.05),
    }

def reference(x_prompt, x_sample, cache_cmp, cache_slc, state_win, state_pool, page_table,
              g_attn, w_in, cmp_pe, cmp_w1, cmp_w2, w_pool, pool_scale, w_out,
              g_mlp, w_up, w_down, g_final):
    slopes = alibi_slopes()
    hp, hs = x_prompt, x_sample
    st_p, st_s = [], []
    for l in range(DEPTH):
        lw = (g_attn[l], w_in[l], cmp_pe[l], cmp_w1[l], cmp_w2[l], w_pool[l], pool_scale[l],
              w_out[l], g_mlp[l], w_up[l], w_down[l])
        hp, sp = prompt_layer(hp, *lw, slopes)
        hs, ss = sample_layer(hs, cache_cmp[l], cache_slc[l], state_win[l], state_pool[l],
                              page_table, *lw, slopes)
        st_p.append(sp)
        st_s.append(ss)
    y_prompt = rms_norm(hp, g_final)
    y_sample = rms_norm(hs, g_final)
    stk = lambda states, i: jnp.stack([s[i] for s in states], axis=0)
    return (y_prompt, y_sample,
            stk(st_p, 0), stk(st_p, 1), stk(st_p, 2), stk(st_p, 3),
            stk(st_s, 0), stk(st_s, 1), stk(st_s, 2), stk(st_s, 3))


_drawn_inputs = setup_inputs


def setup_inputs(seed=0):
    import zlib

    import numpy as np

    out = dict(_drawn_inputs(seed))
    spreads = {}
    factors = {}
    for name, (base, spread) in spreads.items():
        noise = np.random.default_rng([zlib.crc32(name.encode()), seed]).standard_normal(out[name].shape)
        drawn = base * np.exp(spread * noise) if base else spread * noise
        out[name] = __import__('jax').numpy.asarray(drawn.astype(out[name].dtype))
    for name, factor in factors.items():
        out[name] = (out[name] * factor).astype(out[name].dtype)
    return out
```

```python
from contextlib import ExitStack

import concourse.bass as bass
from concourse import mybir
import numpy as np

ALU = mybir.AluOpType
ACT = mybir.ActivationFunctionType
AX = mybir.AxisListType
F32 = mybir.dt.float32
BF16 = mybir.dt.bfloat16
I32 = mybir.dt.int32
U32 = mybir.dt.uint32

P = 128
D = 1024
KT_D = D // P
SEQ = 512
NB_SEQ = 8
DEC = 8
NS = NB_SEQ * DEC
TOK = SEQ + NS
HALF = TOK // 2
PTILES = SEQ // P
TILES = PTILES + 1
PAST = 2048
PAGE = 128
PAGES = PAST // PAGE
HD = 64
NKV = 2
HPG = 4
NH = NKV * HPG
KV = NKV * 2 * HD
BLK = 64
NBLK = PAST // BLK
PBLK = SEQ // BLK
N_SELECT = 16
WINDOW = 512
HID = 128
FF = 4096
FT = FF // P
PG = 128
POOLW = (2, 4, 8, 16)
HIST = 15
UEXT = HIST + SEQ
USAM = HIST + DEC
UW = UEXT + NB_SEQ * USAM
SCALE = HD ** -0.5
EPS = 1e-6
NEG = -1e30
FORCE = 5.0
Q0, KV0, GL0, U0, PROJ = 0, 512, 1280, 1304, 1816
ROWW = GL0 + 24 - KV0
CHUNK_L = 8
CHUNKS = BLK // CHUNK_L
LP = CHUNK_L // 2
CHUNKF = CHUNK_L * KV
QUAD = 4
SLOTF = 5 * QUAD * KV
GELU_C = 0.7978845608028654


def rows(i):
    return P if i < PTILES else NS


def tables():
    t = {}
    p = np.arange(P)
    t["ident"] = np.eye(P)
    x = np.arange(SEQ)[None, :] - (SEQ - P)
    t["negd"] = np.where(x <= p[:, None], x - p[:, None], NEG)
    q = np.arange(SEQ).reshape(PTILES, P).T[:, :, None]
    dist = q - (64 * (np.arange(PBLK)[None, None, :] + 1) - 1)
    t["cmpd"] = np.where(dist >= 0, -dist, NEG).reshape(P, -1)
    t["cmpm"] = (dist >= 0).astype(float).reshape(P, -1)
    t["slopes"] = np.broadcast_to(2.0 ** -(np.arange(NH) + 1.0), (P, NH))
    t["corr"] = np.stack([np.broadcast_to(w / np.minimum(w, np.arange(16) + 1.0), (P, 16)) for w in POOLW],
                         1).reshape(P, -1)
    t["page4"] = (p[:, None] // 32 == np.arange(4)[None]).astype(float)
    t["page64"] = (p[:, None] // 2 == np.arange(64)[None]).astype(float)
    t["quad"] = (p % 32)[:, None].astype(float)
    t["chunk"] = ((p % 2) * CHUNKS)[:, None] + np.arange(CHUNKS)[None] * 1.0
    seq, g, h, tt = p // 64, (p // 32) % 2, (p // 8) % 4, p % 8
    head = g * HPG + h
    slope = 2.0 ** -(head + 1.0)
    end = 64 * (np.arange(NBLK) + 1) - 1
    t["s_cmp"] = -slope[:, None] * (PAST + tt[:, None] - end[None])
    same = (seq[:, None] == seq[None]) & (g[:, None] == g[None]) & (tt[:, None] == tt[None])
    t["headsum"] = same.astype(float)
    t["headrow"] = (head[:, None] == np.arange(NH)[None]).astype(float)
    tok = np.arange(NS)
    pair = np.arange(NB_SEQ // 2)
    d = tt[:, None, None] - (tok % 8)[None, None]
    ok = ((2 * pair[None, :, None] + seq[:, None, None]) == (tok // 8)[None, None]) & (d >= 0)
    t["s_new"] = np.where(ok, -slope[:, None, None] * d, NEG).reshape(P, -1)
    sel = np.zeros((P, len(pair), P))
    for a in pair:
        sel[(2 * a + seq) * 8 + tt, a, p] = 1.0
    t["tokrow"] = sel.reshape(P, -1)
    small = {k: np.ascontiguousarray(v, dtype=np.float32) for k, v in t.items()}
    big = {}
    pos = (np.arange(4)[:, None, None] * 512 + 4 * p[None, None, :] + np.arange(4)[None, :, None]).reshape(-1)
    big["s_slc"] = -slope[:, None] * (PAST + tt[:, None] - pos[None])
    r = (4 * p[None, :] + np.arange(4)[:, None]).reshape(-1)
    dw = WINDOW + tt[:, None] - r[None]
    big["s_win"] = np.where((dw >= 0) & (dw < WINDOW), -slope[:, None] * dw, NEG)
    i = np.arange(NBLK)
    big["before"] = np.broadcast_to((i[None, :] < i[:, None]).astype(float).reshape(1, -1), (P, NBLK * NBLK))
    big = {k: np.ascontiguousarray(v, dtype=np.float32) for k, v in big.items()}
    return small, big


def columns(t):
    at, out = 0, {}
    for k, v in t.items():
        out[k] = (at, v.shape[1])
        at += v.shape[1]
    return out, at


class Mem:
    pass


def place(nc, ctx, m):
    def sb(name, shape, dt=F32):
        return ctx.enter_context(nc.sbuf_tensor(name, shape, dt))

    small, big = tables()
    m.ccols, cw = columns(small)
    m.bcols, bw = columns(big)
    m.consts = sb("consts", [P, cw])
    m.hT = sb("hT", [P, KT_D, TOK])
    m.mixT = sb("mixT", [P, KT_D, TOK])
    m.rowsT = sb("rowsT", [P, TILES, ROWW])
    m.qT = sb("qT", [P, HPG, TOK])
    m.kT = sb("kT", [P, 2, TOK])
    m.kcT = sb("kcT", [P, NB_SEQ * NBLK + PBLK])
    vcw = sb("vc_wpool", [P, (NB_SEQ + 1) * P])
    m.vc = vcw[0:NBLK, :].rearrange("p (b d) -> p b d", d=P)
    m.wpool = vcw[:, 0:4 * PG].rearrange("p (g d) -> p g d", d=PG)
    m.w2 = sb("w2", [P, 2, HD])
    m.peT = sb("peT", [P, BLK])
    m.gates = sb("gates", [P, TILES, 24])
    m.grow = sb("grow", [P, 12])
    m.small = sb("small", [P, 160])
    m.cols = sb("cols", [P, 20])
    m.tab = sb("tab", [P, NB_SEQ * PAGES], I32)
    m.idx_cmp = sb("idx_cmp", [P, 2, CHUNKS], U32)
    m.idx_slc = sb("idx_slc", [P, NB_SEQ * 4], U32)
    m.zeros = sb("zeros", [1, 640], BF16)
    m.ones = sb("ones", [P, P])
    m.zone = sb("zone", [P, 31200])
    m.pb = [ctx.enter_context(nc.psum_tensor(f"bank{i}", [P, 512], F32)) for i in range(8)]
    z = m.zone

    def at(a, *shape):
        n = int(np.prod(shape))
        v = z[:, a:a + n]
        if len(shape) == 1:
            return v
        names = "abcd"[:len(shape)]
        return v.rearrange(f"p ({' '.join(names)}) -> p {' '.join(names)}", **dict(zip(names, shape)))

    m.w_in = at(0, KT_D, PROJ)
    m.uT = at(14528, 4, UW)
    m.pa = at(14528 + 4 * UW, UW)
    m.pbuf = at(14528 + 5 * UW, UW)
    m.spool = at(14528 + 6 * UW, 512)
    m.utok = at(14528 + 6 * UW, 3, 512)
    m.colrows = m.pbuf[0:20, 512:512 + P]
    m.x = at(20480, TILES, D)
    m.xnT = at(25600, KT_D, TOK)
    m.dT = m.mixT[:, 0:4, :]
    m.raw = [at(20480 + 5120 * s, 2, CHUNKF) for s in range(2)]
    m.w1 = [at(20480 + 5120 * s + 2 * CHUNKF, 2, LP, HID) for s in range(2)]
    m.blkT_p = at(14528, 2, BLK // 2, 2 * PBLK)
    m.blkT = [[at(15552 + 1024 * s + 512 * c, 512) for c in range(2)] for s in range(2)]
    m.pe_in = at(17600, P)
    m.hx = at(18000, 2, 2, NB_SEQ * NBLK // 1 + PBLK)
    m.ht = at(0, 2, 2, NB_SEQ * NBLK + PBLK)
    m.slot = [at(SLOTF * s, 5, QUAD, KV) for s in range(4)]
    w = 20480
    m.cp = [at(w + 1024 * s, 2, 512) for s in range(3)]
    m.cpT = [at(w + 3072 + 1024 * s, 2, 512) for s in range(2)]
    m.pre = [at(w + 5120 + 1024 * s, 2, 512) for s in range(2)]
    m.qst = [at(w + 7168 + 512 * s, 512) for s in range(2)]
    m.cc = at(w + 8192, 2, PTILES, PBLK)
    m.ccT = at(w + 8256, 2, 512)
    m.skT = [at(w + 512 * s, 512) for s in range(2)]
    m.kst = [at(w + 1024 + 512 * s, 512) for s in range(2)]
    m.sp = at(w + 2048, 2720)
    m.spT = [at(w + 4768 + 512 * s, 512) for s in range(2)]
    m.spX = at(w + 5792, 384)
    m.big = at(w + 6176, bw)
    m.qs = [at(w + 9760 + 64 * s, 64) for s in range(2)]
    m.vcs = [at(w + 9888 + 128 * s, 128) for s in range(2)]
    m.cmpp = at(w + 10144, 32)
    m.imp = at(w + 10176, 32)
    m.selb = at(w + 10208, 32)
    m.snew = at(w + 10240, 64)
    m.kcs = at(w + 10304, 64)
    m.gt = at(w + 2048, NBLK, NBLK)
    m.eq = at(w + 2048 + 1024, NBLK, NBLK)
    m.wring = [at(4096 * s, 4096) for s in range(2)]
    m.aT = at(8192, FT, TOK)
    m.gfin = at(8192 + FT * TOK, D)
    m.yo = [at(8192 + FT * TOK + D * (1 + s), D) for s in range(2)]
    qf = m.qT[:, :, :]
    m.sq = [qf[:, 0, :], qf[:, 1, :]]
    m.var, m.rb = qf[:, 2, :], qf[:, 3, :]
    m.hnT = m.mixT
    m.junk = m.mixT[:, 4:6, :].rearrange("p a b -> p (a b)")[:, 0:D]


def const(m, name):
    a, n = m.ccols[name]
    return m.consts[:, a:a + n]


def bigconst(m, name):
    a, n = m.bcols[name]
    return m.big[:, a:a + n]


def keys(m, i, br, n=P):
    return m.rowsT[0:n, i, KV * (br + 1):KV * (br + 1) + P]


def values_at(m, i, br, n=P):
    return m.rowsT[0:n, i, KV * (br + 1) + P:KV * (br + 2)]


def hold(dve, m, k):
    dve.memset(m.small[:, 150 + k:151 + k], 0.0)


def load_slot(eng, m, s, b, sems):
    cache = m.cache_slc.rearrange("l n (r q) g c d -> (l n r) (q g c d)", q=QUAD)
    for pg in range(4):
        eng.indirect_dma_start(m.slot[s][:, pg, :, :].rearrange("p q c -> p (q c)"), None, cache,
                               bass.IndirectOffsetOnAxis(ap=m.idx_slc[:, b * 4 + pg:b * 4 + pg + 1], axis=0))\
           .then_inc(sems.slc_in[s], 16)


def load_window(eng, m, s, b, sems):
    eng.dma_start(m.slot[s][:, 4, :, :].rearrange("p q c -> p (q c)"),
                  m.state_win[0, b].rearrange("(p q) g c d -> p (q g c d)", q=QUAD)).then_inc(sems.win_in[s], 16)


def project(nc, m, sems, sem):
    g = m
    pb = m.pb
    ident = const(m, "ident")
    x_in = [sem(f"x_in{i}") for i in range(TILES)]
    table_in, rowsw_in, uw_in, qw_in = sem("table_in"), sem("rowsw_in"), sem("uw_in"), sem("qw_in")
    spool_in, cols_in, cols_turned, cols_kept = sem("spool_in"), sem("cols_in"), sem("cols_turned"), sem("cols_kept")
    ss_clear, ss_ready, var_ready, std_ready, rstd_ready = (
        sem("ss_clear"), sem("ss_ready"), sem("var_ready"), sem("std_ready"), sem("rstd_ready"))
    raw_turned, xt_kept, xn_ready, xn_turned, xnt_ready = (
        sem("raw_turned"), sem("xt_kept"), sem("xn_ready"), sem("xn_turned"), sem("xnt_ready"))
    rows_mm, rows_kept, tile_mm, tile_kept = sem("rows_mm"), sem("rows_kept"), sem("tile_mm"), sem("tile_kept")
    sp_turned, sp_kept, upad = sem("sp_turned"), sem("sp_kept"), sem("upad")
    ut_turned, ut_kept, pool_step, d_ready, pool_mm = (
        sem("ut_turned"), sem("ut_kept"), sem("pool_step"), sem("d_ready"), sem("pool_mm"))
    pool_kept, egate, gate1, idx_step = sem("pool_kept"), sem("egate"), sem("gate1"), sem("idx_step")
    ss, rstd = m.small[:, 0:TILES], m.small[:, 8:8 + TILES]
    var = m.small[:, 16:16 + TILES]
    ga, psc = m.cols[:, 0:8], m.cols[:, 16:20]
    pgc = m.small[:, 56:58]
    pgs = m.small[:, 64:96]

    with nc.Block() as block:
        @block.sync
        def _(sp):
            sp.dma_start(m.x[:, 0, :], m.x_prompt[0, 0:P, :]).then_inc(x_in[0], 16)
            sp.dma_start(m.consts[:, :], m.c_small).then_inc(sems.const_in, 16)
            for i in range(1, PTILES):
                sp.dma_start(m.x[:, i, :], m.x_prompt[0, P * i:P * i + P, :]).then_inc(x_in[i], 16)
            sp.dma_start(m.x[0:NS, PTILES, :], m.x_sample.rearrange("b t d -> (b t) d")).then_inc(x_in[PTILES], 16)
            for a, src in ((0, m.g_attn), (8, m.g_mlp), (16, m.pool_scale)):
                n = src.shape[1] // P
                sp.dma_start(m.colrows[a:a + n, :], src.rearrange("l (k p) -> (l k) p", p=P)).then_inc(cols_in, 16)
            wv = m.w_in_d[0].rearrange("(k p) n -> p k n", p=P)
            for k in range(0, KT_D, 4):
                sp.dma_start(m.w_in[:, k:k + 4, KV0:U0], wv[:, k:k + 4, KV0:U0]).then_inc(rowsw_in, 16)
            sp.dma_start(m.tab[:, :], m.page_table.rearrange("(o b) n -> o (b n)", o=1).broadcast_to([P, P]))\
              .then_inc(table_in, 16)
            sp.dma_start(m.w_in[:, :, U0:PROJ], wv[:, :, U0:PROJ]).then_inc(uw_in, 16)
            sp.dma_start(m.spool[0:NB_SEQ * HIST, :], m.state_pool[0].rearrange("b r c -> (b r) c"))\
              .then_inc(spool_in, 16)
            for g in range(NKV):
                for k in range(KT_D):
                    sp.dma_start(m.w_in[:, k, Q0:KV0].rearrange("p (j g d) -> p g j d", g=NKV, j=HPG)[:, g],
                                 wv[:, k, 256 * g:256 * g + 256].rearrange("p (j d) -> p j d", j=HPG))\
                      .then_inc(qw_in, 16)
            sp.dma_start(m.wpool[:, :, :], m.w_pool[0].rearrange("g c d -> c g d")).then_inc(sems.wpool_in, 16)
            sp.dma_start(m.w2[:, :, :], m.cmp_w2[0].rearrange("c h d -> h c d")).then_inc(sems.w2_in, 16)
            for b in range(NB_SEQ):
                sp.dma_start(m.o_swin[0, b, 0:WINDOW - DEC].rearrange("(a r) g c d -> a (r g c d)", a=28),
                             m.state_win[0, b, DEC:WINDOW].rearrange("(a r) g c d -> a (r g c d)", a=28))\
                  .then_inc(sems.out, 16)
            sp.wait_ge(rows_kept, 2 * TILES)
            sp.dma_start(m.o_pcmp[0, 0].rearrange("(i p) g c d -> p i (g c d)", p=P), m.rowsT[:, 0:PTILES, 0:KV])\
              .then_inc(sems.out, 16)
            sp.dma_start(m.o_scmp[0].rearrange("b t g c d -> (b t) (g c d)"), m.rowsT[0:NS, PTILES, 0:KV])\
              .then_inc(sems.out, 16)
            cgd = lambda v: v.rearrange("p (c g d) -> p g c d", c=2, g=NKV)
            for i in range(PTILES):
                for br, po in ((1, m.o_pslc), (2, m.o_pwin)):
                    for g in range(NKV):
                        sp.dma_start(po[0, 0, P * i:P * i + P, g], cgd(m.rowsT[:, i, KV * br:KV * br + KV])[:, g])\
                          .then_inc(sems.out, 16)
            for g in range(NKV):
                sp.dma_start(m.o_sslc[0].rearrange("b t g c d -> (b t) g c d")[:, g],
                             cgd(m.rowsT[0:NS, PTILES, KV:2 * KV])[:, g]).then_inc(sems.out, 16)
                for b in range(NB_SEQ):
                    sp.dma_start(m.o_swin[0, b, WINDOW - DEC:WINDOW, g],
                                 cgd(m.rowsT[b * DEC:(b + 1) * DEC, PTILES, 2 * KV:3 * KV])[:, g])\
                      .then_inc(sems.out, 16)
            sp.wait_ge(ut_kept, 3)
            for b in range(NB_SEQ):
                a = USAM * (b % 4) + DEC
                sp.dma_start(m.o_spool[0, b], m.utok[a:a + HIST, b // 4, :]).then_inc(sems.out, 16)
            sp.dma_start(m.o_ppool[0, 0], m.utok[0:HIST, 2, :]).then_inc(sems.out, 16)
            sems.n_out = 16 * (NB_SEQ + 2 + 4 * PTILES + 2 + 2 * NB_SEQ + NB_SEQ + 1)
            sp.wait_ge(sems.out, sems.n_out)

        @block.gpsimd
        def _(pool):
            pool.memset(m.zeros[:, :], 0.0).then_inc(sems.ones_set, 1)
            pool.memset(m.ones[:, :], 1.0).then_inc(sems.ones_set, 1)
            pool.memset(m.uT[:, :, 0:HIST], 0.0).then_inc(upad, 1)
            pool.wait_ge(idx_step, 7)
            pool.wait_ge(xn_turned, 2 * TILES)
            load_chunk(pool, m, sems, 0)

        @block.scalar
        def _(act):
            act.wait_ge(ss_clear, 1)
            for i in range(TILES):
                n = rows(i)
                act.wait_ge(x_in[i], 16)
                if i:
                    act.wait_ge(ss_ready, i)
                act.activation(m.junk[0:n, :], m.x[0:n, i, :], ACT.Square, accum_out=ss[0:n, i:i + 1])\
                   .then_inc(ss_ready, 1)
                for kk in range(2):
                    u = 2 * i + kk
                    act.wait_ge(raw_turned, u + 1)
                    act.activation(m.hT[:, 4 * kk:4 * kk + 4, P * i:P * i + n],
                                   pb[u % 4][:, :].rearrange("p (k t) -> p k t", k=4)[:, :, 0:n], ACT.Copy)\
                       .then_inc(xt_kept, 1)
            act.wait_ge(var_ready, 1)
            act.activation(rstd, var, ACT.Sqrt).then_inc(std_ready, 1)
            for u in range(2 * TILES):
                i, n = u // 2, rows(u // 2)
                act.wait_ge(rows_mm, u + 1)
                if u % 2 == 0:
                    act.activation(m.rowsT[0:n, i, 0:KV], pb[u % 4][0:n, 0:KV], ACT.Copy)
                    act.activation(m.rowsT[0:n, i, KV:2 * KV].rearrange("p (c g d) -> p g c d", c=2, g=NKV),
                                   pb[u % 4][0:n, KV:2 * KV].rearrange("p (g c d) -> p g c d", c=2, g=NKV), ACT.Copy)\
                       .then_inc(rows_kept, 1)
                else:
                    act.activation(m.rowsT[0:n, i, 2 * KV:3 * KV].rearrange("p (c g d) -> p g c d", c=2, g=NKV),
                                   pb[u % 4][0:n, 0:KV].rearrange("p (g c d) -> p g c d", c=2, g=NKV), ACT.Copy)
                    act.activation(m.rowsT[0:n, i, 3 * KV:ROWW], pb[u % 4][0:n, KV:ROWW - 2 * KV], ACT.Copy)\
                       .then_inc(rows_kept, 1)
            act.wait_ge(rows_kept, 2 * TILES)
            act.activation(m.gates[:, 0:PTILES, :], m.rowsT[:, 0:PTILES, 3 * KV:ROWW], ACT.Exp, scale=-1.0)\
               .then_inc(egate, 1)
            act.activation(m.gates[0:NS, PTILES, :], m.rowsT[0:NS, PTILES, 3 * KV:ROWW], ACT.Exp, scale=-1.0)\
               .then_inc(egate, 1)
            for e, n in ((0, 4 * USAM), (1, 4 * USAM), (2, HIST)):
                act.wait_ge(ut_turned, e + 1)
                act.activation(m.utok[0:n, e, :], pb[1 + e][0:n, :], ACT.Copy).then_inc(ut_kept, 1)
            act.wait_ge(cols_kept, 1)
            for gi in range(4):
                act.wait_ge(pool_mm, gi + 1)
                for hf in range(2):
                    last = act.activation(m.mixT[:, 4 + gi, HALF * hf:HALF * hf + HALF],
                                          pb[4 + 2 * (gi % 2) + hf][:, 0:HALF], ACT.Identity, scale=psc[:, gi:gi + 1])
                last.then_inc(pool_kept, 1)

        @block.vector
        def _(dve):
            dve.memset(ss, 1.0).then_inc(ss_clear, 1)
            dve.wait_ge(ss_ready, TILES)
            dve.tensor_scalar(var, ss, 1.0 / D, EPS, ALU.mult, ALU.add).then_inc(var_ready, 1)
            dve.wait_ge(std_ready, 1)
            dve.reciprocal(rstd, rstd).then_inc(rstd_ready, 1)
            dve.wait_ge(rstd_ready, 1)
            for i in range(TILES):
                n = rows(i)
                dve.wait_ge(raw_turned, 2 * i + 2)
                dve.tensor_scalar(m.x[0:n, i, :], m.x[0:n, i, :], rstd[0:n, i:i + 1], None, ALU.mult)\
                   .then_inc(xn_ready, 1)
            dve.wait_ge(cols_turned, 1)
            dve.tensor_copy(m.cols[:, :], pb[7][:, 0:20]).then_inc(cols_kept, 1)
            dve.wait_ge(cols_kept, 1)
            for u in range(2 * TILES):
                i, kk, n = u // 2, u % 2, rows(u // 2)
                dve.wait_ge(xn_turned, u + 1)
                dve.tensor_tensor(m.xnT[:, 4 * kk:4 * kk + 4, P * i:P * i + n],
                                  pb[4 + u % 4][:, :].rearrange("p (k t) -> p k t", k=4)[:, :, 0:n],
                                  ga[:, 4 * kk:4 * kk + 4].unsqueeze(2).broadcast_to([P, 4, n]), ALU.mult)\
                   .then_inc(xnt_ready, 1)
            dve.wait_ge(table_in, 16)
            dve.wait_ge(sems.const_in, 16)
            tf, t2 = m.pa[:, 0:P], m.pbuf[:, 0:P]
            dve.tensor_copy(tf, m.tab[:, :]).then_inc(idx_step, 1)
            dve.wait_ge(idx_step, 1)
            dve.tensor_tensor(t2.rearrange("p (a k) -> p a k", k=4), tf.rearrange("p (a k) -> p a k", k=4),
                              const(m, "page4").unsqueeze(1).broadcast_to([P, 32, 4]), ALU.mult).then_inc(idx_step, 1)
            dve.wait_ge(idx_step, 2)
            dve.tensor_reduce(pgs, t2.rearrange("p (a k) -> p a k", k=4), AX.X, ALU.add).then_inc(idx_step, 1)
            dve.wait_ge(idx_step, 3)
            dve.tensor_scalar(m.idx_slc[:, :], pgs, 32.0, const(m, "quad"), ALU.mult, ALU.add).then_inc(idx_step, 1)
            dve.tensor_tensor(t2.rearrange("p (a k) -> p a k", k=64), tf.rearrange("p (a k) -> p a k", k=64),
                              const(m, "page64").unsqueeze(1).broadcast_to([P, 2, 64]), ALU.mult).then_inc(idx_step, 1)
            dve.wait_ge(idx_step, 5)
            dve.tensor_reduce(pgc, t2.rearrange("p (a k) -> p a k", k=64), AX.X, ALU.add).then_inc(idx_step, 1)
            dve.wait_ge(idx_step, 6)
            dve.scalar_tensor_tensor(out=m.idx_cmp[:, :, :], in0=pgc.unsqueeze(2).broadcast_to([P, 2, CHUNKS]),
                                     scalar=2.0 * CHUNKS,
                                     in1=const(m, "chunk").unsqueeze(1).broadcast_to([P, 2, CHUNKS]),
                                     op0=ALU.mult, op1=ALU.add).then_inc(idx_step, 1)
            dve.wait_ge(sp_turned, 1)
            dve.tensor_copy(m.uT[:, :, UEXT:UW].rearrange("p g (b r) -> p g b r", b=NB_SEQ)[:, :, :, 0:HIST],
                            pb[0][:, 0:480].rearrange("p (g b r) -> p g b r", g=4, b=NB_SEQ)).then_inc(sp_kept, 1)
            for u in range(8):
                dve.wait_ge(tile_mm, u + 1)
                a, b = pb[4 + 2 * (u % 2)], pb[5 + 2 * (u % 2)]
                if u < 4:
                    dve.tensor_copy(m.uT[:, u, HIST:HIST + HALF], a[:, 0:HALF])
                    dve.tensor_copy(m.uT[:, u, HIST + HALF:UEXT], b[:, 0:SEQ - HALF])
                    dve.tensor_copy(m.uT[:, u, UEXT:UW].rearrange("p (b r) -> p b r", b=NB_SEQ)[:, :, HIST:USAM],
                                    b[:, SEQ - HALF:HALF].rearrange("p (b t) -> p b t", b=NB_SEQ))\
                       .then_inc(tile_kept, 1)
                else:
                    dve.tensor_scalar(m.qT[:, u - 4, 0:HALF], a[:, 0:HALF], SCALE, None, ALU.mult)
                    dve.tensor_scalar(m.qT[:, u - 4, HALF:TOK], b[:, 0:HALF], SCALE, None, ALU.mult)\
                       .then_inc(tile_kept, 1)
            dve.wait_ge(upad, 1)
            dve.wait_ge(sp_kept, 1)
            dve.wait_ge(tile_kept, 4)
            steps = 0
            for gi, w in enumerate(POOLW):
                src, dst, other = m.uT[:, gi, :], m.pa, m.pbuf
                s = 1
                while s < w:
                    if steps:
                        dve.wait_ge(pool_step, steps)
                    dve.tensor_tensor(dst[:, 2 * s - 1:UW], src[:, 2 * s - 1:UW], src[:, s - 1:UW - s], ALU.add)\
                       .then_inc(pool_step, 1)
                    steps += 1
                    src, dst, other = dst, other, dst
                    s *= 2
                dve.wait_ge(pool_step, steps)
                dve.tensor_tensor(src[:, HIST:HIST + 16], src[:, HIST:HIST + 16],
                                  const(m, "corr")[:, 16 * gi:16 * gi + 16], ALU.mult).then_inc(pool_step, 1)
                steps += 1
                dve.wait_ge(pool_step, steps)
                sam = lambda v: v[:, UEXT:UW].rearrange("p (b r) -> p b r", b=NB_SEQ)[:, :, HIST:USAM]
                dve.scalar_tensor_tensor(out=m.dT[:, gi, 0:SEQ], in0=src[:, HIST:UEXT], scalar=1.0 / w,
                                         in1=m.uT[:, gi, HIST:UEXT], op0=ALU.mult, op1=ALU.subtract)\
                   .then_inc(pool_step, 1)
                dve.scalar_tensor_tensor(out=m.dT[:, gi, SEQ:TOK].rearrange("p (b t) -> p b t", b=NB_SEQ),
                                         in0=sam(src), scalar=1.0 / w, in1=sam(m.uT[:, gi, :]),
                                         op0=ALU.mult, op1=ALU.subtract).then_inc(pool_step, 1)
                steps += 2
                dve.wait_ge(pool_step, steps)
                dve.sem_inc(d_ready, 1)
            dve.wait_ge(egate, 2)
            dve.tensor_scalar(m.gates[:, 0:PTILES, :], m.gates[:, 0:PTILES, :], 1.0, None, ALU.add).then_inc(gate1, 1)
            dve.tensor_scalar(m.gates[0:NS, PTILES, :], m.gates[0:NS, PTILES, :], 1.0, None, ALU.add)\
               .then_inc(gate1, 1)
            dve.wait_ge(gate1, 2)
            dve.reciprocal(m.gates[:, 0:PTILES, :], m.gates[:, 0:PTILES, :])
            dve.reciprocal(m.gates[0:NS, PTILES, :], m.gates[0:NS, PTILES, :]).then_inc(gate1, 1)

        @block.tensor
        def _(pe):
            pe.wait_ge(sems.const_in, 16)
            for u in range(2 * TILES):
                i, kk, n = u // 2, u % 2, rows(u // 2)
                if kk == 0:
                    pe.wait_ge(x_in[i], 16)
                if u >= 4:
                    pe.wait_ge(xt_kept, u - 3)
                for k in range(4):
                    last = pe.transpose(pb[u % 4][:, P * k:P * k + n],
                                        m.x[0:n, i, P * (4 * kk + k):P * (4 * kk + k) + P], ident[0:n, 0:n])
                last.then_inc(raw_turned, 1)

            pe.wait_ge(cols_in, 48)
            pe.transpose(pb[7][:, 0:20], m.colrows, ident[0:20, 0:20]).then_inc(cols_turned, 1)

            def turn_normed(u):
                i, kk, n = u // 2, u % 2, rows(u // 2)
                pe.wait_ge(xn_ready, i + 1)
                if u == 3:
                    pe.wait_ge(cols_kept, 1)
                if u >= 4:
                    pe.wait_ge(xnt_ready, u - 3)
                for k in range(4):
                    last = pe.transpose(pb[4 + u % 4][:, P * k:P * k + n],
                                        m.x[0:n, i, P * (4 * kk + k):P * (4 * kk + k) + P], ident[0:n, 0:n])
                last.then_inc(xn_turned, 1)

            def project_rows(u):
                i, n = u // 2, rows(u // 2)
                if u == 0:
                    pe.wait_ge(rowsw_in, 32)
                if u % 2 == 0:
                    pe.wait_ge(xnt_ready, 2 * i + 2)
                if u < 4:
                    pe.wait_ge(xt_kept, 7 + u)
                else:
                    pe.wait_ge(rows_kept, u - 3)
                a, b = (KV0, KV0 + 512) if u % 2 == 0 else (KV0 + 512, U0)
                for k in range(KT_D):
                    last = pe.matmul(pb[u % 4][0:n, 0:b - a], m.xnT[:, k, P * i:P * i + n], m.w_in[:, k, a:b],
                                     start=(k == 0), stop=(k == KT_D - 1))
                last.then_inc(rows_mm, 1)

            for i in range(TILES):
                turn_normed(2 * i)
                turn_normed(2 * i + 1)
                if i:
                    project_rows(2 * i - 2)
                    project_rows(2 * i - 1)
            project_rows(2 * TILES - 2)
            project_rows(2 * TILES - 1)
            pe.wait_ge(spool_in, 16)
            pe.wait_ge(rows_kept, 9)
            for gi in range(4):
                last = pe.transpose(pb[0][:, 120 * gi:120 * gi + 120], m.spool[0:120, P * gi:P * gi + P],
                                    ident[0:120, 0:120])
            last.then_inc(sp_turned, 1)
            for u in range(8):
                if u == 0:
                    pe.wait_ge(xnt_ready, 2 * TILES)
                    pe.wait_ge(uw_in, 16)
                if u == 4:
                    pe.wait_ge(qw_in, 16 * NKV * KT_D)
                if u >= 2:
                    pe.wait_ge(tile_kept, u - 1)
                for hf in range(2):
                    for k in range(KT_D):
                        a = U0 + PG * u if u < 4 else Q0 + P * (u - 4)
                        w = m.w_in[:, k, a:a + P]
                        last = pe.matmul(pb[4 + 2 * (u % 2) + hf][:, 0:HALF], w,
                                         m.xnT[:, k, HALF * hf:HALF * hf + HALF],
                                         start=(k == 0), stop=(k == KT_D - 1))
                last.then_inc(tile_mm, 1)
            pe.wait_ge(rows_kept, 2 * TILES)
            for e in range(2):
                for gi in range(4):
                    a = UEXT + 4 * USAM * e
                    last = pe.transpose(pb[1 + e][0:4 * USAM, P * gi:P * gi + P], m.uT[:, gi, a:a + 4 * USAM], ident)
                last.then_inc(ut_turned, 1)
            for gi in range(4):
                last = pe.transpose(pb[3][0:HIST, P * gi:P * gi + P], m.uT[:, gi, UEXT - HIST:UEXT], ident)
            last.then_inc(ut_turned, 1)
            pe.wait_ge(sems.wpool_in, 16)
            for gi in range(4):
                pe.wait_ge(d_ready, gi + 1)
                if gi < 2:
                    pe.wait_ge(tile_kept, 7 + gi)
                else:
                    pe.wait_ge(pool_kept, gi - 1)
                for hf in range(2):
                    last = pe.matmul(pb[4 + 2 * (gi % 2) + hf][:, 0:HALF], m.wpool[:, gi, :],
                                     m.dT[:, gi, HALF * hf:HALF * hf + HALF], start=True, stop=True)
                last.then_inc(pool_mm, 1)


def load_chunk(eng, m, sems, ck):
    cache = m.cache_cmp.rearrange("l n (h k q) g c d -> (l n h k) (q g c d)", h=2, k=CHUNKS)
    for hf in range(2):
        eng.indirect_dma_start(m.raw[ck % 2][:, hf, :], None, cache,
                               bass.IndirectOffsetOnAxis(ap=m.idx_cmp[:, hf, ck:ck + 1], axis=0))\
           .then_inc(sems.raw_in[ck % 2], 16)


def compress(nc, m, sems, sem):
    pb = m.pb
    ident = const(m, "ident")
    pe_in, pe_turned, pe_kept = sem("pe_in"), sem("pe_turned"), sem("pe_kept")
    w1_in = [sem("w1_in0"), sem("w1_in1")]
    kt_turned, kt_kept, pblk_turned, pblk_kept = (
        sem("kt_turned"), sem("kt_kept"), sem("pblk_turned"), sem("pblk_kept"))
    blk_turned, blk_kept, hid_done = sem("blk_turned"), [sem("blk_kept_k"), sem("blk_kept_v")], sem("hid_done")
    hx_ready, gelu, gtanh, kc_mm, kc_kept = (
        sem("hx_ready"), sem("gelu"), sem("gtanh"), sem("kc_mm"), sem("kc_kept"))
    NBT = NB_SEQ * NBLK

    with nc.Block() as block:
        @block.sync
        def _(sp):
            sp.dma_start(m.pe_in[0:BLK, :], m.cmp_pe[0].rearrange("l c d -> l (c d)")).then_inc(pe_in, 16)
            for ck in range(CHUNKS):
                s = ck % 2
                if ck >= 2:
                    sp.wait_ge(hid_done, 2 * LP * (ck - 1))
                for c in range(2):
                    sp.dma_start(m.w1[s][:, c, :, :],
                                 m.cmp_w1[0, c].rearrange("(k a q) d h -> k (q d) a h", k=CHUNKS, q=2)[ck])\
                      .then_inc(w1_in[s], 16)
            sp.wait_ge(gelu, 3)
            for b in range(2):
                load_window(sp, m, b, b, sems)

        @block.gpsimd
        def _(pool):
            for ck in range(1, CHUNKS):
                if ck >= 2:
                    pool.wait_ge(blk_turned, CHUNK_L * (ck - 1))
                load_chunk(pool, m, sems, ck)
            pool.wait_ge(gelu, 3)
            for b in range(2):
                load_slot(pool, m, b, b, sems)

        @block.scalar
        def _(act):
            act.wait_ge(pe_turned, 1)
            act.activation(m.peT[:, :], pb[7][:, 0:BLK], ACT.Copy)\
               .then_inc(pe_kept, 1)
            for br in range(2):
                act.wait_ge(kt_turned, br + 1)
                act.activation(m.kT[:, br, 0:SEQ], pb[4 + br][:, :], ACT.Copy).then_inc(kt_kept, 1)
            act.wait_ge(kt_turned, 3)
            act.activation(m.kT[:, :, SEQ:TOK], pb[6][:, 0:2 * NS].rearrange("p (b t) -> p b t", b=2), ACT.Copy)\
               .then_inc(kt_kept, 1)
            act.wait_ge(pe_kept, 1)
            with act.Fori(0, CHUNKS // 2) as it:
                for v in range(2 * CHUNK_L):
                    lo = HD * (v % 2)
                    act.wait_ge(blk_turned, it * (2 * CHUNK_L) + v + 1)
                    act.activation(m.blkT[(v // 2) % 2][0][lo:lo + HD, :], pb[4 + v % 4][0:HD, :], ACT.Identity,
                                   bias=m.peT[0:HD, bass.ds(it * (2 * CHUNK_L) + v, 1)]).then_inc(blk_kept[0], 1)
            act.wait_ge(hid_done, BLK)
            for c in range(2):
                act.activation(m.hx[:, c, :, 0:NBT // 1].rearrange("p g (h n) -> p h g n", h=2),
                               pb[c][:, :].rearrange("p (h g n) -> p h g n", h=2, g=2), ACT.Copy)\
                   .then_inc(hx_ready, 1)
            act.activation(m.hx[:, :, :, NBT:NBT + PBLK],
                           pb[2][:, 0:32].rearrange("p (c g n) -> p c g n", c=2, g=2), ACT.Copy).then_inc(hx_ready, 1)
            act.wait_ge(gelu, 2)
            act.activation(m.ht[:, :, :, :], m.ht[:, :, :, :], ACT.Tanh, scale=GELU_C).then_inc(gtanh, 1)
            act.wait_ge(kc_mm, 1)
            act.activation(m.kcT[:, :], pb[0][:, 0:NBT + PBLK], ACT.Copy, scale=0.5).then_inc(kc_kept, 1)

        @block.vector
        def _(dve):
            dve.wait_ge(pe_kept, 1)
            for g in range(2):
                dve.wait_ge(pblk_turned, g + 1)
                for c in range(2):
                    for par in range(2):
                        lo, hi = HD * c, HD * par
                        src = pb[g][lo:lo + HD, :].rearrange("p (b l q) -> p b l q", b=PBLK, q=2)[:, :, :, par]
                        dst = m.blkT_p[hi:hi + HD, c, :, PBLK * g:PBLK * g + PBLK].rearrange("p l b -> p b l")
                        pe_b = m.peT[lo:lo + HD, :].rearrange("p (l q) -> p l q", q=2)[:, :, par]
                        last = dve.tensor_tensor(dst, src, pe_b.unsqueeze(1).broadcast_to([HD, PBLK, BLK // 2]),
                                                 ALU.add)
                last.then_inc(pblk_kept, 1)
            with dve.Fori(0, CHUNKS // 2) as it:
                for v in range(2 * CHUNK_L):
                    lo = HD * (v % 2)
                    dve.wait_ge(blk_turned, it * (2 * CHUNK_L) + v + 1)
                    dve.tensor_scalar(m.blkT[(v // 2) % 2][1][lo:lo + HD, :], pb[4 + v % 4][HD:P, :],
                                      m.peT[HD:P, bass.ds(it * (2 * CHUNK_L) + v, 1)], None, ALU.add)\
                       .then_inc(blk_kept[1], 1)
            hx, ht = m.hx[:, :, :, :], m.ht[:, :, :, :]
            dve.wait_ge(hx_ready, 3)
            dve.tensor_tensor(ht, hx, hx, ALU.mult).then_inc(gelu, 1)
            dve.wait_ge(gelu, 1)
            sq = sems.gelu_sq
            dve.tensor_scalar(ht, ht, 0.044715, 1.0, ALU.mult, ALU.add).then_inc(sq, 1)
            dve.wait_ge(sq, 1)
            dve.tensor_tensor(ht, ht, hx, ALU.mult).then_inc(gelu, 1)
            dve.wait_ge(gtanh, 1)
            dve.scalar_tensor_tensor(out=hx, in0=ht, scalar=1.0, in1=hx, op0=ALU.add, op1=ALU.mult).then_inc(gelu, 1)
            for n in range(3):
                dve.wait_ge(kc_mm, n + 2)
                if n < 2:
                    dve.tensor_scalar(m.vc[:, 4 * n:4 * n + 4, :],
                                      pb[1 + n][0:NBLK, :].rearrange("p (b d) -> p b d", b=4), 0.5, None, ALU.mult)\
                       .then_inc(kc_kept, 1)
                else:
                    dve.tensor_scalar(m.vc[0:PBLK, NB_SEQ, :], pb[3][0:PBLK, 0:P], 0.5, None, ALU.mult)\
                       .then_inc(kc_kept, 1)

        @block.tensor
        def _(pe):
            pe.wait_ge(pe_in, 16)
            pe.transpose(pb[7][:, 0:BLK], m.pe_in[0:BLK, :], ident[0:BLK, 0:BLK]).then_inc(pe_turned, 1)
            for br in range(2):
                for i in range(PTILES):
                    last = pe.transpose(pb[4 + br][:, P * i:P * i + P], keys(m, i, br), ident)
                last.then_inc(kt_turned, 1)
            for br in range(2):
                last = pe.transpose(pb[6][:, NS * br:NS * br + NS], keys(m, PTILES, br, NS), ident[0:NS, 0:NS])
            last.then_inc(kt_turned, 1)
            for g in range(2):
                for i in range(PTILES):
                    last = pe.transpose(pb[g][:, P * i:P * i + P], m.rowsT[:, i, P * g:P * g + P], ident)
                last.then_inc(pblk_turned, 1)
            pe.wait_ge(pblk_kept, 2)
            pe.wait_ge(pe_kept, 1)
            pe.wait_ge(kt_kept, 3)
            for n in range(3):
                pe.matmul(pb[n][:, :], m.zeros[0:1, 0:P], m.zeros[0:1, P:P + 512], start=True, stop=True)

            with pe.Fori(0, CHUNKS // 2) as it:
                def turn(v):
                    s, l = v // CHUNK_L, v % CHUNK_L
                    if l == 0:
                        pe.wait_ge(sems.raw_in[s], it * 32 + 32)
                    for hg in range(4):
                        a = KV * l + P * (hg % 2)
                        last = pe.transpose(pb[4 + v % 4][:, P * hg:P * hg + P], m.raw[s][:, hg // 2, a:a + P], ident)
                    last.then_inc(blk_turned, 1)

                def hidden(p):
                    s, a = p // LP, p % LP
                    if a == 0:
                        pe.wait_ge(w1_in[s], it * 32 + 32)
                    for c in range(2):
                        pe.wait_ge(blk_kept[c], it * (2 * CHUNK_L) + (2 * p + 2))
                        w = m.w1[s][:, c, a, :]
                        pe.matmul(pb[2][:, 16 * c:16 * c + 16], w,
                                  m.blkT_p[:, c, bass.ds(it * (2 * LP) + p, 1), :].rearrange("p a b -> p (a b)"),
                                  start=False, stop=False, skip_group_check=True)
                        pe.matmul(pb[c][:, :], w, m.blkT[p % 2][c], start=False, stop=False, skip_group_check=True)\
                          .then_inc(hid_done, 1)

                for p in range(2 * LP):
                    turn(2 * p)
                    turn(2 * p + 1)
                    if p >= 1:
                        hidden(p - 1)
                hidden(2 * LP - 1)

            pe.wait_ge(gelu, 3)
            pe.wait_ge(sems.w2_in, 16)
            for g in range(2):
                last = pe.matmul(pb[0][HD * g:HD * g + HD, 0:NBT + PBLK], m.w2[:, 0, :], m.hx[:, 0, g, :],
                                 start=True, stop=True)
            last.then_inc(kc_mm, 1)
            for b in range(NB_SEQ + 1):
                n = NBLK if b < NB_SEQ else PBLK
                for g in range(2):
                    last = pe.matmul(pb[1 + b // 4][0:n, P * (b % 4) + HD * g:P * (b % 4) + HD * g + HD],
                                     m.hx[:, 1, g, NBLK * b:NBLK * b + n], m.w2[:, 1, :], start=True, stop=True)
                if b in (3, 7, 8):
                    last.then_inc(kc_mm, 1)


def prompt(nc, m, sems, sem):
    pb = m.pb
    ident = const(m, "ident")
    q_staged, pre_ready = sem("q_staged"), sem("pre_ready")
    scored, summed, exped, smax, scl_ready, p_ready = (
        sem("scored"), sem("summed"), sem("exped"), sem("smax"), sem("scl_ready"), sem("p_ready"))
    rec, p_turned, pt_ready, o_done, o_kept = (
        sem("rec"), sem("p_turned"), sem("pt_ready"), sem("o_done"), sem("o_kept"))
    c_scored, c_step, c_exp, c_turned, ct_ready = (
        sem("c_scored"), sem("c_step"), sem("c_exp"), sem("c_turned"), sem("ct_ready"))
    U = 2 * PTILES
    units = [(g, i) for i in (3, 2, 1, 0) for g in range(2)]
    LAG_T, LAG_V = 2, 3
    nm = lambda u: m.small[:, 2 * (u % 3):2 * (u % 3) + 2]
    su = lambda u: m.small[:, 8 + 2 * (u % 3):8 + 2 * (u % 3) + 2]
    cst = m.small[:, 32:32 + 8]
    csum = m.small[:, 40:48]
    C_STEPS = 8

    with nc.Block() as block:
        @block.sync
        def _(sp):
            for b in range(2, 4):
                load_window(sp, m, b, b, sems)

        @block.gpsimd
        def _(pool):
            for b in range(2, 4):
                load_slot(pool, m, b, b, sems)

        @block.scalar
        def _(act):
            with act.Fori(0, HPG) as j:
                def c_exponent():
                    act.wait_ge(c_step, j * C_STEPS + 3)
                    act.activation(m.cc[:, :, :, :], m.cc[:, :, :, :], ACT.Exp).then_inc(c_exp, 1)

                def exponent(u):
                    g, i = units[u]
                    w = P * (i + 1)
                    act.wait_ge(smax, j * U + (u + 1))
                    for br in range(2):
                        last = act.activation(m.cp[u % 3][:, br, 0:w], m.cp[u % 3][:, br, 0:w], ACT.Exp,
                                              bias=nm(u)[:, br:br + 1], accum_out=su(u)[:, br:br + 1])
                    last.then_inc(exped, 1)

                def scale(u):
                    g, i = units[u]
                    w = P * (i + 1)
                    act.wait_ge(scl_ready, j * U + (u + 1))
                    for br in range(2):
                        last = act.activation(m.cp[u % 3][:, br, 0:w], m.cp[u % 3][:, br, 0:w], ACT.Copy,
                                              scale=su(u)[:, br:br + 1])
                    last.then_inc(p_ready, 1)

                c_exponent()
                for u in range(U + 1):
                    if u < U:
                        exponent(u)
                    if u >= 1:
                        scale(u - 1)
                for g in range(2):
                    act.wait_ge(o_done, j * U + (U - 1 + g))
                    act.activation(m.mixT[HD * g:HD * g + HD, bass.ds(j, 1), 0:SEQ]
                                   .rearrange("p a t -> p (a t)"), pb[6][HD * g:HD * g + HD, :], ACT.Copy)\
                       .then_inc(o_kept, 1)

        @block.vector
        def _(dve):
            with dve.Fori(0, HPG) as j:
                dve.wait_ge(o_kept, j * 2 + 2)
                dve.tensor_copy(m.qst[0], m.qT[:, bass.ds(j, 1), 0:SEQ].rearrange("p a t -> p (a t)"))\
                   .then_inc(q_staged, 1)
                for g in range(2):
                    last = dve.tensor_scalar(m.pre[0][:, g, :], const(m, "negd"),
                                             const(m, "slopes")[:, bass.ds(j + HPG * g, 1)], None, ALU.mult)
                last.then_inc(pre_ready, 1)

                def c_scores():
                    cc = m.cc[:, :, :, :].rearrange("p g i n -> p (g i) n")
                    dve.wait_ge(c_scored, j + 1)
                    for g in range(2):
                        last = dve.scalar_tensor_tensor(
                            out=m.cc[:, g, :, :].rearrange("p i n -> p (i n)"), in0=const(m, "cmpd"),
                            scalar=const(m, "slopes")[:, bass.ds(j + HPG * g, 1)],
                            in1=pb[7 - g][:, 0:32], op0=ALU.mult, op1=ALU.add)
                    last.then_inc(c_step, 1)
                    dve.wait_ge(c_step, j * C_STEPS + 1)
                    dve.tensor_reduce(cst, cc, AX.X, ALU.max).then_inc(c_step, 1)
                    dve.wait_ge(c_step, j * C_STEPS + 2)
                    dve.tensor_tensor(cc, cc, cst.unsqueeze(2).broadcast_to([P, 8, PBLK]), ALU.subtract)\
                       .then_inc(c_step, 1)

                def c_probs():
                    cc = m.cc[:, :, :, :].rearrange("p g i n -> p (g i) n")
                    dve.wait_ge(c_exp, j + 1)
                    for g in range(2):
                        last = dve.tensor_tensor(m.cc[:, g, :, :].rearrange("p i n -> p (i n)"),
                                                 m.cc[:, g, :, :].rearrange("p i n -> p (i n)"),
                                                 const(m, "cmpm"), ALU.mult)
                    last.then_inc(c_step, 1)
                    dve.wait_ge(c_step, j * C_STEPS + 4)
                    dve.tensor_reduce(csum, cc, AX.X, ALU.add).then_inc(c_step, 1)
                    dve.wait_ge(c_step, j * C_STEPS + 5)
                    dve.tensor_scalar(csum, csum, 1e-30, None, ALU.max).then_inc(c_step, 1)
                    dve.wait_ge(c_step, j * C_STEPS + 6)
                    dve.reciprocal(csum, csum).then_inc(c_step, 1)
                    dve.wait_ge(c_step, j * C_STEPS + 7)
                    for g in range(2):
                        last = dve.tensor_tensor(
                            csum[:, 4 * g:4 * g + 4], csum[:, 4 * g:4 * g + 4],
                            m.gates[:, 0:PTILES, bass.ds(j + HPG * g, 1)].rearrange("p i a -> p (i a)"), ALU.mult)
                    last.then_inc(c_step, 1)
                    dve.wait_ge(c_step, j * C_STEPS + 8)
                    dve.tensor_tensor(cc, cc, csum.unsqueeze(2).broadcast_to([P, 8, PBLK]), ALU.mult)\
                       .then_inc(ct_ready, 1)

                def sums(u):
                    g, i = units[u]
                    w = P * (i + 1)
                    if u == 0:
                        dve.wait_ge(pre_ready, j + 1)
                    dve.wait_ge(scored, j * U + (u + 1))
                    if u >= 3:
                        dve.wait_ge(p_turned, j * U + (u - 2))
                    hold(dve, m, u)
                    for br in range(2):
                        last = dve.tensor_tensor_reduce(m.cp[u % 3][:, br, 0:w], m.pre[0][:, g, SEQ - w:SEQ],
                                                        pb[2 * (u % 2) + br][:, 0:w], 1.0, -3e38, ALU.add, ALU.max,
                                                        nm(u)[:, br:br + 1])
                    last.then_inc(summed, 1)
                    dve.wait_ge(summed, j * U + (u + 1))
                    dve.tensor_scalar(nm(u), nm(u), -1.0, None, ALU.mult).then_inc(smax, 1)

                def factors(u):
                    g, i = units[u]
                    dve.wait_ge(exped, j * U + (u + 1))
                    dve.reciprocal(su(u), su(u)).then_inc(rec, 1)
                    dve.wait_ge(rec, j * U + (u + 1))
                    gt = m.gates[:, i, :].rearrange("p (r h) -> p r h", r=3)[:, 1:3, bass.ds(j + HPG * g, 1)]
                    dve.tensor_tensor(su(u), su(u), gt.rearrange("p r a -> p (r a)"), ALU.mult)\
                       .then_inc(scl_ready, 1)

                def keep_turned(u):
                    g, i = units[u]
                    w = P * (i + 1)
                    dve.wait_ge(p_turned, j * U + (u + 1))
                    for br in range(2):
                        last = dve.tensor_copy(m.cpT[u % 2][:, br, 0:w], pb[4 + br][:, 0:w])
                    last.then_inc(pt_ready, 1)

                c_scores()
                sums(0)
                c_probs()
                factors(0)
                for g in range(2):
                    dve.wait_ge(c_turned, j * 2 + (g + 1))
                    dve.tensor_copy(m.ccT[0:PBLK, g, :], pb[7][0:PBLK, :]).then_inc(ct_ready, 1)
                for u in range(1, U + LAG_T + 1):
                    if u < U:
                        sums(u)
                    if u >= LAG_T and u - LAG_T < U:
                        keep_turned(u - LAG_T)
                    if u < U:
                        factors(u)

        @block.tensor
        def _(pe):
            pe.sem_inc(o_kept, 2)
            with pe.Fori(0, HPG) as j:
                def c_scores():
                    for g in range(2):
                        for i in range(PTILES):
                            last = pe.matmul(pb[7 - g][:, PBLK * i:PBLK * i + PBLK], m.qst[0][HD * g:HD * g + HD, P * i:P * i + P],
                                             m.kcT[HD * g:HD * g + HD, NB_SEQ * NBLK:NB_SEQ * NBLK + PBLK],
                                             start=True, stop=True)
                    last.then_inc(c_scored, 1)

                def c_turn(g):
                    pe.wait_ge(ct_ready, j * 3 + (g + 1))
                    for i in range(PTILES):
                        last = pe.transpose(pb[7][0:PBLK, P * i:P * i + P], m.cc[:, g, i, :], ident)
                    last.then_inc(c_turned, 1)

                def scores(u):
                    g, i = units[u]
                    w = P * (i + 1)
                    if u >= 2:
                        pe.wait_ge(summed, j * U + (u - 1))
                    for br in range(2):
                        last = pe.matmul(pb[2 * (u % 2) + br][:, 0:w], m.qst[0][HD * g:HD * g + HD, P * i:P * i + P],
                                         m.kT[HD * g:HD * g + HD, br, 0:w], start=True, stop=True)
                    last.then_inc(scored, 1)

                def turn(u):
                    g, i = units[u]
                    pe.wait_ge(p_ready, j * U + (u + 1))
                    if u >= 1:
                        pe.wait_ge(pt_ready, j * U + u)
                    for br in range(2):
                        for k in range(i + 1):
                            last = pe.transpose(pb[4 + br][:, P * k:P * k + P],
                                                m.cp[u % 3][:, br, P * k:P * k + P], ident)
                    last.then_inc(p_turned, 1)

                def values(u):
                    g, i = units[u]
                    pe.wait_ge(pt_ready, j * U + (u + 1))
                    if u == 0:
                        pe.wait_ge(ct_ready, j * 3 + 3)
                        pe.wait_ge(o_kept, j * 2 + 2)
                    o = pb[6][HD * g:HD * g + HD, P * i:P * i + P]
                    for br in range(2):
                        for k in range(i + 1):
                            pe.matmul(o, values_at(m, k, br)[:, HD * g:HD * g + HD], m.cpT[u % 2][:, br, P * k:P * k + P],
                                      start=(br == 0 and k == 0), stop=False)
                    pe.matmul(o, m.vc[0:PBLK, NB_SEQ, HD * g:HD * g + HD], m.ccT[0:PBLK, g, P * i:P * i + P],
                              start=False, stop=True).then_inc(o_done, 1)

                pe.wait_ge(q_staged, j + 1)
                c_scores()
                scores(0)
                scores(1)
                c_turn(0)
                c_turn(1)
                for u in range(2, U + LAG_V):
                    if u < U:
                        scores(u)
                    if u >= LAG_T and u - LAG_T < U:
                        turn(u - LAG_T)
                    if u >= LAG_V:
                        values(u - LAG_V)


def sample(nc, m, sems, sem):
    pb = m.pb
    ident = const(m, "ident")
    NP_ = NB_SEQ // 2
    big_in, g_mm, g_step, qs_clear, staged = (
        sem("big_in"), sem("g_mm"), sem("g_step"), sem("qs_clear"), sem("staged"))
    n_scored, scored = sem("sn_scored"), sem("s_scored")
    k_packed, k_turned, k_kept = sem("k_packed"), sem("k_turned"), sem("k_kept")
    c_step, c_exp, p_cmp, imp_mm, sel_step, selb_ready, pre_ready = (
        sem("sc_step"), sem("sc_exp"), sem("p_cmp"), sem("imp_mm"), sem("sel_step"), sem("selb_ready"),
        sem("s_pre_ready"))
    summed, mx_ready, exped, f_step, f_ready, p_ready = (
        sem("s_summed"), sem("mx_ready"), sem("s_exped"), sem("f_step"), sem("f_ready"), sem("s_p_ready"))
    p_turned, pt_ready, o_done, bank0_free = sem("s_p_turned"), sem("s_pt_ready"), sem("s_o_done"), sem("bank0_free")
    sm = m.small
    cmax, cneg, csum = sm[:, 0:1], sm[:, 1:2], sm[:, 2:3]
    mx, nmx, ssum = sm[:, 8:16], sm[:, 16:18], sm[:, 20:22]
    NSL = PAST + NS
    WIN0 = NSL
    CMP0 = NSL + WINDOW + NS
    X = 5
    C_STEPS, SEL_STEPS, F_STEPS = 3, 5, 2

    with nc.Block() as block:
        @block.sync
        def _(sp):
            sp.dma_start(m.big, m.c_big).then_inc(big_in, 16)
            for n in range(2, NP_):
                sp.wait_ge(o_done, n - 1)
                for e in range(2):
                    load_window(sp, m, 2 * (n % 2) + e, 2 * n + e, sems)
            sp.wait_ge(o_done, NP_ - 1)
            for s in range(2):
                load_w_out(sp, m, sems, s)

        @block.gpsimd
        def _(pool):
            for e in range(2):
                pool.memset(m.qs[e], 0.0).then_inc(qs_clear, 1)
            pool.wait_ge(qs_clear, 2)
            pool.wait_ge(big_in, 16)
            for n in range(NP_):
                if n:
                    pool.wait_ge(o_done, n)
                if n >= 2:
                    for e in range(2):
                        pool.wait_ge(sems.slc_in[2 * (n % 2) + e], 128)
                b0 = 2 * n
                copies = []
                for e in range(2):
                    for g in range(2):
                        copies.append((m.qs[e][HD * g:HD * g + HD, 32 * g:32 * g + 32]
                                       .rearrange("p (h t) -> p h t", h=HPG),
                                       m.qT[HD * g:HD * g + HD, :, SEQ + DEC * (b0 + e):SEQ + DEC * (b0 + e + 1)]))
                    copies.append((m.vcs[e][0:NBLK, :], m.vc[:, b0 + e, :]))
                copies.append((m.kcs, m.kcT[:, NBLK * b0:NBLK * (b0 + 2)]))
                copies.append((m.snew, const(m, "s_new")[:, NS * n:NS * n + NS]))
                for k, (dst, src) in enumerate(copies):
                    pool.tensor_copy(dst, src).then_inc(staged, 1)
                    pool.wait_ge(staged, 8 * n + k + 1)
                if 1 <= n < NP_ - 1:
                    for e in range(2):
                        load_slot(pool, m, 2 * ((n + 1) % 2) + e, 2 * (n + 1) + e, sems)
                for u in range(2 * X):
                    e, x = u // X, u % X
                    if x == 0:
                        pool.wait_ge(sems.slc_in[2 * (n % 2) + e], 64 * (n // 2 + 1))
                    if x == X - 1:
                        pool.wait_ge(sems.win_in[2 * (n % 2) + e], 16 * (n // 2 + 1))
                    if 2 * X * n + u >= 2:
                        pool.wait_ge(k_turned, 2 * X * n + u - 1)
                    pool.tensor_copy(m.kst[u % 2].rearrange("p (a d) -> p a d", d=HD),
                                     m.slot[2 * (n % 2) + e][:, x].rearrange("p q (g k) -> p (q g) k", g=NKV)
                                     [:, :, 0:HD]).then_inc(k_packed, 1)
                pool.wait_ge(selb_ready, n + 1)
                for x in range(4):
                    pool.tensor_tensor(
                        m.sp[:, 512 * x:512 * x + 512].rearrange("p (m b q) -> p m b q", m=4, b=8),
                        bigconst(m, "s_slc")[:, 512 * x:512 * x + 512].rearrange("p (m b q) -> p m b q", m=4, b=8),
                        m.selb[:, 8 * x:8 * x + 8].unsqueeze(1).unsqueeze(3).broadcast_to([P, 4, 8, 16]),
                        ALU.add).then_inc(pre_ready, 1)

        @block.scalar
        def _(act):
            act.wait_ge(g_mm, 1)
            act.activation(m.imp_g, pb[0][:, 0:96], ACT.Copy).then_inc(bank0_free, 1)
            with act.Fori(0, NP_ // 2) as it:
                for q in range(2):
                    n = it * 2 + q

                    def keep_keys(u):
                        act.wait_ge(k_turned, n * (2 * X) + (u + 1))
                        act.activation(m.skT[u % 2], pb[6 + u % 2][:, :], ACT.Copy).then_inc(k_kept, 1)

                    for u in range(2 * X):
                        if u == 2:
                            act.wait_ge(c_step, n * C_STEPS + 2)
                            act.activation(m.cmpp, m.cmpp, ACT.Exp, bias=cneg, accum_out=csum).then_inc(c_exp, 1)
                        keep_keys(u)
                    act.wait_ge(mx_ready, n + 1)
                    act.activation(m.sp[:, 0:NSL], m.sp[:, 0:NSL], ACT.Exp, bias=nmx[:, 0:1], accum_out=ssum[:, 0:1])
                    act.activation(m.sp[:, WIN0:CMP0], m.sp[:, WIN0:CMP0], ACT.Exp, bias=nmx[:, 1:2],
                                   accum_out=ssum[:, 1:2]).then_inc(exped, 1)
                    act.wait_ge(f_ready, n + 1)
                    act.activation(m.sp[:, WIN0:CMP0], m.sp[:, WIN0:CMP0], ACT.Copy, scale=ssum[:, 1:2])\
                       .then_inc(p_ready, 1)
                    act.wait_ge(o_done, n + 1)
                    for g in range(2):
                        a = HD * g
                        last = act.activation(
                            m.mixT[a:a + HD, 0:HPG, bass.ds(n * (2 * DEC) + SEQ, 2 * DEC)]
                            .rearrange("p h (e t) -> p e h t", e=2),
                            pb[0][a:a + HD, 0:P].rearrange("p (e g h t) -> p e g h t", e=2, g=2, h=HPG)[:, :, g],
                            ACT.Copy)
                    last.then_inc(bank0_free, 1)

        @block.vector
        def _(dve):
            dve.wait_ge(bank0_free, 1)
            gt12 = m.imp_g.rearrange("p (a r h) -> p (a r) h", a=NP_, r=3)
            dve.tensor_tensor(gt12, gt12, const(m, "headrow").unsqueeze(1).broadcast_to([P, 12, NH]), ALU.mult)\
               .then_inc(g_step, 1)
            dve.wait_ge(g_step, 1)
            dve.tensor_reduce(m.grow[:, :], gt12, AX.X, ALU.add).then_inc(g_step, 1)
            dve.wait_ge(g_step, 2)
            dve.wait_ge(big_in, 16)
            with dve.Fori(0, NP_ // 2) as it:
                for q in range(2):
                    n = it * 2 + q
                    gate = lambda r: m.grow[:, bass.ds(n * 3 + r, 1)]
                    dve.wait_ge(n_scored, n + 1)
                    hold(dve, m, 0)
                    dve.tensor_tensor_reduce(m.cmpp, const(m, "s_cmp"), pb[5][:, 128:160], 1.0, -3e38, ALU.add,
                                             ALU.max, cmax).then_inc(c_step, 1)
                    dve.wait_ge(c_step, n * C_STEPS + 1)
                    dve.tensor_scalar(cneg, cmax, -1.0, None, ALU.mult).then_inc(c_step, 1)
                    dve.tensor_tensor_reduce(m.sp[:, PAST:NSL], m.snew, pb[5][:, 0:NS], 1.0, -3e38, ALU.add,
                                             ALU.max, mx[:, 4:5])
                    dve.tensor_tensor_reduce(m.sp[:, WIN0 + WINDOW:CMP0], m.snew, pb[5][:, NS:2 * NS], 1.0, -3e38,
                                             ALU.add, ALU.max, mx[:, 6:7])
                    dve.wait_ge(c_exp, n + 1)
                    dve.reciprocal(csum, csum).then_inc(c_step, 1)
                    dve.wait_ge(c_step, n * C_STEPS + 3)
                    dve.tensor_scalar(m.cmpp, m.cmpp, csum, None, ALU.mult).then_inc(p_cmp, 1)
                    dve.wait_ge(p_cmp, n + 1)
                    dve.wait_ge(imp_mm, n + 1)
                    dve.tensor_copy(m.imp, pb[5][:, 160:192]).then_inc(sel_step, 1)
                    dve.wait_ge(sel_step, n * SEL_STEPS + 1)
                    dve.memset(m.imp[:, 0:NBLK:NBLK - 1], FORCE).then_inc(sel_step, 1)
                    dve.wait_ge(sel_step, n * SEL_STEPS + 2)
                    ib = m.imp.unsqueeze(1).broadcast_to([P, NBLK, NBLK])
                    ia = m.imp.unsqueeze(2).broadcast_to([P, NBLK, NBLK])
                    dve.tensor_tensor(m.gt, ib, ia, ALU.is_gt)
                    dve.tensor_tensor(m.eq, ib, ia, ALU.is_equal).then_inc(sel_step, 1)
                    dve.wait_ge(sel_step, n * SEL_STEPS + 3)
                    dve.tensor_tensor(m.eq, m.eq, bigconst(m, "before").rearrange("p (a b) -> p a b", a=NBLK),
                                      ALU.mult).then_inc(sel_step, 1)
                    dve.wait_ge(sel_step, n * SEL_STEPS + 4)
                    dve.tensor_tensor(m.gt, m.gt, m.eq, ALU.add).then_inc(sel_step, 1)
                    dve.wait_ge(sel_step, n * SEL_STEPS + 5)
                    dve.tensor_reduce(m.selb, m.gt, AX.X, ALU.add).then_inc(sems.rank, 1)
                    dve.wait_ge(sems.rank, n + 1)
                    dve.tensor_scalar(m.selb, m.selb, N_SELECT - 1.5, NEG, ALU.is_ge, ALU.mult)\
                       .then_inc(selb_ready, 1)
                    dve.wait_ge(scored, n * (2 * X) + 2 * X)
                    hold(dve, m, 1)
                    dve.tensor_tensor_reduce(m.sp[:, WIN0:WIN0 + WINDOW], bigconst(m, "s_win"), pb[4][:, :], 1.0,
                                             -3e38, ALU.add, ALU.max, mx[:, 5:6])
                    for x in range(4):
                        dve.wait_ge(pre_ready, n * 4 + (x + 1))
                        hold(dve, m, 2 + x)
                        last = dve.tensor_tensor_reduce(m.sp[:, 512 * x:512 * x + 512], m.sp[:, 512 * x:512 * x + 512],
                                                        pb[x][:, :], 1.0, -3e38, ALU.add, ALU.max, mx[:, x:x + 1])
                    last.then_inc(summed, 1)
                    dve.wait_ge(summed, n + 1)
                    dve.tensor_reduce(nmx[:, 0:1], mx[:, 0:5], AX.X, ALU.max, negate=True)
                    dve.tensor_reduce(nmx[:, 1:2], mx[:, 5:7], AX.X, ALU.max, negate=True).then_inc(mx_ready, 1)
                    dve.tensor_scalar(m.sp[:, CMP0:CMP0 + NBLK], m.cmpp, gate(0), None, ALU.mult)
                    dve.wait_ge(exped, n + 1)
                    dve.reciprocal(ssum, ssum).then_inc(f_step, 1)
                    dve.wait_ge(f_step, n * F_STEPS + 1)
                    dve.tensor_tensor(ssum, ssum, m.grow[:, bass.ds(n * 3 + 1, 2)], ALU.mult).then_inc(f_step, 1)
                    dve.wait_ge(f_step, n * F_STEPS + 2)
                    dve.sem_inc(f_ready, 1)
                    dve.tensor_scalar(m.sp[:, 0:NSL], m.sp[:, 0:NSL], ssum[:, 0:1], None, ALU.mult)\
                       .then_inc(p_ready, 1)
                    for x in range(X + 1):
                        dve.wait_ge(p_turned, n * (X + 1) + (x + 1))
                        if x < X:
                            dve.tensor_copy(m.spT[x % 2], pb[6 + x % 2][:, :]).then_inc(pt_ready, 1)
                        else:
                            dve.tensor_copy(m.spX[0:NS, 0:256], pb[6 + x % 2][0:NS, 0:256])
                            dve.tensor_copy(m.spX[0:NBLK, 256:384], pb[6 + x % 2][0:NBLK, 256:384])\
                               .then_inc(pt_ready, 1)

        @block.tensor
        def _(pe):
            for n in range(NP_):
                last = pe.matmul(pb[0][:, 24 * n:24 * n + 24], const(m, "tokrow")[0:NS, P * n:P * n + P],
                                 m.gates[0:NS, PTILES, :], start=True, stop=True)
            last.then_inc(g_mm, 1)
            with pe.Fori(0, NP_ // 2) as it:
                for q in range(2):
                    n = it * 2 + q
                    slot = [m.slot[2 * q], m.slot[2 * q + 1]]
                    pe.wait_ge(staged, n * 8 + 8)
                    for e in range(2):
                        pe.matmul(pb[5][64 * e:64 * e + 64, 128:160], m.qs[e],
                                         m.kcs[:, NBLK * e:NBLK * e + NBLK], start=True, stop=True)
                    for e in range(2):
                        for br in range(2):
                            last = pe.matmul(pb[5][64 * e:64 * e + 64, NS * br:NS * br + NS], m.qs[e],
                                             m.kT[:, br, SEQ:TOK], start=True, stop=True)
                    last.then_inc(n_scored, 1)

                    def turn_keys(u):
                        e, x = u // X, u % X
                        pe.wait_ge(k_packed, n * (2 * X) + (u + 1))
                        if u >= 2:
                            pe.wait_ge(k_kept, n * (2 * X) + (u - 1))
                        for mm in range(QUAD):
                            last = pe.transpose(pb[6 + u % 2][:, P * mm:P * mm + P],
                                                m.kst[u % 2][:, P * mm:P * mm + P], ident)
                        last.then_inc(k_turned, 1)

                    def scores(u):
                        e, x = u // X, u % X
                        pe.wait_ge(k_kept, n * (2 * X) + (u + 1))
                        if u == 0:
                            pe.wait_ge(bank0_free, n + 1)
                        pe.matmul(pb[x][64 * e:64 * e + 64, :], m.qs[e], m.skT[u % 2], start=True, stop=True)\
                          .then_inc(scored, 1)

                    for u in range(2 * X + 1):
                        if u < 2 * X:
                            turn_keys(u)
                        if u >= 1:
                            scores(u - 1)
                        if u == 5:
                            pe.wait_ge(p_cmp, n + 1)
                            pe.matmul(pb[5][:, 160:192], const(m, "headsum"), m.cmpp, start=True, stop=True)\
                              .then_inc(imp_mm, 1)

                    def turn_probs(x):
                        if x == 0:
                            pe.wait_ge(p_ready, n * 2 + 2)
                        if x >= 2:
                            pe.wait_ge(pt_ready, n * (X + 1) + (x - 1))
                        if x < X:
                            a = 512 * x if x < 4 else WIN0
                            for mm in range(QUAD):
                                last = pe.transpose(pb[6 + x % 2][:, P * mm:P * mm + P],
                                                    m.sp[:, a + P * mm:a + P * mm + P], ident)
                        else:
                            pe.transpose(pb[6 + x % 2][0:NBLK, 2 * P:3 * P], m.sp[:, CMP0:CMP0 + NBLK], ident)
                            pe.transpose(pb[6 + x % 2][0:NS, 0:P], m.sp[:, PAST:NSL], ident)
                            last = pe.transpose(pb[6 + x % 2][0:NS, P:2 * P], m.sp[:, WIN0 + WINDOW:CMP0], ident)
                        last.then_inc(p_turned, 1)

                    def values(x):
                        pe.wait_ge(pt_ready, n * (X + 1) + (x + 1))
                        if x < X:
                            for mm in range(QUAD):
                                for e in range(2):
                                    for g in range(NKV):
                                        a = 64 * e + 32 * g
                                        pe.matmul(pb[0][HD * g:HD * g + HD, a:a + 32],
                                                  slot[e][:, x, mm, P * g + HD:P * g + P],
                                                  m.spT[x % 2][:, P * mm + a:P * mm + a + 32],
                                                  start=(x == 0 and mm == 0 and e == 0), stop=False,
                                                  skip_group_check=True)
                        else:
                            for e in range(2):
                                for g in range(NKV):
                                    a, d = 64 * e + 32 * g, HD * g
                                    o = pb[0][d:d + HD, a:a + 32]
                                    pe.matmul(o, m.vcs[e][0:NBLK, d:d + HD],
                                              m.spX[0:NBLK, 2 * P + a:2 * P + a + 32],
                                              start=False, stop=False, skip_group_check=True)
                                    for br in range(2):
                                        last = pe.matmul(o, values_at(m, PTILES, br, NS)[:, d:d + HD],
                                                         m.spX[0:NS, P * br + a:P * br + a + 32],
                                                         start=False, stop=(e == 1 and br == 1),
                                                         skip_group_check=True)
                            last.then_inc(o_done, 1)

                    for x in range(X + 2):
                        if x <= X:
                            turn_probs(x)
                        if x >= 1:
                            values(x - 1)


def load_w_out(eng, m, sems, s):
    dst = m.wring[s].rearrange("p (k n) -> p k n", k=KT_D)
    src = m.w_out[0][:, 512 * s:512 * s + 512]
    for g in range(2):
        eng.dma_start(dst[HD * g:HD * g + HD, 0:HPG, :],
                      src[256 * g:256 * g + 256, :].rearrange("(j d) n -> d j n", d=HD)).then_inc(sems.ring_in[s], 16)
    eng.dma_start(dst[:, HPG:KT_D, :], src[512:D, :].rearrange("(k p) n -> p k n", p=P)).then_inc(sems.ring_in[s], 16)


def mlp(nc, m, sems, sem):
    pb = m.pb
    ident = const(m, "ident")
    gf_in = sem("gf_in")
    out_mm, h_ready, sq_ready, ssq_mm, var_ready, std_ready, rb_ready, hn_ready = (
        sem("out_mm"), sem("h_ready"), sem("sq_ready"), sem("ssq_mm"), sem("m_var"), sem("m_std"), sem("rb_ready"),
        sem("hn_ready"))
    up_mm, relu_done, a_ready = sem("up_mm"), sem("relu_done"), sem("a_ready")
    down_mm, down_kept = sem("down_mm"), sem("down_kept")
    y_turned, y_sq, y_var, y_std, y_rstd, y_part, y_done = (
        sem("y_turned"), sem("y_sq"), sem("y_var"), sem("y_std"), sem("y_rstd"), sem("y_part"), sem("y_done"))
    y_out = [sem("y_out0"), sem("y_out1")]
    gml = m.cols[:, 8:16]
    ysum = lambda i: m.small[:, 16 + 2 * i:18 + 2 * i]
    yv = lambda i: m.small[:, 32 + i:33 + i]
    W0 = 48

    with nc.Block() as block:
        @block.sync
        def _(sp):
            up = m.w_up[0].rearrange("(k p) n -> p k n", p=P)
            down = m.w_down[0].rearrange("(k p) n -> p k n", p=P)
            sp.dma_start(m.gfin, m.g_final.rearrange("(o d) -> o d", o=1).broadcast_to([P, D])).then_inc(gf_in, 16)
            for n in range(8):
                sp.wait_ge(out_mm, 4 * n + 4) if n < 2 else sp.wait_ge(up_mm, 4 * n - 4)
                sp.dma_start(m.wring[n % 2].rearrange("p (k n) -> p k n", k=KT_D), up[:, :, 512 * n:512 * n + 512])\
                  .then_inc(sems.ring_in[n % 2], 16)
            for n in range(8):
                sp.wait_ge(up_mm, 28 + 4 * n) if n < 2 else sp.wait_ge(down_mm, n - 1)
                sp.dma_start(m.wring[n % 2].rearrange("p (k n) -> p k n", k=FT), down[:, :, P * n:P * n + P])\
                  .then_inc(sems.ring_in[n % 2], 16)
            for i in range(TILES):
                sp.wait_ge(y_done, i + 1)
                if i < PTILES:
                    sp.dma_start(m.o_yp[0, P * i:P * i + P, :], m.yo[i % 2]).then_inc(y_out[i % 2], 16)
                else:
                    sp.dma_start(m.o_ys.rearrange("b t d -> (b t) d"), m.yo[i % 2][0:NS, :]).then_inc(y_out[i % 2], 16)
            sp.wait_ge(y_out[0], 48)
            sp.wait_ge(y_out[1], 32)

        @block.scalar
        def _(act):
            for dt in range(KT_D):
                act.wait_ge(h_ready, dt + 1)
                if dt >= 2:
                    act.wait_ge(ssq_mm, dt - 1)
                act.activation(m.sq[dt % 2], m.hT[:, dt, :], ACT.Square).then_inc(sq_ready, 1)
            act.wait_ge(var_ready, 1)
            act.activation(m.rb, m.var, ACT.Sqrt).then_inc(std_ready, 1)
            act.sem_inc(relu_done, 4)
            with act.Fori(0, 4) as it:
                for u in range(8):
                    act.wait_ge(up_mm, it * 8 + (u + 1))
                    for hf in range(2):
                        last = act.activation(m.aT[:, bass.ds(it * 8 + u, 1), HALF * hf:HALF * hf + HALF]
                                              .rearrange("p a t -> p (a t)"),
                                              pb[2 * (u % 4) + hf][:, 0:HALF], ACT.Relu)
                    last.then_inc(relu_done, 1)
            for i in range(TILES):
                n = rows(i)
                act.wait_ge(y_turned, i + 1)
                if i:
                    act.wait_ge(y_sq, i)
                for hf in range(2):
                    last = act.activation(m.aT[0:n, 2 * (i % 2) + hf, 0:512], pb[2 * (i % 4) + hf][0:n, :], ACT.Square,
                                          accum_out=ysum(i)[0:n, hf:hf + 1])
                last.then_inc(y_sq, 1)
                act.wait_ge(y_var, i + 1)
                act.activation(yv(i)[0:n, :], yv(i)[0:n, :], ACT.Sqrt).then_inc(y_std, 1)

        @block.vector
        def _(dve):
            for dt in range(KT_D):
                dve.wait_ge(out_mm, dt + 1)
                for hf in range(2):
                    h = m.hT[:, dt, HALF * hf:HALF * hf + HALF]
                    last = dve.tensor_tensor(h, pb[2 * (dt % 3) + hf][:, 0:HALF], h, ALU.add)
                last.then_inc(h_ready, 1)
            dve.wait_ge(ssq_mm, KT_D)
            for hf in range(2):
                last = dve.tensor_scalar(m.var[:, HALF * hf:HALF * hf + HALF], pb[6 + hf][:, 0:HALF], 1.0 / D, EPS,
                                         ALU.mult, ALU.add)
            last.then_inc(var_ready, 1)
            dve.wait_ge(std_ready, 1)
            dve.reciprocal(m.rb, m.rb).then_inc(rb_ready, 1)
            dve.wait_ge(rb_ready, 1)
            for k in range(KT_D):
                dve.scalar_tensor_tensor(out=m.hnT[:, k, :], in0=m.hT[:, k, :], scalar=gml[:, k:k + 1], in1=m.rb,
                                         op0=ALU.mult, op1=ALU.mult).then_inc(hn_ready, 1)
            with dve.Fori(0, 4) as it:
                for u in range(8):
                    dve.wait_ge(relu_done, it * 8 + (u + 5))
                    a = m.aT[:, bass.ds(it * 8 + u, 1), :].rearrange("p a t -> p (a t)")
                    dve.tensor_tensor(a, a, a, ALU.mult).then_inc(a_ready, 1)
            dve.sem_inc(down_kept, 2)
            with dve.Fori(0, 4) as it:
                for s in range(2):
                    dve.wait_ge(down_mm, it * 2 + (s + 1))
                    for hf in range(2):
                        h = m.hT[:, bass.ds(it * 2 + s, 1), HALF * hf:HALF * hf + HALF].rearrange("p a t -> p (a t)")
                        last = dve.tensor_tensor(h, pb[2 * s + hf][:, 0:HALF], h, ALU.add)
                    last.then_inc(down_kept, 1)
            dve.wait_ge(gf_in, 16)
            for i in range(TILES):
                n = rows(i)
                dve.wait_ge(y_sq, i + 1)
                dve.tensor_tensor(yv(i)[0:n, :], ysum(i)[0:n, 0:1], ysum(i)[0:n, 1:2], ALU.add).then_inc(y_part, 1)
                dve.wait_ge(y_part, 2 * i + 1)
                dve.tensor_scalar(yv(i)[0:n, :], yv(i)[0:n, :], 1.0 / D, EPS, ALU.mult, ALU.add).then_inc(y_var, 1)
                dve.wait_ge(y_std, i + 1)
                dve.reciprocal(yv(i)[0:n, :], yv(i)[0:n, :]).then_inc(y_part, 1)
                dve.wait_ge(y_part, 2 * i + 2)
                if i >= 2:
                    dve.wait_ge(y_out[i % 2], 16 * (i // 2))
                for hf in range(2):
                    last = dve.scalar_tensor_tensor(out=m.yo[i % 2][0:n, 512 * hf:512 * hf + 512],
                                                    in0=pb[2 * (i % 4) + hf][0:n, :], scalar=yv(i)[0:n, :],
                                                    in1=m.gfin[0:n, 512 * hf:512 * hf + 512], op0=ALU.mult,
                                                    op1=ALU.mult)
                last.then_inc(y_done, 1)

        @block.tensor
        def _(pe):
            def sum_squares(dt):
                pe.wait_ge(sq_ready, dt + 1)
                for hf in range(2):
                    last = pe.matmul(pb[6 + hf][:, 0:HALF], m.ones[:, :], m.sq[dt % 2][:, HALF * hf:HALF * hf + HALF],
                                     start=(dt == 0), stop=(dt == KT_D - 1))
                last.then_inc(ssq_mm, 1)

            for dt in range(KT_D):
                s = dt // 4
                if dt % 4 == 0:
                    pe.wait_ge(sems.ring_in[s], W0)
                if dt >= 3:
                    pe.wait_ge(h_ready, dt - 2)
                w = m.wring[s].rearrange("p (k n) -> p k n", k=KT_D)[:, :, P * (dt % 4):P * (dt % 4) + P]
                for hf in range(2):
                    for k in range(KT_D):
                        last = pe.matmul(pb[2 * (dt % 3) + hf][:, 0:HALF], w[:, k, :],
                                         m.mixT[:, k, HALF * hf:HALF * hf + HALF],
                                         start=(k == 0), stop=(k == KT_D - 1))
                last.then_inc(out_mm, 1)
                if dt >= 1:
                    sum_squares(dt - 1)
            sum_squares(KT_D - 1)
            pe.wait_ge(hn_ready, KT_D)
            with pe.Fori(0, 4) as it:
                for u in range(8):
                    s = u // 4
                    if u % 4 == 0:
                        pe.wait_ge(sems.ring_in[s], it * 16 + (W0 + 16))
                    pe.wait_ge(relu_done, it * 8 + (u + 1))
                    w = m.wring[s].rearrange("p (k n) -> p k n", k=KT_D)[:, :, P * (u % 4):P * (u % 4) + P]
                    for hf in range(2):
                        for k in range(KT_D):
                            last = pe.matmul(pb[2 * (u % 4) + hf][:, 0:HALF], w[:, k, :],
                                             m.hnT[:, k, HALF * hf:HALF * hf + HALF],
                                             start=(k == 0), stop=(k == KT_D - 1))
                    last.then_inc(up_mm, 1)
            pe.wait_ge(a_ready, FT)
            with pe.Fori(0, 4) as it:
                for s in range(2):
                    pe.wait_ge(sems.ring_in[s], it * 16 + (W0 + 80))
                    pe.wait_ge(down_kept, it * 2 + (s + 1))
                    w = m.wring[s].rearrange("p (k n) -> p k n", k=FT)
                    for hf in range(2):
                        for k in range(FT):
                            last = pe.matmul(pb[2 * s + hf][:, 0:HALF], w[:, k, :],
                                             m.aT[:, k, HALF * hf:HALF * hf + HALF],
                                             start=(k == 0), stop=(k == FT - 1))
                    last.then_inc(down_mm, 1)
            pe.wait_ge(down_kept, KT_D + 2)
            for i in range(TILES):
                n = rows(i)
                if i >= 4:
                    pe.wait_ge(y_done, i - 3)
                for k in range(KT_D):
                    last = pe.transpose(pb[2 * (i % 4) + k // 4][0:n, P * (k % 4):P * (k % 4) + P],
                                        m.hT[:, k, P * i:P * i + n], ident)
                last.then_inc(y_turned, 1)


INPUTS = ["x_prompt", "x_sample", "cache_cmp", "cache_slc", "state_win", "state_pool", "page_table", "g_attn", "w_in",
          "cmp_pe", "cmp_w1", "cmp_w2", "w_pool", "pool_scale", "w_out", "g_mlp", "w_up", "w_down", "g_final"]
OUTPUTS = [("o_yp", (1, SEQ, D)), ("o_ys", (NB_SEQ, DEC, D)),
           ("o_pcmp", (1, 1, SEQ, NKV, 2, HD)), ("o_pslc", (1, 1, SEQ, NKV, 2, HD)),
           ("o_pwin", (1, 1, SEQ, NKV, 2, HD)), ("o_ppool", (1, 1, HIST, 512)),
           ("o_scmp", (1, NB_SEQ, DEC, NKV, 2, HD)), ("o_sslc", (1, NB_SEQ, DEC, NKV, 2, HD)),
           ("o_swin", (1, NB_SEQ, WINDOW, NKV, 2, HD)), ("o_spool", (1, NB_SEQ, HIST, 512))]


def build(nc, m):
    with ExitStack() as ctx:
        place(nc, ctx, m)
        m.imp_g = m.spX[:, 0:96]

        def sem(name):
            return ctx.enter_context(nc.semaphore(name))

        sems = Mem()
        sems.const_in, sems.wpool_in, sems.w2_in = sem("const_in"), sem("wpool_in"), sem("w2_in")
        sems.out = sem("states_out")
        sems.ones_set = sem("ones_set")
        sems.raw_in = [sem("raw_in0"), sem("raw_in1")]
        sems.slc_in = [sem(f"slc_in{s}") for s in range(4)]
        sems.win_in = [sem(f"win_in{s}") for s in range(4)]
        sems.ring_in = [sem("ring_in0"), sem("ring_in1")]
        sems.gelu_sq, sems.rank = sem("gelu_sq"), sem("rank")
        project(nc, m, sems, sem)
        compress(nc, m, sems, sem)
        prompt(nc, m, sems, sem)
        sample(nc, m, sems, sem)
        mlp(nc, m, sems, sem)


def kernel(**inputs):
    import concourse.bacc as _bacc
    from concourse.bass_utils import run_bass_kernel_spmd as _run

    nc = _bacc.Bacc("TRN2", target_bir_lowering=False, num_devices=1)
    arrays, m = {}, Mem()
    for name in INPUTS:
        a = np.ascontiguousarray(inputs[name])
        arrays[f"in_{name}"] = a
        ap = nc.dram_tensor(f"in_{name}", a.shape, mybir.dt.from_np(a.dtype), kind="ExternalInput").ap()
        m.__dict__["w_in_d" if name == "w_in" else name] = ap
    for name, group in zip(("c_small", "c_big"), tables()):
        a = np.ascontiguousarray(np.concatenate(list(group.values()), axis=1))
        arrays[name] = a
        m.__dict__[name] = nc.dram_tensor(name, a.shape, F32, kind="ExternalInput").ap()
    for name, shape in OUTPUTS:
        m.__dict__[name] = nc.dram_tensor(name, shape, F32, kind="ExternalOutput").ap()
    build(nc, m)
    r = _run(nc, [arrays], core_ids=[0])
    return tuple(r.results[0][name] for name, _ in OUTPUTS)
```

```python
from contextlib import ExitStack

import concourse.bass as bass
from concourse import mybir
import numpy as np

ALU = mybir.AluOpType
ACT = mybir.ActivationFunctionType
AX = mybir.AxisListType
F32 = mybir.dt.float32
F32R = mybir.dt.float32r
BF16 = mybir.dt.bfloat16
I32 = mybir.dt.int32
U32 = mybir.dt.uint32

P = 128
D = 1024
KT_D = D // P
SEQ = 512
NB_SEQ = 8
DEC = 8
NS = NB_SEQ * DEC
TOK = SEQ + NS
HALF = TOK // 2
PTILES = SEQ // P
TILES = PTILES + 1
PAST = 2048
PAGE = 128
PAGES = PAST // PAGE
HD = 64
NKV = 2
HPG = 4
NH = NKV * HPG
KV = NKV * 2 * HD
BLK = 64
NBLK = PAST // BLK
PBLK = SEQ // BLK
N_SELECT = 16
WINDOW = 512
HID = 128
FF = 4096
FT = FF // P
PG = 128
POOLW = (2, 4, 8, 16)
HIST = 15
UEXT = HIST + SEQ
USAM = HIST + DEC
UW = UEXT + NB_SEQ * USAM
SCALE = HD ** -0.5
EPS = 1e-6
NEG = -1e30
FORCE = 5.0
Q0, KV0, GL0, U0, PROJ = 0, 512, 1280, 1304, 1816
ROWW = GL0 + 24 - KV0
CHUNK_L = 8
CHUNKS = BLK // CHUNK_L
LP = CHUNK_L // 2
CHUNKF = CHUNK_L * KV
QUAD = 4
SLOTF = 5 * QUAD * KV
GELU_C = 0.7978845608028654


def rows(i):
    return P if i < PTILES else NS


def tables():
    t = {}
    p = np.arange(P)
    t["ident"] = np.eye(P)
    x = np.arange(SEQ)[None, :] - (SEQ - P)
    t["negd"] = np.where(x <= p[:, None], x - p[:, None], NEG)
    q = np.arange(SEQ).reshape(PTILES, P).T[:, :, None]
    dist = q - (64 * (np.arange(PBLK)[None, None, :] + 1) - 1)
    t["cmpd"] = np.where(dist >= 0, -dist, NEG).reshape(P, -1)
    t["cmpm"] = (dist >= 0).astype(float).reshape(P, -1)
    t["slopes"] = np.broadcast_to(2.0 ** -(np.arange(NH) + 1.0), (P, NH))
    t["corr"] = np.stack([np.broadcast_to(w / np.minimum(w, np.arange(16) + 1.0), (P, 16)) for w in POOLW],
                         1).reshape(P, -1)
    t["page4"] = (p[:, None] // 32 == np.arange(4)[None]).astype(float)
    t["page64"] = (p[:, None] // 2 == np.arange(64)[None]).astype(float)
    t["quad"] = (p % 32)[:, None].astype(float)
    t["chunk"] = ((p % 2) * CHUNKS)[:, None] + np.arange(CHUNKS)[None] * 1.0
    seq, g, h, tt = p // 64, (p // 32) % 2, (p // 8) % 4, p % 8
    head = g * HPG + h
    slope = 2.0 ** -(head + 1.0)
    end = 64 * (np.arange(NBLK) + 1) - 1
    t["s_cmp"] = -slope[:, None] * (PAST + tt[:, None] - end[None])
    same = (seq[:, None] == seq[None]) & (g[:, None] == g[None]) & (tt[:, None] == tt[None])
    t["headsum"] = same.astype(float)
    t["headrow"] = (head[:, None] == np.arange(NH)[None]).astype(float)
    tok = np.arange(NS)
    pair = np.arange(NB_SEQ // 2)
    d = tt[:, None, None] - (tok % 8)[None, None]
    ok = ((2 * pair[None, :, None] + seq[:, None, None]) == (tok // 8)[None, None]) & (d >= 0)
    t["s_new"] = np.where(ok, -slope[:, None, None] * d, NEG).reshape(P, -1)
    sel = np.zeros((P, len(pair), P))
    for a in pair:
        sel[(2 * a + seq) * 8 + tt, a, p] = 1.0
    t["tokrow"] = sel.reshape(P, -1)
    small = {k: np.ascontiguousarray(v, dtype=np.float32) for k, v in t.items()}
    big = {}
    pos = (np.arange(4)[:, None, None] * 512 + 4 * p[None, None, :] + np.arange(4)[None, :, None]).reshape(-1)
    big["s_slc"] = -slope[:, None] * (PAST + tt[:, None] - pos[None])
    r = (4 * p[None, :] + np.arange(4)[:, None]).reshape(-1)
    dw = WINDOW + tt[:, None] - r[None]
    big["s_win"] = np.where((dw >= 0) & (dw < WINDOW), -slope[:, None] * dw, NEG)
    i = np.arange(NBLK)
    big["before"] = np.broadcast_to((i[None, :] < i[:, None]).astype(float).reshape(1, -1), (P, NBLK * NBLK))
    big = {k: np.ascontiguousarray(v, dtype=np.float32) for k, v in big.items()}
    return small, big


def columns(t):
    at, out = 0, {}
    for k, v in t.items():
        out[k] = (at, v.shape[1])
        at += v.shape[1]
    return out, at


class Mem:
    pass


def view(v, *shape):
    if len(shape) == 1:
        return v
    names = "abcd"[:len(shape)]
    return v.rearrange(f"p ({' '.join(names)}) -> p {' '.join(names)}", **dict(zip(names, shape)))


LOW = 10432


def place(nc, ctx, m):
    def sb(name, shape, dt=F32):
        return ctx.enter_context(nc.sbuf_tensor(name, shape, dt))

    small, _ = tables()
    m.ccols, cw = columns(small)
    m.consts = sb("consts", [P, cw])
    m.hT = sb("hT", [P, KT_D, TOK])
    m.mixT = sb("mixT", [P, KT_D, TOK])
    m.small = sb("small", [P, 160])
    m.cols = sb("cols", [P, 20])
    m.zeros = sb("zeros", [1, 640], BF16)
    m.ones = sb("ones", [P, P])
    m.low = sb("low", [P, LOW])
    m.raw_w = [view(m.low[:, 4096 * s:4096 * s + 4096], KT_D, 512) for s in range(2)]
    m.gfin = m.low[:, 8192:8192 + D]
    m.sq = [m.low[:, 9216 + TOK * s:9216 + TOK * (s + 1)] for s in range(2)]
    m.pb = [ctx.enter_context(nc.psum_tensor(f"bank{i}", [P, 512], F32)) for i in range(8)]
    m.junk = m.mixT[:, 4:6, :].rearrange("p a b -> p (a b)")[:, 0:D]


def place_attention(nc, ctx, m):
    def sb(name, shape, dt=F32):
        return ctx.enter_context(nc.sbuf_tensor(name, shape, dt))

    _, big = tables()
    m.bcols, bw = columns(big)
    m.rowsT = sb("rowsT", [P, TILES, ROWW])
    m.qT = sb("qT", [P, HPG, TOK])
    m.kT = sb("kT", [P, 2, TOK])
    m.kcT = sb("kcT", [P, NB_SEQ * NBLK + PBLK])
    vcw = sb("vc_wpool", [P, (NB_SEQ + 1) * P])
    m.vc = vcw[0:NBLK, :].rearrange("p (b d) -> p b d", d=P)
    m.wpool = vcw[:, 0:4 * PG].rearrange("p (g d) -> p g d", d=PG)
    m.w2 = sb("w2", [P, 2, HD])
    m.peT = sb("peT", [P, BLK])
    m.gates = sb("gates", [P, TILES, 24])
    m.grow = sb("grow", [P, 12])
    m.tab = sb("tab", [P, NB_SEQ * PAGES], I32)
    m.idx_cmp = sb("idx_cmp", [P, 2, CHUNKS], U32)
    m.idx_slc = sb("idx_slc", [P, NB_SEQ * 4], U32)
    m.zone = sb("zone", [P, 31200 - LOW])

    def at(a, *shape):
        n = int(np.prod(shape))
        return view(m.low[:, a:a + n] if a < LOW else m.zone[:, a - LOW:a - LOW + n], *shape)

    m.w_rows = at(0, KT_D, ROWW)
    m.w_q = at(KT_D * ROWW, KT_D, 512)
    m.w_u = at(LOW, KT_D, 512)
    m.uT = at(14528, 4, UW)
    m.pa = at(14528 + 4 * UW, UW)
    m.pbuf = at(14528 + 5 * UW, UW)
    m.spool = at(14528 + 6 * UW, 512)
    m.utok = at(14528 + 6 * UW, 3, 512)
    m.colrows = m.pbuf[0:20, 512:512 + P]
    m.x = at(20672, TILES, D)
    m.xnT = at(25792, KT_D, TOK)
    m.dT = m.mixT[:, 0:4, :]
    m.raw = [at(20672 + 5120 * s, 2, CHUNKF) for s in range(2)]
    m.w1 = [at(20672 + 5120 * s + 2 * CHUNKF, 2, LP, HID) for s in range(2)]
    m.blkT_p = at(14528, 2, BLK // 2, 2 * PBLK)
    m.blkT = [[at(15552 + 1024 * s + 512 * c, 512) for c in range(2)] for s in range(2)]
    m.pe_in = at(17600, P)
    m.hx = at(18000, 2, 2, NB_SEQ * NBLK // 1 + PBLK)
    m.ht = at(0, 2, 2, NB_SEQ * NBLK + PBLK)
    m.slot = [at(SLOTF * s + (s // 2) * (LOW - 2 * SLOTF), 5, QUAD, KV) for s in range(4)]
    w = 20672
    m.cp = [at(w + 1024 * s, 2, 512) for s in range(3)]
    m.cpT = [at(w + 3072 + 1024 * s, 2, 512) for s in range(2)]
    m.pre = [at(w + 5120 + 1024 * s, 2, 512) for s in range(2)]
    m.qst = [at(w + 7168 + 512 * s, 512) for s in range(2)]
    m.cc = at(w + 8192, 2, PTILES, PBLK)
    m.ccT = at(w + 8256, 2, 512)
    m.skT = [at(w + 512 * s, 512) for s in range(2)]
    m.kst = [at(w + 1024 + 512 * s, 512) for s in range(2)]
    m.sp = at(w + 2048, 2720)
    m.spT = [at(w + 4768 + 512 * s, 512) for s in range(2)]
    m.spX = at(w + 5792, 384)
    m.big = at(w + 6176, bw)
    m.qs = [at(w + 9760 + 64 * s, 64) for s in range(2)]
    m.vcs = [at(w + 9888 + 128 * s, 128) for s in range(2)]
    m.cmpp = at(w + 10144, 32)
    m.imp = at(w + 10176, 32)
    m.selb = at(w + 10208, 32)
    m.snew = at(w + 10240, 64)
    m.kcs = at(w + 10304, 64)
    m.gt = at(w + 2048, NBLK, NBLK)
    m.eq = at(w + 2048 + 1024, NBLK, NBLK)


def place_mlp(nc, ctx, m):
    def sb(name, shape, dt=F32):
        return ctx.enter_context(nc.sbuf_tensor(name, shape, dt))

    m.xh, m.xl = sb("xh", [P, KT_D, TOK], F32R), sb("xl", [P, KT_D, TOK], F32R)
    m.wh, m.wl = sb("wh", [P, 4, KT_D * P], F32R), sb("wl", [P, 4, KT_D * P], F32R)
    m.ah, m.al = sb("ah", [P, KT_D, TOK], F32R), sb("al", [P, KT_D, TOK], F32R)
    m.tmp = sb("tmp", [P, 4 * TOK])
    m.relu = [m.tmp[:, TOK * s:TOK * s + TOK] for s in range(2)]
    m.act = [m.tmp[:, TOK * (2 + s):TOK * (3 + s)] for s in range(2)]
    m.yo = [m.tmp[:, D * s:D * s + D] for s in range(2)]
    m.norm = sb("norm", [P, 2, TOK])
    m.var, m.rb = m.norm[:, 0, :], m.norm[:, 1, :]


def const(m, name):
    a, n = m.ccols[name]
    return m.consts[:, a:a + n]


def bigconst(m, name):
    a, n = m.bcols[name]
    return m.big[:, a:a + n]


def keys(m, i, br, n=P):
    return m.rowsT[0:n, i, KV * (br + 1):KV * (br + 1) + P]


def values_at(m, i, br, n=P):
    return m.rowsT[0:n, i, KV * (br + 1) + P:KV * (br + 2)]


def hold(dve, m, k):
    dve.memset(m.small[:, 150 + k:151 + k], 0.0)


def load_slot(eng, m, s, b, sems):
    cache = m.cache_slc.rearrange("l n (r q) g c d -> (l n r) (q g c d)", q=QUAD)
    for pg in range(4):
        eng.indirect_dma_start(m.slot[s][:, pg, :, :].rearrange("p q c -> p (q c)"), None, cache,
                               bass.IndirectOffsetOnAxis(ap=m.idx_slc[:, b * 4 + pg:b * 4 + pg + 1], axis=0))\
           .then_inc(sems.slc_in[s], 16)


def load_window(eng, m, s, b, sems):
    eng.dma_start(m.slot[s][:, 4, :, :].rearrange("p q c -> p (q c)"),
                  m.state_win[0, b].rearrange("(p q) g c d -> p (q g c d)", q=QUAD)).then_inc(sems.win_in[s], 16)


def project(nc, m, sems, sem):
    g = m
    pb = m.pb
    ident = const(m, "ident")
    x_in = [sem(f"x_in{i}") for i in range(TILES)]
    table_in, rowsw_in, uw_in, qw_in = sem("table_in"), sem("rowsw_in"), sem("uw_in"), sem("qw_in")
    spool_in, cols_in, cols_turned, cols_kept = sem("spool_in"), sem("cols_in"), sem("cols_turned"), sem("cols_kept")
    ss_clear, ss_ready, var_ready, std_ready, rstd_ready = (
        sem("ss_clear"), sem("ss_ready"), sem("var_ready"), sem("std_ready"), sem("rstd_ready"))
    raw_turned, xt_kept, xn_ready, xn_turned, xnt_ready = (
        sem("raw_turned"), sem("xt_kept"), sem("xn_ready"), sem("xn_turned"), sem("xnt_ready"))
    rows_mm, rows_kept, tile_mm, tile_kept = sem("rows_mm"), sem("rows_kept"), sem("tile_mm"), sem("tile_kept")
    sp_turned, sp_kept, upad = sem("sp_turned"), sem("sp_kept"), sem("upad")
    ut_turned, ut_kept, pool_step, d_ready, pool_mm = (
        sem("ut_turned"), sem("ut_kept"), sem("pool_step"), sem("d_ready"), sem("pool_mm"))
    pool_kept, egate, gate1, idx_step = sem("pool_kept"), sem("egate"), sem("gate1"), sem("idx_step")
    ss, rstd = m.small[:, 0:TILES], m.small[:, 8:8 + TILES]
    var = m.small[:, 16:16 + TILES]
    ga, psc = m.cols[:, 0:8], m.cols[:, 16:20]
    pgc = m.small[:, 56:58]
    pgs = m.small[:, 64:96]

    with nc.Block() as block:
        @block.sync
        def _(sp):
            sp.dma_start(m.x[:, 0, :], m.x_prompt[0, 0:P, :]).then_inc(x_in[0], 16)
            sp.dma_start(m.consts[:, :], m.c_small).then_inc(sems.const_in, 16)
            for i in range(1, PTILES):
                sp.dma_start(m.x[:, i, :], m.x_prompt[0, P * i:P * i + P, :]).then_inc(x_in[i], 16)
            sp.dma_start(m.x[0:NS, PTILES, :], m.x_sample.rearrange("b t d -> (b t) d")).then_inc(x_in[PTILES], 16)
            for a, src in ((0, m.g_attn), (8, m.g_mlp), (16, m.pool_scale)):
                n = src.shape[1] // P
                sp.dma_start(m.colrows[a:a + n, :], src.rearrange("l (k p) -> (l k) p", p=P)).then_inc(cols_in, 16)
            wv = m.w_in_d[0].rearrange("(k p) n -> p k n", p=P)
            for k in range(0, KT_D, 4):
                sp.dma_start(m.w_rows[:, k:k + 4, :], wv[:, k:k + 4, KV0:U0]).then_inc(rowsw_in, 16)
            sp.dma_start(m.tab[:, :], m.page_table.rearrange("(o b) n -> o (b n)", o=1).broadcast_to([P, P]))\
              .then_inc(table_in, 16)
            sp.dma_start(m.w_u, wv[:, :, U0:PROJ]).then_inc(uw_in, 16)
            sp.dma_start(m.spool[0:NB_SEQ * HIST, :], m.state_pool[0].rearrange("b r c -> (b r) c"))\
              .then_inc(spool_in, 16)
            for g in range(NKV):
                for k in range(KT_D):
                    sp.dma_start(m.w_q[:, k, :].rearrange("p (j g d) -> p g j d", g=NKV, j=HPG)[:, g],
                                 wv[:, k, 256 * g:256 * g + 256].rearrange("p (j d) -> p j d", j=HPG))\
                      .then_inc(qw_in, 16)
            sp.dma_start(m.wpool[:, :, :], m.w_pool[0].rearrange("g c d -> c g d")).then_inc(sems.wpool_in, 16)
            sp.dma_start(m.w2[:, :, :], m.cmp_w2[0].rearrange("c h d -> h c d")).then_inc(sems.w2_in, 16)
            for b in range(NB_SEQ):
                sp.dma_start(m.o_swin[0, b, 0:WINDOW - DEC].rearrange("(a r) g c d -> a (r g c d)", a=28),
                             m.state_win[0, b, DEC:WINDOW].rearrange("(a r) g c d -> a (r g c d)", a=28))\
                  .then_inc(sems.out, 16)
            sp.wait_ge(rows_kept, 2 * TILES)
            sp.dma_start(m.o_pcmp[0, 0].rearrange("(i p) g c d -> p i (g c d)", p=P), m.rowsT[:, 0:PTILES, 0:KV])\
              .then_inc(sems.out, 16)
            sp.dma_start(m.o_scmp[0].rearrange("b t g c d -> (b t) (g c d)"), m.rowsT[0:NS, PTILES, 0:KV])\
              .then_inc(sems.out, 16)
            cgd = lambda v: v.rearrange("p (c g d) -> p g c d", c=2, g=NKV)
            for i in range(PTILES):
                for br, po in ((1, m.o_pslc), (2, m.o_pwin)):
                    for g in range(NKV):
                        sp.dma_start(po[0, 0, P * i:P * i + P, g], cgd(m.rowsT[:, i, KV * br:KV * br + KV])[:, g])\
                          .then_inc(sems.out, 16)
            for g in range(NKV):
                sp.dma_start(m.o_sslc[0].rearrange("b t g c d -> (b t) g c d")[:, g],
                             cgd(m.rowsT[0:NS, PTILES, KV:2 * KV])[:, g]).then_inc(sems.out, 16)
                for b in range(NB_SEQ):
                    sp.dma_start(m.o_swin[0, b, WINDOW - DEC:WINDOW, g],
                                 cgd(m.rowsT[b * DEC:(b + 1) * DEC, PTILES, 2 * KV:3 * KV])[:, g])\
                      .then_inc(sems.out, 16)
            sp.wait_ge(ut_kept, 3)
            for b in range(NB_SEQ):
                a = USAM * (b % 4) + DEC
                sp.dma_start(m.o_spool[0, b], m.utok[a:a + HIST, b // 4, :]).then_inc(sems.out, 16)
            sp.dma_start(m.o_ppool[0, 0], m.utok[0:HIST, 2, :]).then_inc(sems.out, 16)
            sems.n_out = 16 * (NB_SEQ + 2 + 4 * PTILES + 2 + 2 * NB_SEQ + NB_SEQ + 1)
            sp.wait_ge(sems.out, sems.n_out)

        @block.gpsimd
        def _(pool):
            pool.memset(m.zeros[:, :], 0.0).then_inc(sems.ones_set, 1)
            pool.memset(m.ones[:, :], 1.0).then_inc(sems.ones_set, 1)
            pool.memset(m.uT[:, :, 0:HIST], 0.0).then_inc(upad, 1)
            pool.wait_ge(idx_step, 7)
            pool.wait_ge(xn_turned, 2 * TILES)
            load_chunk(pool, m, sems, 0)

        @block.scalar
        def _(act):
            act.wait_ge(ss_clear, 1)
            for i in range(TILES):
                n = rows(i)
                act.wait_ge(x_in[i], 16)
                if i:
                    act.wait_ge(ss_ready, i)
                act.activation(m.junk[0:n, :], m.x[0:n, i, :], ACT.Square, accum_out=ss[0:n, i:i + 1])\
                   .then_inc(ss_ready, 1)
                for kk in range(2):
                    u = 2 * i + kk
                    act.wait_ge(raw_turned, u + 1)
                    act.activation(m.hT[:, 4 * kk:4 * kk + 4, P * i:P * i + n],
                                   pb[u % 4][:, :].rearrange("p (k t) -> p k t", k=4)[:, :, 0:n], ACT.Copy)\
                       .then_inc(xt_kept, 1)
            act.wait_ge(var_ready, 1)
            act.activation(rstd, var, ACT.Sqrt).then_inc(std_ready, 1)
            for u in range(2 * TILES):
                i, n = u // 2, rows(u // 2)
                act.wait_ge(rows_mm, u + 1)
                if u % 2 == 0:
                    act.activation(m.rowsT[0:n, i, 0:KV], pb[u % 4][0:n, 0:KV], ACT.Copy)
                    act.activation(m.rowsT[0:n, i, KV:2 * KV].rearrange("p (c g d) -> p g c d", c=2, g=NKV),
                                   pb[u % 4][0:n, KV:2 * KV].rearrange("p (g c d) -> p g c d", c=2, g=NKV), ACT.Copy)\
                       .then_inc(rows_kept, 1)
                else:
                    act.activation(m.rowsT[0:n, i, 2 * KV:3 * KV].rearrange("p (c g d) -> p g c d", c=2, g=NKV),
                                   pb[u % 4][0:n, 0:KV].rearrange("p (g c d) -> p g c d", c=2, g=NKV), ACT.Copy)
                    act.activation(m.rowsT[0:n, i, 3 * KV:ROWW], pb[u % 4][0:n, KV:ROWW - 2 * KV], ACT.Copy)\
                       .then_inc(rows_kept, 1)
            act.wait_ge(rows_kept, 2 * TILES)
            act.activation(m.gates[:, 0:PTILES, :], m.rowsT[:, 0:PTILES, 3 * KV:ROWW], ACT.Exp, scale=-1.0)\
               .then_inc(egate, 1)
            act.activation(m.gates[0:NS, PTILES, :], m.rowsT[0:NS, PTILES, 3 * KV:ROWW], ACT.Exp, scale=-1.0)\
               .then_inc(egate, 1)
            for e, n in ((0, 4 * USAM), (1, 4 * USAM), (2, HIST)):
                act.wait_ge(ut_turned, e + 1)
                act.activation(m.utok[0:n, e, :], pb[1 + e][0:n, :], ACT.Copy).then_inc(ut_kept, 1)
            act.wait_ge(cols_kept, 1)
            for gi in range(4):
                act.wait_ge(pool_mm, gi + 1)
                for hf in range(2):
                    last = act.activation(m.mixT[:, 4 + gi, HALF * hf:HALF * hf + HALF],
                                          pb[4 + 2 * (gi % 2) + hf][:, 0:HALF], ACT.Identity, scale=psc[:, gi:gi + 1])
                last.then_inc(pool_kept, 1)

        @block.vector
        def _(dve):
            dve.memset(ss, 1.0).then_inc(ss_clear, 1)
            dve.wait_ge(ss_ready, TILES)
            dve.tensor_scalar(var, ss, 1.0 / D, EPS, ALU.mult, ALU.add).then_inc(var_ready, 1)
            dve.wait_ge(std_ready, 1)
            dve.reciprocal(rstd, rstd).then_inc(rstd_ready, 1)
            dve.wait_ge(rstd_ready, 1)
            for i in range(TILES):
                n = rows(i)
                dve.wait_ge(raw_turned, 2 * i + 2)
                dve.tensor_scalar(m.x[0:n, i, :], m.x[0:n, i, :], rstd[0:n, i:i + 1], None, ALU.mult)\
                   .then_inc(xn_ready, 1)
            dve.wait_ge(cols_turned, 1)
            dve.tensor_copy(m.cols[:, :], pb[7][:, 0:20]).then_inc(cols_kept, 1)
            dve.wait_ge(cols_kept, 1)
            for u in range(2 * TILES):
                i, kk, n = u // 2, u % 2, rows(u // 2)
                dve.wait_ge(xn_turned, u + 1)
                dve.tensor_tensor(m.xnT[:, 4 * kk:4 * kk + 4, P * i:P * i + n],
                                  pb[4 + u % 4][:, :].rearrange("p (k t) -> p k t", k=4)[:, :, 0:n],
                                  ga[:, 4 * kk:4 * kk + 4].unsqueeze(2).broadcast_to([P, 4, n]), ALU.mult)\
                   .then_inc(xnt_ready, 1)
            dve.wait_ge(table_in, 16)
            dve.wait_ge(sems.const_in, 16)
            tf, t2 = m.pa[:, 0:P], m.pbuf[:, 0:P]
            dve.tensor_copy(tf, m.tab[:, :]).then_inc(idx_step, 1)
            dve.wait_ge(idx_step, 1)
            dve.tensor_tensor(t2.rearrange("p (a k) -> p a k", k=4), tf.rearrange("p (a k) -> p a k", k=4),
                              const(m, "page4").unsqueeze(1).broadcast_to([P, 32, 4]), ALU.mult).then_inc(idx_step, 1)
            dve.wait_ge(idx_step, 2)
            dve.tensor_reduce(pgs, t2.rearrange("p (a k) -> p a k", k=4), AX.X, ALU.add).then_inc(idx_step, 1)
            dve.wait_ge(idx_step, 3)
            dve.tensor_scalar(m.idx_slc[:, :], pgs, 32.0, const(m, "quad"), ALU.mult, ALU.add).then_inc(idx_step, 1)
            dve.tensor_tensor(t2.rearrange("p (a k) -> p a k", k=64), tf.rearrange("p (a k) -> p a k", k=64),
                              const(m, "page64").unsqueeze(1).broadcast_to([P, 2, 64]), ALU.mult).then_inc(idx_step, 1)
            dve.wait_ge(idx_step, 5)
            dve.tensor_reduce(pgc, t2.rearrange("p (a k) -> p a k", k=64), AX.X, ALU.add).then_inc(idx_step, 1)
            dve.wait_ge(idx_step, 6)
            dve.scalar_tensor_tensor(out=m.idx_cmp[:, :, :], in0=pgc.unsqueeze(2).broadcast_to([P, 2, CHUNKS]),
                                     scalar=2.0 * CHUNKS,
                                     in1=const(m, "chunk").unsqueeze(1).broadcast_to([P, 2, CHUNKS]),
                                     op0=ALU.mult, op1=ALU.add).then_inc(idx_step, 1)
            dve.wait_ge(sp_turned, 1)
            dve.tensor_copy(m.uT[:, :, UEXT:UW].rearrange("p g (b r) -> p g b r", b=NB_SEQ)[:, :, :, 0:HIST],
                            pb[0][:, 0:480].rearrange("p (g b r) -> p g b r", g=4, b=NB_SEQ)).then_inc(sp_kept, 1)
            for u in range(8):
                dve.wait_ge(tile_mm, u + 1)
                a, b = pb[4 + 2 * (u % 2)], pb[5 + 2 * (u % 2)]
                if u < 4:
                    dve.tensor_copy(m.uT[:, u, HIST:HIST + HALF], a[:, 0:HALF])
                    dve.tensor_copy(m.uT[:, u, HIST + HALF:UEXT], b[:, 0:SEQ - HALF])
                    dve.tensor_copy(m.uT[:, u, UEXT:UW].rearrange("p (b r) -> p b r", b=NB_SEQ)[:, :, HIST:USAM],
                                    b[:, SEQ - HALF:HALF].rearrange("p (b t) -> p b t", b=NB_SEQ))\
                       .then_inc(tile_kept, 1)
                else:
                    dve.tensor_scalar(m.qT[:, u - 4, 0:HALF], a[:, 0:HALF], SCALE, None, ALU.mult)
                    dve.tensor_scalar(m.qT[:, u - 4, HALF:TOK], b[:, 0:HALF], SCALE, None, ALU.mult)\
                       .then_inc(tile_kept, 1)
            dve.wait_ge(upad, 1)
            dve.wait_ge(sp_kept, 1)
            dve.wait_ge(tile_kept, 4)
            steps = 0
            for gi, w in enumerate(POOLW):
                src, dst, other = m.uT[:, gi, :], m.pa, m.pbuf
                s = 1
                while s < w:
                    if steps:
                        dve.wait_ge(pool_step, steps)
                    dve.tensor_tensor(dst[:, 2 * s - 1:UW], src[:, 2 * s - 1:UW], src[:, s - 1:UW - s], ALU.add)\
                       .then_inc(pool_step, 1)
                    steps += 1
                    src, dst, other = dst, other, dst
                    s *= 2
                dve.wait_ge(pool_step, steps)
                dve.tensor_tensor(src[:, HIST:HIST + 16], src[:, HIST:HIST + 16],
                                  const(m, "corr")[:, 16 * gi:16 * gi + 16], ALU.mult).then_inc(pool_step, 1)
                steps += 1
                dve.wait_ge(pool_step, steps)
                sam = lambda v: v[:, UEXT:UW].rearrange("p (b r) -> p b r", b=NB_SEQ)[:, :, HIST:USAM]
                dve.scalar_tensor_tensor(out=m.dT[:, gi, 0:SEQ], in0=src[:, HIST:UEXT], scalar=1.0 / w,
                                         in1=m.uT[:, gi, HIST:UEXT], op0=ALU.mult, op1=ALU.subtract)\
                   .then_inc(pool_step, 1)
                dve.scalar_tensor_tensor(out=m.dT[:, gi, SEQ:TOK].rearrange("p (b t) -> p b t", b=NB_SEQ),
                                         in0=sam(src), scalar=1.0 / w, in1=sam(m.uT[:, gi, :]),
                                         op0=ALU.mult, op1=ALU.subtract).then_inc(pool_step, 1)
                steps += 2
                dve.wait_ge(pool_step, steps)
                dve.sem_inc(d_ready, 1)
            dve.wait_ge(egate, 2)
            dve.tensor_scalar(m.gates[:, 0:PTILES, :], m.gates[:, 0:PTILES, :], 1.0, None, ALU.add).then_inc(gate1, 1)
            dve.tensor_scalar(m.gates[0:NS, PTILES, :], m.gates[0:NS, PTILES, :], 1.0, None, ALU.add)\
               .then_inc(gate1, 1)
            dve.wait_ge(gate1, 2)
            dve.reciprocal(m.gates[:, 0:PTILES, :], m.gates[:, 0:PTILES, :])
            dve.reciprocal(m.gates[0:NS, PTILES, :], m.gates[0:NS, PTILES, :]).then_inc(gate1, 1)

        @block.tensor
        def _(pe):
            pe.wait_ge(sems.const_in, 16)
            for u in range(2 * TILES):
                i, kk, n = u // 2, u % 2, rows(u // 2)
                if kk == 0:
                    pe.wait_ge(x_in[i], 16)
                if u >= 4:
                    pe.wait_ge(xt_kept, u - 3)
                for k in range(4):
                    last = pe.transpose(pb[u % 4][:, P * k:P * k + n],
                                        m.x[0:n, i, P * (4 * kk + k):P * (4 * kk + k) + P], ident[0:n, 0:n])
                last.then_inc(raw_turned, 1)

            pe.wait_ge(cols_in, 48)
            pe.transpose(pb[7][:, 0:20], m.colrows, ident[0:20, 0:20]).then_inc(cols_turned, 1)

            def turn_normed(u):
                i, kk, n = u // 2, u % 2, rows(u // 2)
                pe.wait_ge(xn_ready, i + 1)
                if u == 3:
                    pe.wait_ge(cols_kept, 1)
                if u >= 4:
                    pe.wait_ge(xnt_ready, u - 3)
                for k in range(4):
                    last = pe.transpose(pb[4 + u % 4][:, P * k:P * k + n],
                                        m.x[0:n, i, P * (4 * kk + k):P * (4 * kk + k) + P], ident[0:n, 0:n])
                last.then_inc(xn_turned, 1)

            def project_rows(u):
                i, n = u // 2, rows(u // 2)
                if u == 0:
                    pe.wait_ge(rowsw_in, 32)
                if u % 2 == 0:
                    pe.wait_ge(xnt_ready, 2 * i + 2)
                if u < 4:
                    pe.wait_ge(xt_kept, 7 + u)
                else:
                    pe.wait_ge(rows_kept, u - 3)
                a, b = (0, 512) if u % 2 == 0 else (512, ROWW)
                for k in range(KT_D):
                    last = pe.matmul(pb[u % 4][0:n, 0:b - a], m.xnT[:, k, P * i:P * i + n], m.w_rows[:, k, a:b],
                                     start=(k == 0), stop=(k == KT_D - 1))
                last.then_inc(rows_mm, 1)

            for i in range(TILES):
                turn_normed(2 * i)
                turn_normed(2 * i + 1)
                if i:
                    project_rows(2 * i - 2)
                    project_rows(2 * i - 1)
            project_rows(2 * TILES - 2)
            project_rows(2 * TILES - 1)
            pe.wait_ge(spool_in, 16)
            pe.wait_ge(rows_kept, 9)
            for gi in range(4):
                last = pe.transpose(pb[0][:, 120 * gi:120 * gi + 120], m.spool[0:120, P * gi:P * gi + P],
                                    ident[0:120, 0:120])
            last.then_inc(sp_turned, 1)
            for u in range(8):
                if u == 0:
                    pe.wait_ge(xnt_ready, 2 * TILES)
                    pe.wait_ge(uw_in, 16)
                if u == 4:
                    pe.wait_ge(qw_in, 16 * NKV * KT_D)
                if u >= 2:
                    pe.wait_ge(tile_kept, u - 1)
                for hf in range(2):
                    for k in range(KT_D):
                        w = m.w_u[:, k, PG * u:PG * u + PG] if u < 4 else m.w_q[:, k, P * (u - 4):P * (u - 3)]
                        last = pe.matmul(pb[4 + 2 * (u % 2) + hf][:, 0:HALF], w,
                                         m.xnT[:, k, HALF * hf:HALF * hf + HALF],
                                         start=(k == 0), stop=(k == KT_D - 1))
                last.then_inc(tile_mm, 1)
            pe.wait_ge(rows_kept, 2 * TILES)
            for e in range(2):
                for gi in range(4):
                    a = UEXT + 4 * USAM * e
                    last = pe.transpose(pb[1 + e][0:4 * USAM, P * gi:P * gi + P], m.uT[:, gi, a:a + 4 * USAM], ident)
                last.then_inc(ut_turned, 1)
            for gi in range(4):
                last = pe.transpose(pb[3][0:HIST, P * gi:P * gi + P], m.uT[:, gi, UEXT - HIST:UEXT], ident)
            last.then_inc(ut_turned, 1)
            pe.wait_ge(sems.wpool_in, 16)
            for gi in range(4):
                pe.wait_ge(d_ready, gi + 1)
                if gi < 2:
                    pe.wait_ge(tile_kept, 7 + gi)
                else:
                    pe.wait_ge(pool_kept, gi - 1)
                for hf in range(2):
                    last = pe.matmul(pb[4 + 2 * (gi % 2) + hf][:, 0:HALF], m.wpool[:, gi, :],
                                     m.dT[:, gi, HALF * hf:HALF * hf + HALF], start=True, stop=True)
                last.then_inc(pool_mm, 1)


def load_chunk(eng, m, sems, ck):
    cache = m.cache_cmp.rearrange("l n (h k q) g c d -> (l n h k) (q g c d)", h=2, k=CHUNKS)
    for hf in range(2):
        eng.indirect_dma_start(m.raw[ck % 2][:, hf, :], None, cache,
                               bass.IndirectOffsetOnAxis(ap=m.idx_cmp[:, hf, ck:ck + 1], axis=0))\
           .then_inc(sems.raw_in[ck % 2], 16)


def compress(nc, m, sems, sem):
    pb = m.pb
    ident = const(m, "ident")
    pe_in, pe_turned, pe_kept = sem("pe_in"), sem("pe_turned"), sem("pe_kept")
    w1_in = [sem("w1_in0"), sem("w1_in1")]
    kt_turned, kt_kept, pblk_turned, pblk_kept = (
        sem("kt_turned"), sem("kt_kept"), sem("pblk_turned"), sem("pblk_kept"))
    blk_turned, blk_kept, hid_done = sem("blk_turned"), [sem("blk_kept_k"), sem("blk_kept_v")], sem("hid_done")
    hx_ready, gelu, gtanh, kc_mm, kc_kept = (
        sem("hx_ready"), sem("gelu"), sem("gtanh"), sem("kc_mm"), sem("kc_kept"))
    NBT = NB_SEQ * NBLK

    with nc.Block() as block:
        @block.sync
        def _(sp):
            sp.dma_start(m.pe_in[0:BLK, :], m.cmp_pe[0].rearrange("l c d -> l (c d)")).then_inc(pe_in, 16)
            for ck in range(CHUNKS):
                s = ck % 2
                if ck >= 2:
                    sp.wait_ge(hid_done, 2 * LP * (ck - 1))
                for c in range(2):
                    sp.dma_start(m.w1[s][:, c, :, :],
                                 m.cmp_w1[0, c].rearrange("(k a q) d h -> k (q d) a h", k=CHUNKS, q=2)[ck])\
                      .then_inc(w1_in[s], 16)
            sp.wait_ge(gelu, 3)
            for b in range(2):
                load_window(sp, m, b, b, sems)

        @block.gpsimd
        def _(pool):
            for ck in range(1, CHUNKS):
                if ck >= 2:
                    pool.wait_ge(blk_turned, CHUNK_L * (ck - 1))
                load_chunk(pool, m, sems, ck)
            pool.wait_ge(gelu, 3)
            for b in range(2):
                load_slot(pool, m, b, b, sems)

        @block.scalar
        def _(act):
            act.wait_ge(pe_turned, 1)
            act.activation(m.peT[:, :], pb[7][:, 0:BLK], ACT.Copy)\
               .then_inc(pe_kept, 1)
            for br in range(2):
                act.wait_ge(kt_turned, br + 1)
                act.activation(m.kT[:, br, 0:SEQ], pb[4 + br][:, :], ACT.Copy).then_inc(kt_kept, 1)
            act.wait_ge(kt_turned, 3)
            act.activation(m.kT[:, :, SEQ:TOK], pb[6][:, 0:2 * NS].rearrange("p (b t) -> p b t", b=2), ACT.Copy)\
               .then_inc(kt_kept, 1)
            act.wait_ge(pe_kept, 1)
            with act.Fori(0, CHUNKS // 2) as it:
                for v in range(2 * CHUNK_L):
                    lo = HD * (v % 2)
                    act.wait_ge(blk_turned, it * (2 * CHUNK_L) + v + 1)
                    act.activation(m.blkT[(v // 2) % 2][0][lo:lo + HD, :], pb[4 + v % 4][0:HD, :], ACT.Identity,
                                   bias=m.peT[0:HD, bass.ds(it * (2 * CHUNK_L) + v, 1)]).then_inc(blk_kept[0], 1)
            act.wait_ge(hid_done, BLK)
            for c in range(2):
                act.activation(m.hx[:, c, :, 0:NBT // 1].rearrange("p g (h n) -> p h g n", h=2),
                               pb[c][:, :].rearrange("p (h g n) -> p h g n", h=2, g=2), ACT.Copy)\
                   .then_inc(hx_ready, 1)
            act.activation(m.hx[:, :, :, NBT:NBT + PBLK],
                           pb[2][:, 0:32].rearrange("p (c g n) -> p c g n", c=2, g=2), ACT.Copy).then_inc(hx_ready, 1)
            act.wait_ge(gelu, 2)
            act.activation(m.ht[:, :, :, :], m.ht[:, :, :, :], ACT.Tanh, scale=GELU_C).then_inc(gtanh, 1)
            act.wait_ge(kc_mm, 1)
            act.activation(m.kcT[:, :], pb[0][:, 0:NBT + PBLK], ACT.Copy, scale=0.5).then_inc(kc_kept, 1)

        @block.vector
        def _(dve):
            dve.wait_ge(pe_kept, 1)
            for g in range(2):
                dve.wait_ge(pblk_turned, g + 1)
                for c in range(2):
                    for par in range(2):
                        lo, hi = HD * c, HD * par
                        src = pb[g][lo:lo + HD, :].rearrange("p (b l q) -> p b l q", b=PBLK, q=2)[:, :, :, par]
                        dst = m.blkT_p[hi:hi + HD, c, :, PBLK * g:PBLK * g + PBLK].rearrange("p l b -> p b l")
                        pe_b = m.peT[lo:lo + HD, :].rearrange("p (l q) -> p l q", q=2)[:, :, par]
                        last = dve.tensor_tensor(dst, src, pe_b.unsqueeze(1).broadcast_to([HD, PBLK, BLK // 2]),
                                                 ALU.add)
                last.then_inc(pblk_kept, 1)
            with dve.Fori(0, CHUNKS // 2) as it:
                for v in range(2 * CHUNK_L):
                    lo = HD * (v % 2)
                    dve.wait_ge(blk_turned, it * (2 * CHUNK_L) + v + 1)
                    dve.tensor_scalar(m.blkT[(v // 2) % 2][1][lo:lo + HD, :], pb[4 + v % 4][HD:P, :],
                                      m.peT[HD:P, bass.ds(it * (2 * CHUNK_L) + v, 1)], None, ALU.add)\
                       .then_inc(blk_kept[1], 1)
            hx, ht = m.hx[:, :, :, :], m.ht[:, :, :, :]
            dve.wait_ge(hx_ready, 3)
            dve.tensor_tensor(ht, hx, hx, ALU.mult).then_inc(gelu, 1)
            dve.wait_ge(gelu, 1)
            sq = sems.gelu_sq
            dve.tensor_scalar(ht, ht, 0.044715, 1.0, ALU.mult, ALU.add).then_inc(sq, 1)
            dve.wait_ge(sq, 1)
            dve.tensor_tensor(ht, ht, hx, ALU.mult).then_inc(gelu, 1)
            dve.wait_ge(gtanh, 1)
            dve.scalar_tensor_tensor(out=hx, in0=ht, scalar=1.0, in1=hx, op0=ALU.add, op1=ALU.mult).then_inc(gelu, 1)
            for n in range(3):
                dve.wait_ge(kc_mm, n + 2)
                if n < 2:
                    dve.tensor_scalar(m.vc[:, 4 * n:4 * n + 4, :],
                                      pb[1 + n][0:NBLK, :].rearrange("p (b d) -> p b d", b=4), 0.5, None, ALU.mult)\
                       .then_inc(kc_kept, 1)
                else:
                    dve.tensor_scalar(m.vc[0:PBLK, NB_SEQ, :], pb[3][0:PBLK, 0:P], 0.5, None, ALU.mult)\
                       .then_inc(kc_kept, 1)

        @block.tensor
        def _(pe):
            pe.wait_ge(pe_in, 16)
            pe.transpose(pb[7][:, 0:BLK], m.pe_in[0:BLK, :], ident[0:BLK, 0:BLK]).then_inc(pe_turned, 1)
            for br in range(2):
                for i in range(PTILES):
                    last = pe.transpose(pb[4 + br][:, P * i:P * i + P], keys(m, i, br), ident)
                last.then_inc(kt_turned, 1)
            for br in range(2):
                last = pe.transpose(pb[6][:, NS * br:NS * br + NS], keys(m, PTILES, br, NS), ident[0:NS, 0:NS])
            last.then_inc(kt_turned, 1)
            for g in range(2):
                for i in range(PTILES):
                    last = pe.transpose(pb[g][:, P * i:P * i + P], m.rowsT[:, i, P * g:P * g + P], ident)
                last.then_inc(pblk_turned, 1)
            pe.wait_ge(pblk_kept, 2)
            pe.wait_ge(pe_kept, 1)
            pe.wait_ge(kt_kept, 3)
            for n in range(3):
                pe.matmul(pb[n][:, :], m.zeros[0:1, 0:P], m.zeros[0:1, P:P + 512], start=True, stop=True)

            with pe.Fori(0, CHUNKS // 2) as it:
                def turn(v):
                    s, l = v // CHUNK_L, v % CHUNK_L
                    if l == 0:
                        pe.wait_ge(sems.raw_in[s], it * 32 + 32)
                    for hg in range(4):
                        a = KV * l + P * (hg % 2)
                        last = pe.transpose(pb[4 + v % 4][:, P * hg:P * hg + P], m.raw[s][:, hg // 2, a:a + P], ident)
                    last.then_inc(blk_turned, 1)

                def hidden(p):
                    s, a = p // LP, p % LP
                    if a == 0:
                        pe.wait_ge(w1_in[s], it * 32 + 32)
                    for c in range(2):
                        pe.wait_ge(blk_kept[c], it * (2 * CHUNK_L) + (2 * p + 2))
                        w = m.w1[s][:, c, a, :]
                        pe.matmul(pb[2][:, 16 * c:16 * c + 16], w,
                                  m.blkT_p[:, c, bass.ds(it * (2 * LP) + p, 1), :].rearrange("p a b -> p (a b)"),
                                  start=False, stop=False, skip_group_check=True)
                        pe.matmul(pb[c][:, :], w, m.blkT[p % 2][c], start=False, stop=False, skip_group_check=True)\
                          .then_inc(hid_done, 1)

                for p in range(2 * LP):
                    turn(2 * p)
                    turn(2 * p + 1)
                    if p >= 1:
                        hidden(p - 1)
                hidden(2 * LP - 1)

            pe.wait_ge(gelu, 3)
            pe.wait_ge(sems.w2_in, 16)
            for g in range(2):
                last = pe.matmul(pb[0][HD * g:HD * g + HD, 0:NBT + PBLK], m.w2[:, 0, :], m.hx[:, 0, g, :],
                                 start=True, stop=True)
            last.then_inc(kc_mm, 1)
            for b in range(NB_SEQ + 1):
                n = NBLK if b < NB_SEQ else PBLK
                for g in range(2):
                    last = pe.matmul(pb[1 + b // 4][0:n, P * (b % 4) + HD * g:P * (b % 4) + HD * g + HD],
                                     m.hx[:, 1, g, NBLK * b:NBLK * b + n], m.w2[:, 1, :], start=True, stop=True)
                if b in (3, 7, 8):
                    last.then_inc(kc_mm, 1)


def prompt(nc, m, sems, sem):
    pb = m.pb
    ident = const(m, "ident")
    q_staged, pre_ready = sem("q_staged"), sem("pre_ready")
    scored, summed, exped, smax, scl_ready, p_ready = (
        sem("scored"), sem("summed"), sem("exped"), sem("smax"), sem("scl_ready"), sem("p_ready"))
    rec, p_turned, pt_ready, o_done, o_kept = (
        sem("rec"), sem("p_turned"), sem("pt_ready"), sem("o_done"), sem("o_kept"))
    c_scored, c_step, c_exp, c_turned, ct_ready = (
        sem("c_scored"), sem("c_step"), sem("c_exp"), sem("c_turned"), sem("ct_ready"))
    U = 2 * PTILES
    units = [(g, i) for i in (3, 2, 1, 0) for g in range(2)]
    LAG_T, LAG_V = 2, 3
    nm = lambda u: m.small[:, 2 * (u % 3):2 * (u % 3) + 2]
    su = lambda u: m.small[:, 8 + 2 * (u % 3):8 + 2 * (u % 3) + 2]
    cst = m.small[:, 32:32 + 8]
    csum = m.small[:, 40:48]
    C_STEPS = 8

    with nc.Block() as block:
        @block.sync
        def _(sp):
            for b in range(2, 4):
                load_window(sp, m, b, b, sems)

        @block.gpsimd
        def _(pool):
            for b in range(2, 4):
                load_slot(pool, m, b, b, sems)

        @block.scalar
        def _(act):
            with act.Fori(0, HPG) as j:
                def c_exponent():
                    act.wait_ge(c_step, j * C_STEPS + 3)
                    act.activation(m.cc[:, :, :, :], m.cc[:, :, :, :], ACT.Exp).then_inc(c_exp, 1)

                def exponent(u):
                    g, i = units[u]
                    w = P * (i + 1)
                    act.wait_ge(smax, j * U + (u + 1))
                    for br in range(2):
                        last = act.activation(m.cp[u % 3][:, br, 0:w], m.cp[u % 3][:, br, 0:w], ACT.Exp,
                                              bias=nm(u)[:, br:br + 1], accum_out=su(u)[:, br:br + 1])
                    last.then_inc(exped, 1)

                def scale(u):
                    g, i = units[u]
                    w = P * (i + 1)
                    act.wait_ge(scl_ready, j * U + (u + 1))
                    for br in range(2):
                        last = act.activation(m.cp[u % 3][:, br, 0:w], m.cp[u % 3][:, br, 0:w], ACT.Copy,
                                              scale=su(u)[:, br:br + 1])
                    last.then_inc(p_ready, 1)

                c_exponent()
                for u in range(U + 1):
                    if u < U:
                        exponent(u)
                    if u >= 1:
                        scale(u - 1)
                for g in range(2):
                    act.wait_ge(o_done, j * U + (U - 1 + g))
                    act.activation(m.mixT[HD * g:HD * g + HD, bass.ds(j, 1), 0:SEQ]
                                   .rearrange("p a t -> p (a t)"), pb[6][HD * g:HD * g + HD, :], ACT.Copy)\
                       .then_inc(o_kept, 1)

        @block.vector
        def _(dve):
            with dve.Fori(0, HPG) as j:
                dve.wait_ge(o_kept, j * 2 + 2)
                dve.tensor_copy(m.qst[0], m.qT[:, bass.ds(j, 1), 0:SEQ].rearrange("p a t -> p (a t)"))\
                   .then_inc(q_staged, 1)
                for g in range(2):
                    last = dve.tensor_scalar(m.pre[0][:, g, :], const(m, "negd"),
                                             const(m, "slopes")[:, bass.ds(j + HPG * g, 1)], None, ALU.mult)
                last.then_inc(pre_ready, 1)

                def c_scores():
                    cc = m.cc[:, :, :, :].rearrange("p g i n -> p (g i) n")
                    dve.wait_ge(c_scored, j + 1)
                    for g in range(2):
                        last = dve.scalar_tensor_tensor(
                            out=m.cc[:, g, :, :].rearrange("p i n -> p (i n)"), in0=const(m, "cmpd"),
                            scalar=const(m, "slopes")[:, bass.ds(j + HPG * g, 1)],
                            in1=pb[7 - g][:, 0:32], op0=ALU.mult, op1=ALU.add)
                    last.then_inc(c_step, 1)
                    dve.wait_ge(c_step, j * C_STEPS + 1)
                    dve.tensor_reduce(cst, cc, AX.X, ALU.max).then_inc(c_step, 1)
                    dve.wait_ge(c_step, j * C_STEPS + 2)
                    dve.tensor_tensor(cc, cc, cst.unsqueeze(2).broadcast_to([P, 8, PBLK]), ALU.subtract)\
                       .then_inc(c_step, 1)

                def c_probs():
                    cc = m.cc[:, :, :, :].rearrange("p g i n -> p (g i) n")
                    dve.wait_ge(c_exp, j + 1)
                    for g in range(2):
                        last = dve.tensor_tensor(m.cc[:, g, :, :].rearrange("p i n -> p (i n)"),
                                                 m.cc[:, g, :, :].rearrange("p i n -> p (i n)"),
                                                 const(m, "cmpm"), ALU.mult)
                    last.then_inc(c_step, 1)
                    dve.wait_ge(c_step, j * C_STEPS + 4)
                    dve.tensor_reduce(csum, cc, AX.X, ALU.add).then_inc(c_step, 1)
                    dve.wait_ge(c_step, j * C_STEPS + 5)
                    dve.tensor_scalar(csum, csum, 1e-30, None, ALU.max).then_inc(c_step, 1)
                    dve.wait_ge(c_step, j * C_STEPS + 6)
                    dve.reciprocal(csum, csum).then_inc(c_step, 1)
                    dve.wait_ge(c_step, j * C_STEPS + 7)
                    for g in range(2):
                        last = dve.tensor_tensor(
                            csum[:, 4 * g:4 * g + 4], csum[:, 4 * g:4 * g + 4],
                            m.gates[:, 0:PTILES, bass.ds(j + HPG * g, 1)].rearrange("p i a -> p (i a)"), ALU.mult)
                    last.then_inc(c_step, 1)
                    dve.wait_ge(c_step, j * C_STEPS + 8)
                    dve.tensor_tensor(cc, cc, csum.unsqueeze(2).broadcast_to([P, 8, PBLK]), ALU.mult)\
                       .then_inc(ct_ready, 1)

                def sums(u):
                    g, i = units[u]
                    w = P * (i + 1)
                    if u == 0:
                        dve.wait_ge(pre_ready, j + 1)
                    dve.wait_ge(scored, j * U + (u + 1))
                    if u >= 3:
                        dve.wait_ge(p_turned, j * U + (u - 2))
                    hold(dve, m, u)
                    for br in range(2):
                        last = dve.tensor_tensor_reduce(m.cp[u % 3][:, br, 0:w], m.pre[0][:, g, SEQ - w:SEQ],
                                                        pb[2 * (u % 2) + br][:, 0:w], 1.0, -3e38, ALU.add, ALU.max,
                                                        nm(u)[:, br:br + 1])
                    last.then_inc(summed, 1)
                    dve.wait_ge(summed, j * U + (u + 1))
                    dve.tensor_scalar(nm(u), nm(u), -1.0, None, ALU.mult).then_inc(smax, 1)

                def factors(u):
                    g, i = units[u]
                    dve.wait_ge(exped, j * U + (u + 1))
                    dve.reciprocal(su(u), su(u)).then_inc(rec, 1)
                    dve.wait_ge(rec, j * U + (u + 1))
                    gt = m.gates[:, i, :].rearrange("p (r h) -> p r h", r=3)[:, 1:3, bass.ds(j + HPG * g, 1)]
                    dve.tensor_tensor(su(u), su(u), gt.rearrange("p r a -> p (r a)"), ALU.mult)\
                       .then_inc(scl_ready, 1)

                def keep_turned(u):
                    g, i = units[u]
                    w = P * (i + 1)
                    dve.wait_ge(p_turned, j * U + (u + 1))
                    for br in range(2):
                        last = dve.tensor_copy(m.cpT[u % 2][:, br, 0:w], pb[4 + br][:, 0:w])
                    last.then_inc(pt_ready, 1)

                c_scores()
                sums(0)
                c_probs()
                factors(0)
                for g in range(2):
                    dve.wait_ge(c_turned, j * 2 + (g + 1))
                    dve.tensor_copy(m.ccT[0:PBLK, g, :], pb[7][0:PBLK, :]).then_inc(ct_ready, 1)
                for u in range(1, U + LAG_T + 1):
                    if u < U:
                        sums(u)
                    if u >= LAG_T and u - LAG_T < U:
                        keep_turned(u - LAG_T)
                    if u < U:
                        factors(u)

        @block.tensor
        def _(pe):
            pe.sem_inc(o_kept, 2)
            with pe.Fori(0, HPG) as j:
                def c_scores():
                    for g in range(2):
                        for i in range(PTILES):
                            last = pe.matmul(pb[7 - g][:, PBLK * i:PBLK * i + PBLK], m.qst[0][HD * g:HD * g + HD, P * i:P * i + P],
                                             m.kcT[HD * g:HD * g + HD, NB_SEQ * NBLK:NB_SEQ * NBLK + PBLK],
                                             start=True, stop=True)
                    last.then_inc(c_scored, 1)

                def c_turn(g):
                    pe.wait_ge(ct_ready, j * 3 + (g + 1))
                    for i in range(PTILES):
                        last = pe.transpose(pb[7][0:PBLK, P * i:P * i + P], m.cc[:, g, i, :], ident)
                    last.then_inc(c_turned, 1)

                def scores(u):
                    g, i = units[u]
                    w = P * (i + 1)
                    if u >= 2:
                        pe.wait_ge(summed, j * U + (u - 1))
                    for br in range(2):
                        last = pe.matmul(pb[2 * (u % 2) + br][:, 0:w], m.qst[0][HD * g:HD * g + HD, P * i:P * i + P],
                                         m.kT[HD * g:HD * g + HD, br, 0:w], start=True, stop=True)
                    last.then_inc(scored, 1)

                def turn(u):
                    g, i = units[u]
                    pe.wait_ge(p_ready, j * U + (u + 1))
                    if u >= 1:
                        pe.wait_ge(pt_ready, j * U + u)
                    for br in range(2):
                        for k in range(i + 1):
                            last = pe.transpose(pb[4 + br][:, P * k:P * k + P],
                                                m.cp[u % 3][:, br, P * k:P * k + P], ident)
                    last.then_inc(p_turned, 1)

                def values(u):
                    g, i = units[u]
                    pe.wait_ge(pt_ready, j * U + (u + 1))
                    if u == 0:
                        pe.wait_ge(ct_ready, j * 3 + 3)
                        pe.wait_ge(o_kept, j * 2 + 2)
                    o = pb[6][HD * g:HD * g + HD, P * i:P * i + P]
                    for br in range(2):
                        for k in range(i + 1):
                            pe.matmul(o, values_at(m, k, br)[:, HD * g:HD * g + HD], m.cpT[u % 2][:, br, P * k:P * k + P],
                                      start=(br == 0 and k == 0), stop=False)
                    pe.matmul(o, m.vc[0:PBLK, NB_SEQ, HD * g:HD * g + HD], m.ccT[0:PBLK, g, P * i:P * i + P],
                              start=False, stop=True).then_inc(o_done, 1)

                pe.wait_ge(q_staged, j + 1)
                c_scores()
                scores(0)
                scores(1)
                c_turn(0)
                c_turn(1)
                for u in range(2, U + LAG_V):
                    if u < U:
                        scores(u)
                    if u >= LAG_T and u - LAG_T < U:
                        turn(u - LAG_T)
                    if u >= LAG_V:
                        values(u - LAG_V)


def sample(nc, m, sems, sem):
    pb = m.pb
    ident = const(m, "ident")
    NP_ = NB_SEQ // 2
    big_in, g_mm, g_step, qs_clear, staged = (
        sem("big_in"), sem("g_mm"), sem("g_step"), sem("qs_clear"), sem("staged"))
    n_scored, scored = sem("sn_scored"), sem("s_scored")
    k_packed, k_turned, k_kept = sem("k_packed"), sem("k_turned"), sem("k_kept")
    c_step, c_exp, p_cmp, imp_mm, sel_step, selb_ready, pre_ready = (
        sem("sc_step"), sem("sc_exp"), sem("p_cmp"), sem("imp_mm"), sem("sel_step"), sem("selb_ready"),
        sem("s_pre_ready"))
    summed, mx_ready, exped, f_step, f_ready, p_ready = (
        sem("s_summed"), sem("mx_ready"), sem("s_exped"), sem("f_step"), sem("f_ready"), sem("s_p_ready"))
    p_turned, pt_ready, o_done, bank0_free = sem("s_p_turned"), sem("s_pt_ready"), sem("s_o_done"), sem("bank0_free")
    sm = m.small
    cmax, cneg, csum = sm[:, 0:1], sm[:, 1:2], sm[:, 2:3]
    mx, nmx, ssum = sm[:, 8:16], sm[:, 16:18], sm[:, 20:22]
    NSL = PAST + NS
    WIN0 = NSL
    CMP0 = NSL + WINDOW + NS
    X = 5
    C_STEPS, SEL_STEPS, F_STEPS = 3, 5, 2

    with nc.Block() as block:
        @block.sync
        def _(sp):
            sp.dma_start(m.big, m.c_big).then_inc(big_in, 16)
            for n in range(2, NP_):
                sp.wait_ge(o_done, n - 1)
                for e in range(2):
                    load_window(sp, m, 2 * (n % 2) + e, 2 * n + e, sems)
            sp.wait_ge(o_done, NP_ - 1)
            for s in range(2):
                load_w_out(sp, m, sems, s)

        @block.gpsimd
        def _(pool):
            for e in range(2):
                pool.memset(m.qs[e], 0.0).then_inc(qs_clear, 1)
            pool.wait_ge(qs_clear, 2)
            pool.wait_ge(big_in, 16)
            for n in range(NP_):
                if n:
                    pool.wait_ge(o_done, n)
                if n >= 2:
                    for e in range(2):
                        pool.wait_ge(sems.slc_in[2 * (n % 2) + e], 128)
                b0 = 2 * n
                copies = []
                for e in range(2):
                    for g in range(2):
                        copies.append((m.qs[e][HD * g:HD * g + HD, 32 * g:32 * g + 32]
                                       .rearrange("p (h t) -> p h t", h=HPG),
                                       m.qT[HD * g:HD * g + HD, :, SEQ + DEC * (b0 + e):SEQ + DEC * (b0 + e + 1)]))
                    copies.append((m.vcs[e][0:NBLK, :], m.vc[:, b0 + e, :]))
                copies.append((m.kcs, m.kcT[:, NBLK * b0:NBLK * (b0 + 2)]))
                copies.append((m.snew, const(m, "s_new")[:, NS * n:NS * n + NS]))
                for k, (dst, src) in enumerate(copies):
                    pool.tensor_copy(dst, src).then_inc(staged, 1)
                    pool.wait_ge(staged, 8 * n + k + 1)
                if 1 <= n < NP_ - 1:
                    for e in range(2):
                        load_slot(pool, m, 2 * ((n + 1) % 2) + e, 2 * (n + 1) + e, sems)
                for u in range(2 * X):
                    e, x = u // X, u % X
                    if x == 0:
                        pool.wait_ge(sems.slc_in[2 * (n % 2) + e], 64 * (n // 2 + 1))
                    if x == X - 1:
                        pool.wait_ge(sems.win_in[2 * (n % 2) + e], 16 * (n // 2 + 1))
                    if 2 * X * n + u >= 2:
                        pool.wait_ge(k_turned, 2 * X * n + u - 1)
                    pool.tensor_copy(m.kst[u % 2].rearrange("p (a d) -> p a d", d=HD),
                                     m.slot[2 * (n % 2) + e][:, x].rearrange("p q (g k) -> p (q g) k", g=NKV)
                                     [:, :, 0:HD]).then_inc(k_packed, 1)
                pool.wait_ge(selb_ready, n + 1)
                for x in range(4):
                    pool.tensor_tensor(
                        m.sp[:, 512 * x:512 * x + 512].rearrange("p (m b q) -> p m b q", m=4, b=8),
                        bigconst(m, "s_slc")[:, 512 * x:512 * x + 512].rearrange("p (m b q) -> p m b q", m=4, b=8),
                        m.selb[:, 8 * x:8 * x + 8].unsqueeze(1).unsqueeze(3).broadcast_to([P, 4, 8, 16]),
                        ALU.add).then_inc(pre_ready, 1)

        @block.scalar
        def _(act):
            act.wait_ge(g_mm, 1)
            act.activation(m.imp_g, pb[0][:, 0:96], ACT.Copy).then_inc(bank0_free, 1)
            with act.Fori(0, NP_ // 2) as it:
                for q in range(2):
                    n = it * 2 + q

                    def keep_keys(u):
                        act.wait_ge(k_turned, n * (2 * X) + (u + 1))
                        act.activation(m.skT[u % 2], pb[6 + u % 2][:, :], ACT.Copy).then_inc(k_kept, 1)

                    for u in range(2 * X):
                        if u == 2:
                            act.wait_ge(c_step, n * C_STEPS + 2)
                            act.activation(m.cmpp, m.cmpp, ACT.Exp, bias=cneg, accum_out=csum).then_inc(c_exp, 1)
                        keep_keys(u)
                    act.wait_ge(mx_ready, n + 1)
                    act.activation(m.sp[:, 0:NSL], m.sp[:, 0:NSL], ACT.Exp, bias=nmx[:, 0:1], accum_out=ssum[:, 0:1])
                    act.activation(m.sp[:, WIN0:CMP0], m.sp[:, WIN0:CMP0], ACT.Exp, bias=nmx[:, 1:2],
                                   accum_out=ssum[:, 1:2]).then_inc(exped, 1)
                    act.wait_ge(f_ready, n + 1)
                    act.activation(m.sp[:, WIN0:CMP0], m.sp[:, WIN0:CMP0], ACT.Copy, scale=ssum[:, 1:2])\
                       .then_inc(p_ready, 1)
                    act.wait_ge(o_done, n + 1)
                    for g in range(2):
                        a = HD * g
                        last = act.activation(
                            m.mixT[a:a + HD, 0:HPG, bass.ds(n * (2 * DEC) + SEQ, 2 * DEC)]
                            .rearrange("p h (e t) -> p e h t", e=2),
                            pb[0][a:a + HD, 0:P].rearrange("p (e g h t) -> p e g h t", e=2, g=2, h=HPG)[:, :, g],
                            ACT.Copy)
                    last.then_inc(bank0_free, 1)

        @block.vector
        def _(dve):
            dve.wait_ge(bank0_free, 1)
            gt12 = m.imp_g.rearrange("p (a r h) -> p (a r) h", a=NP_, r=3)
            dve.tensor_tensor(gt12, gt12, const(m, "headrow").unsqueeze(1).broadcast_to([P, 12, NH]), ALU.mult)\
               .then_inc(g_step, 1)
            dve.wait_ge(g_step, 1)
            dve.tensor_reduce(m.grow[:, :], gt12, AX.X, ALU.add).then_inc(g_step, 1)
            dve.wait_ge(g_step, 2)
            dve.wait_ge(big_in, 16)
            with dve.Fori(0, NP_ // 2) as it:
                for q in range(2):
                    n = it * 2 + q
                    gate = lambda r: m.grow[:, bass.ds(n * 3 + r, 1)]
                    dve.wait_ge(n_scored, n + 1)
                    hold(dve, m, 0)
                    dve.tensor_tensor_reduce(m.cmpp, const(m, "s_cmp"), pb[5][:, 128:160], 1.0, -3e38, ALU.add,
                                             ALU.max, cmax).then_inc(c_step, 1)
                    dve.wait_ge(c_step, n * C_STEPS + 1)
                    dve.tensor_scalar(cneg, cmax, -1.0, None, ALU.mult).then_inc(c_step, 1)
                    dve.tensor_tensor_reduce(m.sp[:, PAST:NSL], m.snew, pb[5][:, 0:NS], 1.0, -3e38, ALU.add,
                                             ALU.max, mx[:, 4:5])
                    dve.tensor_tensor_reduce(m.sp[:, WIN0 + WINDOW:CMP0], m.snew, pb[5][:, NS:2 * NS], 1.0, -3e38,
                                             ALU.add, ALU.max, mx[:, 6:7])
                    dve.wait_ge(c_exp, n + 1)
                    dve.reciprocal(csum, csum).then_inc(c_step, 1)
                    dve.wait_ge(c_step, n * C_STEPS + 3)
                    dve.tensor_scalar(m.cmpp, m.cmpp, csum, None, ALU.mult).then_inc(p_cmp, 1)
                    dve.wait_ge(p_cmp, n + 1)
                    dve.wait_ge(imp_mm, n + 1)
                    dve.tensor_copy(m.imp, pb[5][:, 160:192]).then_inc(sel_step, 1)
                    dve.wait_ge(sel_step, n * SEL_STEPS + 1)
                    dve.memset(m.imp[:, 0:NBLK:NBLK - 1], FORCE).then_inc(sel_step, 1)
                    dve.wait_ge(sel_step, n * SEL_STEPS + 2)
                    ib = m.imp.unsqueeze(1).broadcast_to([P, NBLK, NBLK])
                    ia = m.imp.unsqueeze(2).broadcast_to([P, NBLK, NBLK])
                    dve.tensor_tensor(m.gt, ib, ia, ALU.is_gt)
                    dve.tensor_tensor(m.eq, ib, ia, ALU.is_equal).then_inc(sel_step, 1)
                    dve.wait_ge(sel_step, n * SEL_STEPS + 3)
                    dve.tensor_tensor(m.eq, m.eq, bigconst(m, "before").rearrange("p (a b) -> p a b", a=NBLK),
                                      ALU.mult).then_inc(sel_step, 1)
                    dve.wait_ge(sel_step, n * SEL_STEPS + 4)
                    dve.tensor_tensor(m.gt, m.gt, m.eq, ALU.add).then_inc(sel_step, 1)
                    dve.wait_ge(sel_step, n * SEL_STEPS + 5)
                    dve.tensor_reduce(m.selb, m.gt, AX.X, ALU.add).then_inc(sems.rank, 1)
                    dve.wait_ge(sems.rank, n + 1)
                    dve.tensor_scalar(m.selb, m.selb, N_SELECT - 1.5, NEG, ALU.is_ge, ALU.mult)\
                       .then_inc(selb_ready, 1)
                    dve.wait_ge(scored, n * (2 * X) + 2 * X)
                    hold(dve, m, 1)
                    dve.tensor_tensor_reduce(m.sp[:, WIN0:WIN0 + WINDOW], bigconst(m, "s_win"), pb[4][:, :], 1.0,
                                             -3e38, ALU.add, ALU.max, mx[:, 5:6])
                    for x in range(4):
                        dve.wait_ge(pre_ready, n * 4 + (x + 1))
                        hold(dve, m, 2 + x)
                        last = dve.tensor_tensor_reduce(m.sp[:, 512 * x:512 * x + 512], m.sp[:, 512 * x:512 * x + 512],
                                                        pb[x][:, :], 1.0, -3e38, ALU.add, ALU.max, mx[:, x:x + 1])
                    last.then_inc(summed, 1)
                    dve.wait_ge(summed, n + 1)
                    dve.tensor_reduce(nmx[:, 0:1], mx[:, 0:5], AX.X, ALU.max, negate=True)
                    dve.tensor_reduce(nmx[:, 1:2], mx[:, 5:7], AX.X, ALU.max, negate=True).then_inc(mx_ready, 1)
                    dve.tensor_scalar(m.sp[:, CMP0:CMP0 + NBLK], m.cmpp, gate(0), None, ALU.mult)
                    dve.wait_ge(exped, n + 1)
                    dve.reciprocal(ssum, ssum).then_inc(f_step, 1)
                    dve.wait_ge(f_step, n * F_STEPS + 1)
                    dve.tensor_tensor(ssum, ssum, m.grow[:, bass.ds(n * 3 + 1, 2)], ALU.mult).then_inc(f_step, 1)
                    dve.wait_ge(f_step, n * F_STEPS + 2)
                    dve.sem_inc(f_ready, 1)
                    dve.tensor_scalar(m.sp[:, 0:NSL], m.sp[:, 0:NSL], ssum[:, 0:1], None, ALU.mult)\
                       .then_inc(p_ready, 1)
                    for x in range(X + 1):
                        dve.wait_ge(p_turned, n * (X + 1) + (x + 1))
                        if x < X:
                            dve.tensor_copy(m.spT[x % 2], pb[6 + x % 2][:, :]).then_inc(pt_ready, 1)
                        else:
                            dve.tensor_copy(m.spX[0:NS, 0:256], pb[6 + x % 2][0:NS, 0:256])
                            dve.tensor_copy(m.spX[0:NBLK, 256:384], pb[6 + x % 2][0:NBLK, 256:384])\
                               .then_inc(pt_ready, 1)

        @block.tensor
        def _(pe):
            for n in range(NP_):
                last = pe.matmul(pb[0][:, 24 * n:24 * n + 24], const(m, "tokrow")[0:NS, P * n:P * n + P],
                                 m.gates[0:NS, PTILES, :], start=True, stop=True)
            last.then_inc(g_mm, 1)
            with pe.Fori(0, NP_ // 2) as it:
                for q in range(2):
                    n = it * 2 + q
                    slot = [m.slot[2 * q], m.slot[2 * q + 1]]
                    pe.wait_ge(staged, n * 8 + 8)
                    for e in range(2):
                        pe.matmul(pb[5][64 * e:64 * e + 64, 128:160], m.qs[e],
                                         m.kcs[:, NBLK * e:NBLK * e + NBLK], start=True, stop=True)
                    for e in range(2):
                        for br in range(2):
                            last = pe.matmul(pb[5][64 * e:64 * e + 64, NS * br:NS * br + NS], m.qs[e],
                                             m.kT[:, br, SEQ:TOK], start=True, stop=True)
                    last.then_inc(n_scored, 1)

                    def turn_keys(u):
                        e, x = u // X, u % X
                        pe.wait_ge(k_packed, n * (2 * X) + (u + 1))
                        if u >= 2:
                            pe.wait_ge(k_kept, n * (2 * X) + (u - 1))
                        for mm in range(QUAD):
                            last = pe.transpose(pb[6 + u % 2][:, P * mm:P * mm + P],
                                                m.kst[u % 2][:, P * mm:P * mm + P], ident)
                        last.then_inc(k_turned, 1)

                    def scores(u):
                        e, x = u // X, u % X
                        pe.wait_ge(k_kept, n * (2 * X) + (u + 1))
                        if u == 0:
                            pe.wait_ge(bank0_free, n + 1)
                        pe.matmul(pb[x][64 * e:64 * e + 64, :], m.qs[e], m.skT[u % 2], start=True, stop=True)\
                          .then_inc(scored, 1)

                    for u in range(2 * X + 1):
                        if u < 2 * X:
                            turn_keys(u)
                        if u >= 1:
                            scores(u - 1)
                        if u == 5:
                            pe.wait_ge(p_cmp, n + 1)
                            pe.matmul(pb[5][:, 160:192], const(m, "headsum"), m.cmpp, start=True, stop=True)\
                              .then_inc(imp_mm, 1)

                    def turn_probs(x):
                        if x == 0:
                            pe.wait_ge(p_ready, n * 2 + 2)
                        if x >= 2:
                            pe.wait_ge(pt_ready, n * (X + 1) + (x - 1))
                        if x < X:
                            a = 512 * x if x < 4 else WIN0
                            for mm in range(QUAD):
                                last = pe.transpose(pb[6 + x % 2][:, P * mm:P * mm + P],
                                                    m.sp[:, a + P * mm:a + P * mm + P], ident)
                        else:
                            pe.transpose(pb[6 + x % 2][0:NBLK, 2 * P:3 * P], m.sp[:, CMP0:CMP0 + NBLK], ident)
                            pe.transpose(pb[6 + x % 2][0:NS, 0:P], m.sp[:, PAST:NSL], ident)
                            last = pe.transpose(pb[6 + x % 2][0:NS, P:2 * P], m.sp[:, WIN0 + WINDOW:CMP0], ident)
                        last.then_inc(p_turned, 1)

                    def values(x):
                        pe.wait_ge(pt_ready, n * (X + 1) + (x + 1))
                        if x < X:
                            for mm in range(QUAD):
                                for e in range(2):
                                    for g in range(NKV):
                                        a = 64 * e + 32 * g
                                        pe.matmul(pb[0][HD * g:HD * g + HD, a:a + 32],
                                                  slot[e][:, x, mm, P * g + HD:P * g + P],
                                                  m.spT[x % 2][:, P * mm + a:P * mm + a + 32],
                                                  start=(x == 0 and mm == 0 and e == 0), stop=False,
                                                  skip_group_check=True)
                        else:
                            for e in range(2):
                                for g in range(NKV):
                                    a, d = 64 * e + 32 * g, HD * g
                                    o = pb[0][d:d + HD, a:a + 32]
                                    pe.matmul(o, m.vcs[e][0:NBLK, d:d + HD],
                                              m.spX[0:NBLK, 2 * P + a:2 * P + a + 32],
                                              start=False, stop=False, skip_group_check=True)
                                    for br in range(2):
                                        last = pe.matmul(o, values_at(m, PTILES, br, NS)[:, d:d + HD],
                                                         m.spX[0:NS, P * br + a:P * br + a + 32],
                                                         start=False, stop=(e == 1 and br == 1),
                                                         skip_group_check=True)
                            last.then_inc(o_done, 1)

                    for x in range(X + 2):
                        if x <= X:
                            turn_probs(x)
                        if x >= 1:
                            values(x - 1)


def load_w_out(eng, m, sems, s):
    dst = m.raw_w[s]
    src = m.w_out[0][:, 512 * s:512 * s + 512]
    for g in range(2):
        eng.dma_start(dst[HD * g:HD * g + HD, 0:HPG, :],
                      src[256 * g:256 * g + 256, :].rearrange("(j d) n -> d j n", d=HD)).then_inc(sems.ring_in[s], 16)
    eng.dma_start(dst[:, HPG:KT_D, :], src[512:D, :].rearrange("(k p) n -> p k n", p=P)).then_inc(sems.ring_in[s], 16)


def mlp(nc, m, sems, sem):
    pb = m.pb
    ident = const(m, "ident")
    gf_in = sem("gf_in")
    xh_ready, xl_ready, wh_ready, wl_ready = sem("xh_ready"), sem("xl_ready"), sem("wh_ready"), sem("wl_ready")
    unit_mm, kept = sem("unit_mm"), sem("kept")
    sq_ready, ssq_mm, var_ready, std_ready, rb_ready = (
        sem("sq_ready"), sem("ssq_mm"), sem("m_var"), sem("m_std"), sem("rb_ready"))
    a_ready, ah_ready, al_ready = sem("a_ready"), sem("ah_ready"), sem("al_ready")
    y_turned, y_sq, y_var, y_std, y_part, y_done = (
        sem("y_turned"), sem("y_sq"), sem("y_var"), sem("y_std"), sem("y_part"), sem("y_done"))
    y_out = [sem("y_out0"), sem("y_out1")]
    g_mlp = m.cols[:, 8:16]
    ysum = lambda i: m.small[:, 16 + 2 * i:18 + 2 * i]
    yv = lambda i: m.small[:, 32 + i:33 + i]
    W0 = 48
    NQ, UQ = 4, 16
    FIRST = KT_D
    UNITS = FIRST + NQ * UQ
    MIX_ORDER = [4, 5, 6, 7, 0, 1, 2, 3]
    out = lambda r, hf: pb[2 * (r % 2) + hf][:, 0:HALF]
    half = lambda v, hf: v[:, HALF * hf:HALF * hf + HALF]

    with nc.Block() as block:
        @block.sync
        def _(sp):
            sp.dma_start(m.gfin, m.g_final.rearrange("(o d) -> o d", o=1).broadcast_to([P, D])).then_inc(gf_in, 16)
            for q in range(NQ):
                for down in range(2):
                    for s in range(2):
                        t = 2 + 4 * q + 2 * down + s
                        sp.wait_ge(wl_ready, 4 * (t - 1))
                        if down:
                            src = m.w_down[0][1024 * q:1024 * q + 1024, 512 * s:512 * s + 512]
                        else:
                            src = m.w_up[0][:, 1024 * q + 512 * s:1024 * q + 512 * s + 512]
                        sp.dma_start(m.raw_w[s], src.rearrange("(k p) n -> p k n", p=P)).then_inc(sems.ring_in[s], 16)
            for i in range(TILES):
                sp.wait_ge(y_done, i + 1)
                if i < PTILES:
                    sp.dma_start(m.o_yp[0, P * i:P * i + P, :], m.yo[i % 2]).then_inc(y_out[i % 2], 16)
                else:
                    sp.dma_start(m.o_ys.rearrange("b t d -> (b t) d"), m.yo[i % 2][0:NS, :]).then_inc(y_out[i % 2], 16)
            sp.wait_ge(y_out[0], 48)
            sp.wait_ge(y_out[1], 32)

        def wcols(t, k):
            return t[:, k % 4, :].rearrange("p (k n) -> p k n", k=KT_D)

        def raw_cols(n):
            return m.raw_w[(n // 4) % 2][:, :, P * (n % 4):P * (n % 4) + P]

        @block.scalar
        def _(act):
            def split(i, base=0, loaded=W0):
                if i % 4 == 0:
                    act.wait_ge(sems.ring_in[(i // 4) % 2], loaded + 16 * (i // 8))
                act.activation(wcols(m.wh, i), raw_cols(i), ACT.Copy).then_inc(wh_ready, 1)

            for i in range(3):
                split(i)
            for k in MIX_ORDER:
                act.activation(m.xh[:, k, :], m.mixT[:, k, :], ACT.Copy).then_inc(xh_ready, 1)
            for n in range(FIRST):
                if n:
                    act.wait_ge(unit_mm, n)
                split(n + 3)
                act.wait_ge(kept, n + 1)
                if n >= 2:
                    act.wait_ge(ssq_mm, n - 1)
                act.activation(m.sq[n % 2], m.hT[:, n, :], ACT.Square).then_inc(sq_ready, 1)
            for k in range(KT_D):
                act.activation(m.xh[:, k, :], m.hT[:, k, :], ACT.Identity, scale=g_mlp[:, k:k + 1])\
                   .then_inc(xh_ready, 1)
            act.wait_ge(var_ready, 1)
            act.activation(m.rb, m.var, ACT.Sqrt).then_inc(std_ready, 1)

            def quarter(q, last):
                for i in range(UQ):
                    n = q * UQ + (FIRST + i)
                    if i < 8:
                        f = q * 8 + i
                        act.wait_ge(kept, n + 1)
                        act.activation(m.act[i % 2], m.relu[i % 2], ACT.Square).then_inc(a_ready, 1)
                        act.wait_ge(a_ready, f + 1)
                        act.activation(m.ah[:, i, :], m.act[i % 2], ACT.Copy).then_inc(ah_ready, 1)
                    if not (last and i + 3 >= UQ):
                        act.wait_ge(unit_mm, n)
                        split(i + 3, q * UQ + FIRST, q * 32 + (W0 + 16))

            with act.Fori(0, NQ - 1) as q:
                quarter(q, False)
            quarter(NQ - 1, True)
            for i in range(TILES):
                n = rows(i)
                act.wait_ge(y_turned, i + 1)
                if i:
                    act.wait_ge(y_sq, i)
                for hf in range(2):
                    last = act.activation(m.sq[0][0:n, 0:512] if hf == 0 else m.sq[1][0:n, 0:512],
                                          pb[2 * (i % 4) + hf][0:n, :], ACT.Square,
                                          accum_out=ysum(i)[0:n, hf:hf + 1])
                last.then_inc(y_sq, 1)
                act.wait_ge(y_var, i + 1)
                act.activation(yv(i)[0:n, :], yv(i)[0:n, :], ACT.Sqrt).then_inc(y_std, 1)

        @block.vector
        def _(dve):
            def split(i, base=0):
                dve.wait_ge(wh_ready, base + (i + 1))
                dve.tensor_tensor(wcols(m.wl, i), raw_cols(i), wcols(m.wh, i).bitcast(F32), ALU.subtract)\
                   .then_inc(wl_ready, 1)

            split(0)
            for c, k in enumerate(MIX_ORDER):
                dve.wait_ge(xh_ready, c + 1)
                dve.tensor_tensor(m.xl[:, k, :], m.mixT[:, k, :], m.xh[:, k, :].bitcast(F32), ALU.subtract)\
                   .then_inc(xl_ready, 1)
            split(1)
            for n in range(FIRST):
                split(n + 2)
                dve.wait_ge(unit_mm, n + 1)
                for hf in range(2):
                    last = dve.tensor_tensor(half(m.hT[:, n, :], hf), out(n, hf), half(m.hT[:, n, :], hf), ALU.add)
                last.then_inc(kept, 1)
            for n in range(FIRST):
                dve.wait_ge(xh_ready, KT_D + n + 1)
                dve.scalar_tensor_tensor(out=m.xl[:, n, :], in0=m.hT[:, n, :], scalar=g_mlp[:, n:n + 1],
                                         in1=m.xh[:, n, :].bitcast(F32), op0=ALU.mult, op1=ALU.subtract)\
                   .then_inc(xl_ready, 1)
            dve.wait_ge(ssq_mm, KT_D)
            for hf in range(2):
                last = dve.tensor_scalar(half(m.var, hf), pb[6 + hf][:, 0:HALF], 1.0 / D, EPS, ALU.mult, ALU.add)
            last.then_inc(var_ready, 1)
            dve.wait_ge(std_ready, 1)
            dve.reciprocal(m.rb, m.rb).then_inc(rb_ready, 1)
            dve.wait_ge(rb_ready, 1)

            def quarter(q, last):
                for i in range(UQ):
                    n = q * UQ + (FIRST + i)
                    dve.wait_ge(unit_mm, n + 1)
                    for hf in range(2):
                        if i < 8:
                            op = dve.scalar_tensor_tensor(out=half(m.relu[i % 2], hf), in0=out(i, hf), scalar=0.0,
                                                          in1=half(m.rb, hf), op0=ALU.max, op1=ALU.mult)
                        else:
                            h = half(m.hT[:, i - 8, :], hf)
                            op = dve.tensor_tensor(h, out(i, hf), h, ALU.add)
                    op.then_inc(kept, 1)
                    if not (last and i + 2 >= UQ):
                        split(i + 2, q * UQ + FIRST)
                    if i < 8:
                        dve.wait_ge(ah_ready, q * 8 + (i + 1))
                        dve.tensor_tensor(m.al[:, i, :], m.act[i % 2], m.ah[:, i, :].bitcast(F32), ALU.subtract)\
                           .then_inc(al_ready, 1)

            with dve.Fori(0, NQ - 1) as q:
                quarter(q, False)
            quarter(NQ - 1, True)
            dve.wait_ge(gf_in, 16)
            for i in range(TILES):
                n = rows(i)
                dve.wait_ge(y_sq, i + 1)
                dve.tensor_tensor(yv(i)[0:n, :], ysum(i)[0:n, 0:1], ysum(i)[0:n, 1:2], ALU.add).then_inc(y_part, 1)
                dve.wait_ge(y_part, 2 * i + 1)
                dve.tensor_scalar(yv(i)[0:n, :], yv(i)[0:n, :], 1.0 / D, EPS, ALU.mult, ALU.add).then_inc(y_var, 1)
                dve.wait_ge(y_std, i + 1)
                dve.reciprocal(yv(i)[0:n, :], yv(i)[0:n, :]).then_inc(y_part, 1)
                dve.wait_ge(y_part, 2 * i + 2)
                if i >= 2:
                    dve.wait_ge(y_out[i % 2], 16 * (i // 2))
                for hf in range(2):
                    last = dve.scalar_tensor_tensor(out=m.yo[i % 2][0:n, 512 * hf:512 * hf + 512],
                                                    in0=pb[2 * (i % 4) + hf][0:n, :], scalar=yv(i)[0:n, :],
                                                    in1=m.gfin[0:n, 512 * hf:512 * hf + 512], op0=ALU.mult,
                                                    op1=ALU.mult)
                last.then_inc(y_done, 1)

        @block.tensor
        def _(pe):
            def product(i, k, xh, xl, first, end):
                w = (wcols(m.wh, i)[:, k, :], wcols(m.wl, i)[:, k, :])
                for part, (wi, x) in enumerate(((0, xh), (0, xl), (1, xh))):
                    for hf in range(2):
                        last = pe.matmul(out(i, hf), w[wi], half(x[:, k, :], hf), start=first and part == 0,
                                         stop=end and part == 2)
                return last

            def sum_squares(dt):
                pe.wait_ge(sq_ready, dt + 1)
                for hf in range(2):
                    last = pe.matmul(pb[6 + hf][:, 0:HALF], m.ones[:, :], half(m.sq[dt % 2], hf),
                                     start=(dt == 0), stop=(dt == KT_D - 1))
                last.then_inc(ssq_mm, 1)

            for n in range(FIRST):
                pe.wait_ge(wl_ready, n + 1)
                if n >= 2:
                    pe.wait_ge(kept, n - 1)
                for c, k in enumerate(MIX_ORDER):
                    if n == 0:
                        pe.wait_ge(xl_ready, c + 1)
                    last = product(n, k, m.xh, m.xl, c == 0, c == KT_D - 1)
                last.then_inc(unit_mm, 1)
                if n >= 1:
                    sum_squares(n - 1)
            sum_squares(KT_D - 1)
            with pe.Fori(0, NQ) as q:
                for down in range(2):
                    with pe.Fori(0, 2) as s:
                        for r in range(4):
                            n = q * UQ + s * 4 + (FIRST + 8 * down + r)
                            pe.wait_ge(wl_ready, n + 1)
                            pe.wait_ge(kept, n - 1)
                            for k in range(KT_D):
                                if r == 0 and not down:
                                    pe.wait_ge(xl_ready, KT_D + k + 1)
                                if r == 0 and down:
                                    pe.wait_ge(al_ready, q * 8 + (k + 1))
                                last = product(r, k, m.ah if down else m.xh, m.al if down else m.xl, k == 0,
                                               k == KT_D - 1)
                            last.then_inc(unit_mm, 1)
            pe.wait_ge(kept, UNITS)
            for i in range(TILES):
                n = rows(i)
                if i >= 4:
                    pe.wait_ge(y_done, i - 3)
                for k in range(KT_D):
                    last = pe.transpose(pb[2 * (i % 4) + k // 4][0:n, P * (k % 4):P * (k % 4) + P],
                                        m.hT[:, k, P * i:P * i + n], ident)
                last.then_inc(y_turned, 1)


INPUTS = ["x_prompt", "x_sample", "cache_cmp", "cache_slc", "state_win", "state_pool", "page_table", "g_attn", "w_in",
          "cmp_pe", "cmp_w1", "cmp_w2", "w_pool", "pool_scale", "w_out", "g_mlp", "w_up", "w_down", "g_final"]
OUTPUTS = [("o_yp", (1, SEQ, D)), ("o_ys", (NB_SEQ, DEC, D)),
           ("o_pcmp", (1, 1, SEQ, NKV, 2, HD)), ("o_pslc", (1, 1, SEQ, NKV, 2, HD)),
           ("o_pwin", (1, 1, SEQ, NKV, 2, HD)), ("o_ppool", (1, 1, HIST, 512)),
           ("o_scmp", (1, NB_SEQ, DEC, NKV, 2, HD)), ("o_sslc", (1, NB_SEQ, DEC, NKV, 2, HD)),
           ("o_swin", (1, NB_SEQ, WINDOW, NKV, 2, HD)), ("o_spool", (1, NB_SEQ, HIST, 512))]


def build(nc, m):
    with ExitStack() as ctx:
        place(nc, ctx, m)

        def sem(name):
            return ctx.enter_context(nc.semaphore(name))

        sems = Mem()
        sems.const_in, sems.wpool_in, sems.w2_in = sem("const_in"), sem("wpool_in"), sem("w2_in")
        sems.out = sem("states_out")
        sems.ones_set = sem("ones_set")
        sems.raw_in = [sem("raw_in0"), sem("raw_in1")]
        sems.slc_in = [sem(f"slc_in{s}") for s in range(4)]
        sems.win_in = [sem(f"win_in{s}") for s in range(4)]
        sems.ring_in = [sem("ring_in0"), sem("ring_in1")]
        sems.gelu_sq, sems.rank = sem("gelu_sq"), sem("rank")
        with ExitStack() as attention:
            place_attention(nc, attention, m)
            m.imp_g = m.spX[:, 0:96]
            project(nc, m, sems, sem)
            compress(nc, m, sems, sem)
            prompt(nc, m, sems, sem)
            sample(nc, m, sems, sem)
        with ExitStack() as last:
            place_mlp(nc, last, m)
            mlp(nc, m, sems, sem)


def kernel(**inputs):
    import concourse.bacc as _bacc
    from concourse.bass_utils import run_bass_kernel_spmd as _run

    nc = _bacc.Bacc("TRN2", target_bir_lowering=False, num_devices=1)
    arrays, m = {}, Mem()
    for name in INPUTS:
        a = np.ascontiguousarray(inputs[name])
        arrays[f"in_{name}"] = a
        ap = nc.dram_tensor(f"in_{name}", a.shape, mybir.dt.from_np(a.dtype), kind="ExternalInput").ap()
        m.__dict__["w_in_d" if name == "w_in" else name] = ap
    for name, group in zip(("c_small", "c_big"), tables()):
        a = np.ascontiguousarray(np.concatenate(list(group.values()), axis=1))
        arrays[name] = a
        m.__dict__[name] = nc.dram_tensor(name, a.shape, F32, kind="ExternalInput").ap()
    for name, shape in OUTPUTS:
        m.__dict__[name] = nc.dram_tensor(name, shape, F32, kind="ExternalOutput").ap()
    build(nc, m)
    r = _run(nc, [arrays], core_ids=[0])
    return tuple(r.results[0][name] for name, _ in OUTPUTS)
```

```python
from contextlib import ExitStack

import concourse.bass as bass
from concourse import mybir
import numpy as np

ALU = mybir.AluOpType
ACT = mybir.ActivationFunctionType
AX = mybir.AxisListType
F32 = mybir.dt.float32
F32R = mybir.dt.float32r
BF16 = mybir.dt.bfloat16
I32 = mybir.dt.int32
U32 = mybir.dt.uint32

P = 128
D = 1024
KT_D = D // P
SEQ = 512
NB_SEQ = 8
DEC = 8
NS = NB_SEQ * DEC
TOK = SEQ + NS
HALF = TOK // 2
PTILES = SEQ // P
TILES = PTILES + 1
PAST = 2048
PAGE = 128
PAGES = PAST // PAGE
HD = 64
NKV = 2
HPG = 4
NH = NKV * HPG
KV = NKV * 2 * HD
BLK = 64
NBLK = PAST // BLK
PBLK = SEQ // BLK
N_SELECT = 16
WINDOW = 512
HID = 128
FF = 4096
FT = FF // P
PG = 128
POOLW = (2, 4, 8, 16)
HIST = 15
UEXT = HIST + SEQ
USAM = HIST + DEC
UW = UEXT + NB_SEQ * USAM
POOL_CH = len(POOLW) * PG
SCALE = HD ** -0.5
EPS = 1e-6
NEG = -1e30
FORCE = 5.0
Q0, KV0, GL0, U0, PROJ = 0, 512, 1280, 1304, 1816
ROWW = GL0 + 24 - KV0
CHUNK_L = 8
CHUNKS = BLK // CHUNK_L
LP = CHUNK_L // 2
CHUNKF = CHUNK_L * KV
QUAD = 4
SLOTF = 5 * QUAD * KV
GELU_C, GELU_K = 0.7978845608028654, 0.044715


def rows(i):
    return P if i < PTILES else NS


def tables():
    t = {}
    p = np.arange(P)
    t["ident"] = np.eye(P)
    x = np.arange(SEQ)[None, :] - (SEQ - P)
    t["negd"] = np.where(x <= p[:, None], x - p[:, None], NEG)
    q = np.arange(SEQ).reshape(PTILES, P).T[:, :, None]
    dist = q - (64 * (np.arange(PBLK)[None, None, :] + 1) - 1)
    t["cmpd"] = np.where(dist >= 0, -dist, NEG).reshape(P, -1)
    t["cmpm"] = (dist >= 0).astype(float).reshape(P, -1)
    t["slopes"] = np.broadcast_to(2.0 ** -(np.arange(NH) + 1.0), (P, NH))
    t["corr"] = np.stack([np.broadcast_to(w / np.minimum(w, np.arange(16) + 1.0), (P, 16)) for w in POOLW],
                         1).reshape(P, -1)
    t["spread8"] = (p[:, None] == np.arange(64)[None] % 8).astype(float)
    t["hmask"] = (p[:, None] // 8 == np.arange(NH)[None]).astype(float)
    t["page4"] = (p[:, None] // 32 == np.arange(4)[None]).astype(float)
    t["page64"] = (p[:, None] // 2 == np.arange(64)[None]).astype(float)
    t["quad"] = (p % 32)[:, None].astype(float)
    t["chunk"] = ((p % 2) * CHUNKS)[:, None] + np.arange(CHUNKS)[None] * 1.0
    seq, g, h, tt = p // 64, (p // 32) % 2, (p // 8) % 4, p % 8
    head = g * HPG + h
    slope = 2.0 ** -(head + 1.0)
    end = 64 * (np.arange(NBLK) + 1) - 1
    t["s_cmp"] = -slope[:, None] * (PAST + tt[:, None] - end[None])
    same = (seq[:, None] == seq[None]) & (g[:, None] == g[None]) & (tt[:, None] == tt[None])
    t["headsum"] = same.astype(float)
    t["headrow"] = (head[:, None] == np.arange(NH)[None]).astype(float)
    tok = np.arange(NS)
    pair = np.arange(NB_SEQ // 2)
    d = tt[:, None, None] - (tok % 8)[None, None]
    ok = ((2 * pair[None, :, None] + seq[:, None, None]) == (tok // 8)[None, None]) & (d >= 0)
    t["s_new"] = np.where(ok, -slope[:, None, None] * d, NEG).reshape(P, -1)
    sel = np.zeros((P, len(pair), P))
    for a in pair:
        sel[(2 * a + seq) * 8 + tt, a, p] = 1.0
    t["tokrow"] = sel.reshape(P, -1)
    small = {k: np.ascontiguousarray(v, dtype=np.float32) for k, v in t.items()}
    big = {}
    pos = (np.arange(4)[:, None, None] * 512 + 4 * p[None, None, :] + np.arange(4)[None, :, None]).reshape(-1)
    big["s_slc"] = -slope[:, None] * (PAST + tt[:, None] - pos[None])
    r = (4 * p[None, :] + np.arange(4)[:, None]).reshape(-1)
    dw = WINDOW + tt[:, None] - r[None]
    big["s_win"] = np.where((dw >= 0) & (dw < WINDOW), -slope[:, None] * dw, NEG)
    i = np.arange(NBLK)
    big["before"] = np.broadcast_to((i[None, :] < i[:, None]).astype(float).reshape(1, -1), (P, NBLK * NBLK))
    big = {k: np.ascontiguousarray(v, dtype=np.float32) for k, v in big.items()}
    return small, big


def columns(t):
    at, out = 0, {}
    for k, v in t.items():
        out[k] = (at, v.shape[1])
        at += v.shape[1]
    return out, at


class Mem:
    pass


def view(v, *shape):
    if len(shape) == 1:
        return v
    names = "abcd"[:len(shape)]
    return v.rearrange(f"p ({' '.join(names)}) -> p {' '.join(names)}", **dict(zip(names, shape)))


LOW = KT_D * (ROWW + HPG * P)
PART1 = LOW + KT_D * POOL_CH
WORK = LOW + 2 * SLOTF
ZONE = WORK + 10528


def place(nc, ctx, m):
    def sb(name, shape, dt=F32):
        return ctx.enter_context(nc.sbuf_tensor(name, shape, dt))

    small, _ = tables()
    m.ccols, cw = columns(small)
    m.consts = sb("consts", [P, cw])
    m.hT = sb("hT", [P, KT_D, TOK])
    m.mixT = sb("mixT", [P, KT_D, TOK])
    m.small = sb("small", [P, 160])
    m.cols = sb("cols", [P, 20])
    m.zeros = sb("zeros", [1, 640], BF16)
    m.ones = sb("ones", [P, P])
    m.low = sb("low", [P, LOW])
    m.raw_w = [view(m.low[:, 4096 * s:4096 * s + 4096], KT_D, 512) for s in range(2)]
    m.gfin = m.low[:, 8192:8192 + D]
    m.sq = [m.low[:, 9216 + TOK * s:9216 + TOK * (s + 1)] for s in range(2)]
    m.pb = [ctx.enter_context(nc.psum_tensor(f"bank{i}", [P, 512], F32)) for i in range(8)]
    m.junk = m.mixT[:, 4:6, :].rearrange("p a b -> p (a b)")[:, 0:D]


def place_attention(nc, ctx, m):
    def sb(name, shape, dt=F32):
        return ctx.enter_context(nc.sbuf_tensor(name, shape, dt))

    _, big = tables()
    m.bcols, bw = columns(big)
    m.rowsT = sb("rowsT", [P, TILES, ROWW])
    m.qT = sb("qT", [P, HPG, TOK])
    m.kT = sb("kT", [P, 2, TOK])
    m.kcT = sb("kcT", [P, NB_SEQ * NBLK + PBLK])
    vcw = sb("vc_wpool", [P, (NB_SEQ + 1) * P])
    m.vc = vcw[0:NBLK, :].rearrange("p (b d) -> p b d", d=P)
    m.wpool = vcw[:, 0:4 * PG].rearrange("p (g d) -> p g d", d=PG)
    m.w2 = sb("w2", [P, 2, HD])
    m.peT = sb("peT", [P, BLK])
    m.gates = sb("gates", [P, TILES, 24])
    m.grow = sb("grow", [P, 12])
    m.tab = sb("tab", [P, NB_SEQ * PAGES], I32)
    m.idx_cmp = sb("idx_cmp", [P, 2, CHUNKS], U32)
    m.idx_slc = sb("idx_slc", [P, NB_SEQ * 4], U32)
    m.zone = sb("zone", [P, ZONE - LOW])

    def at(a, *shape):
        n = int(np.prod(shape))
        return view(m.low[:, a:a + n] if a < LOW else m.zone[:, a - LOW:a - LOW + n], *shape)

    m.w_rows = at(0, KT_D, ROWW)
    m.w_q = at(KT_D * ROWW, KT_D, 512)
    m.w_u = at(LOW, KT_D, 512)
    m.uT = at(PART1, 4, UW)
    m.pa = at(PART1 + 4 * UW, UW)
    m.pbuf = at(PART1 + 5 * UW, UW)
    m.spool = at(PART1 + 6 * UW, 512)
    m.utok = at(PART1 + 6 * UW, 3, 512)
    m.colrows = m.pbuf[0:20, 512:512 + P]
    m.x = at(WORK, TILES, D)
    m.xnT = at(WORK + TILES * D, KT_D, TOK)
    m.dT = m.mixT[:, 0:4, :]
    m.raw = [at(WORK + 5120 * s, 2, CHUNKF) for s in range(2)]
    m.w1 = [at(WORK + 5120 * s + 2 * CHUNKF, 2, LP, HID) for s in range(2)]
    m.blkT_p = at(PART1, 2, BLK // 2, 2 * PBLK)
    m.blkT = [[at(PART1 + 1024 + 1024 * s + 512 * c, 512) for c in range(2)] for s in range(2)]
    m.pe_in = at(PART1 + 3072, P)
    m.hx = at(PART1 + 3472, 2, 2, NB_SEQ * NBLK + PBLK)
    m.ht = at(LOW, 2, 2, NB_SEQ * NBLK + PBLK)
    m.slot = [at(SLOTF * s + (s // 2) * (LOW - 2 * SLOTF), 5, QUAD, KV) for s in range(4)]
    w = WORK
    m.cp = [at(w + 1024 * s, 2, 512) for s in range(4)]
    m.cpT = [at(w + 4096 + 1024 * s, 2, 512) for s in range(2)]
    m.pre = at(w + 6144, 2, 512)
    m.qst, m.ccT, m.cc = at(w + 7168, 512), at(w + 7680, 512), at(w + 8192, 256)
    m.vrep, m.vst, m.kc2 = at(w + 8448, P), at(w + 8576, P), at(w + 8704, 16)
    m.kst = [at(w + 512 * s, 512) for s in range(3)]
    m.spT = [at(w + 1536 + 512 * s, 512) for s in range(3)]
    m.spX = at(w + 3072, 384)
    m.big = at(w + 3456, bw)
    m.qs = at(w + 7040, NB_SEQ * HD)
    m.imp, m.selb = at(w + 7552, 32), at(w + 7584, 32)
    m.o_sb = at(w + 7616, P)
    m.sp = [at(w + 7744, 2720), m.rowsT[:, 0:4, :].rearrange("p a b -> p (a b)")[:, 0:2720]]
    m.skT = [m.kT[:, s, 0:SEQ] for s in range(2)] + m.spT[0:2]
    m.gt, m.eq = (m.qT[:, 2 * s:2 * s + 2, 0:SEQ].rearrange("p c (a b) -> p c a b", b=NBLK) for s in range(2))


def place_mlp(nc, ctx, m):
    def sb(name, shape, dt=F32):
        return ctx.enter_context(nc.sbuf_tensor(name, shape, dt))

    m.xh, m.xl = sb("xh", [P, KT_D, TOK], F32R), sb("xl", [P, KT_D, TOK], F32R)
    m.wh, m.wl = sb("wh", [P, 4, KT_D * P], F32R), sb("wl", [P, 4, KT_D * P], F32R)
    m.ah, m.al = sb("ah", [P, KT_D, TOK], F32R), sb("al", [P, KT_D, TOK], F32R)
    m.tmp = sb("tmp", [P, 4 * TOK])
    m.relu = [m.tmp[:, TOK * s:TOK * s + TOK] for s in range(2)]
    m.act = [m.tmp[:, TOK * (2 + s):TOK * (3 + s)] for s in range(2)]
    m.yo = [m.low[:, D * i:D * i + D] for i in range(TILES)]
    m.norm = sb("norm", [P, 2, TOK])
    m.var, m.rb = m.norm[:, 0, :], m.norm[:, 1, :]


def const(m, name):
    a, n = m.ccols[name]
    return m.consts[:, a:a + n]


def bigconst(m, name):
    a, n = m.bcols[name]
    return m.big[:, a:a + n]


def keys(m, i, br, n=P):
    return m.rowsT[0:n, i, KV * (br + 1):KV * (br + 1) + P]


def values_at(m, i, br, n=P):
    return m.rowsT[0:n, i, KV * (br + 1) + P:KV * (br + 2)]


def hold(eng, m, k):
    eng.memset(m.small[:, 150 + k:151 + k], 0.0)


def load_pages(eng, m, n, e, x, sems):
    cache = m.cache_slc.rearrange("l n (r q) g c d -> (l n r) (q g c d)", q=QUAD)
    at = (2 * n + e) * 4 + x
    eng.indirect_dma_start(m.slot[2 * (n % 2) + e][:, x, :, :].rearrange("p q c -> p (q c)"), None, cache,
                           bass.IndirectOffsetOnAxis(ap=m.idx_slc[:, at:at + 1], axis=0))\
       .then_inc(sems.slc_in[n % 2][x], 16)


def load_window(eng, m, s, b, sems):
    eng.dma_start(m.slot[s][:, 4, :, :].rearrange("p q c -> p (q c)"),
                  m.state_win[0, b].rearrange("(p q) g c d -> p (q g c d)", q=QUAD)).then_inc(sems.win_in[s // 2], 16)


def project(nc, m, sems, sem):
    pb = m.pb
    ident = const(m, "ident")
    x_in = [sem(f"x_in{i}") for i in range(TILES)]
    table_in, rowsw_in, uw_in, qw_in = sem("table_in"), sem("rowsw_in"), sem("uw_in"), sem("qw_in")
    states_out = sem("states_out")
    spool_in, cols_in, cols_turned, cols_kept = sem("spool_in"), sem("cols_in"), sem("cols_turned"), sem("cols_kept")
    ss_clear, ss_ready, var_ready, std_ready, rstd_ready = (
        sem("ss_clear"), sem("ss_ready"), sem("var_ready"), sem("std_ready"), sem("rstd_ready"))
    raw_turned, xt_kept, xn_ready, xn_turned, xnt_ready = (
        sem("raw_turned"), sem("xt_kept"), sem("xn_ready"), sem("xn_turned"), sem("xnt_ready"))
    rows_mm, rows_kept, tile_mm, tile_kept, q_kept = (
        sem("rows_mm"), sem("rows_kept"), sem("tile_mm"), sem("tile_kept"), sem("q_kept"))
    sp_turned, sp_kept, upad = sem("sp_turned"), sem("sp_kept"), sem("upad")
    ut_turned, ut_kept, pool_step, d_ready, pool_mm = (
        sem("ut_turned"), sem("ut_kept"), sem("pool_step"), sem("d_ready"), sem("pool_mm"))
    pool_kept, egate, gate1, idx_step = sem("pool_kept"), sem("egate"), sem("gate1"), sem("idx_step")
    ss, rstd = m.small[:, 0:TILES], m.small[:, 8:8 + TILES]
    var = m.small[:, 16:16 + TILES]
    ga, psc = m.cols[:, 0:8], m.cols[:, 16:20]
    pgc = m.small[:, 56:58]
    pgs = m.small[:, 64:96]

    with nc.Block() as block:
        @block.sync
        def _(sp):
            sp.dma_start(m.x[:, 0, :], m.x_prompt[0, 0:P, :]).then_inc(x_in[0], 16)
            sp.dma_start(m.consts[:, :], m.c_small).then_inc(sems.const_in, 16)
            for i in range(1, PTILES):
                sp.dma_start(m.x[:, i, :], m.x_prompt[0, P * i:P * i + P, :]).then_inc(x_in[i], 16)
            sp.dma_start(m.x[0:NS, PTILES, :], m.x_sample.rearrange("b t d -> (b t) d")).then_inc(x_in[PTILES], 16)
            for a, src in ((0, m.g_attn), (8, m.g_mlp), (16, m.pool_scale)):
                n = src.shape[1] // P
                sp.dma_start(m.colrows[a:a + n, :], src.rearrange("l (k p) -> (l k) p", p=P)).then_inc(cols_in, 16)
            wv = m.w_in_d[0].rearrange("(k p) n -> p k n", p=P)
            for k in range(0, KT_D, 4):
                sp.dma_start(m.w_rows[:, k:k + 4, :], wv[:, k:k + 4, KV0:U0]).then_inc(rowsw_in, 16)
            sp.dma_start(m.tab[:, :], m.page_table.rearrange("(o b) n -> o (b n)", o=1).broadcast_to([P, P]))\
              .then_inc(table_in, 16)
            sp.dma_start(m.w_u, wv[:, :, U0:PROJ]).then_inc(uw_in, 16)
            sp.dma_start(m.spool[0:NB_SEQ * HIST, :], m.state_pool[0].rearrange("b r c -> (b r) c"))\
              .then_inc(spool_in, 16)
            for g in range(NKV):
                for k in range(KT_D):
                    sp.dma_start(m.w_q[:, k, :].rearrange("p (j g d) -> p g j d", g=NKV, j=HPG)[:, g],
                                 wv[:, k, 256 * g:256 * g + 256].rearrange("p (j d) -> p j d", j=HPG))\
                      .then_inc(qw_in, 16)
            sp.dma_start(m.wpool[:, :, :], m.w_pool[0].rearrange("g c d -> c g d")).then_inc(sems.wpool_in, 16)
            sp.dma_start(m.w2[:, :, :], m.cmp_w2[0].rearrange("c h d -> h c d")).then_inc(sems.w2_in, 16)
            for b in range(NB_SEQ):
                sp.dma_start(m.o_swin[0, b, 0:WINDOW - DEC].rearrange("(a r) g c d -> a (r g c d)", a=28),
                             m.state_win[0, b, DEC:WINDOW].rearrange("(a r) g c d -> a (r g c d)", a=28))\
                  .then_inc(states_out, 16)
            sp.wait_ge(rows_kept, 2 * TILES)
            sp.dma_start(m.o_pcmp[0, 0].rearrange("(i p) g c d -> p i (g c d)", p=P), m.rowsT[:, 0:PTILES, 0:KV])\
              .then_inc(states_out, 16)
            sp.dma_start(m.o_scmp[0].rearrange("b t g c d -> (b t) (g c d)"), m.rowsT[0:NS, PTILES, 0:KV])\
              .then_inc(states_out, 16)
            cgd = lambda v: v.rearrange("p (c g d) -> p g c d", c=2, g=NKV)
            for i in range(PTILES):
                for br, po in ((1, m.o_pslc), (2, m.o_pwin)):
                    for g in range(NKV):
                        sp.dma_start(po[0, 0, P * i:P * i + P, g], cgd(m.rowsT[:, i, KV * br:KV * br + KV])[:, g])\
                          .then_inc(states_out, 16)
            for g in range(NKV):
                sp.dma_start(m.o_sslc[0].rearrange("b t g c d -> (b t) g c d")[:, g],
                             cgd(m.rowsT[0:NS, PTILES, KV:2 * KV])[:, g]).then_inc(states_out, 16)
                for b in range(NB_SEQ):
                    sp.dma_start(m.o_swin[0, b, WINDOW - DEC:WINDOW, g],
                                 cgd(m.rowsT[b * DEC:(b + 1) * DEC, PTILES, 2 * KV:3 * KV])[:, g])\
                      .then_inc(states_out, 16)
            sp.wait_ge(ut_kept, 3)
            for b in range(NB_SEQ):
                a = USAM * (b % 4) + DEC
                sp.dma_start(m.o_spool[0, b], m.utok[a:a + HIST, b // 4, :]).then_inc(states_out, 16)
            sp.dma_start(m.o_ppool[0, 0], m.utok[0:HIST, 2, :]).then_inc(states_out, 16)
            sp.wait_ge(states_out, 16 * (NB_SEQ + 2 + 4 * PTILES + 2 + 2 * NB_SEQ + NB_SEQ + 1))

        @block.gpsimd
        def _(pool):
            pool.memset(m.zeros[:, :], 0.0).then_inc(sems.cleared, 1)
            pool.memset(m.ones[:, :], 1.0).then_inc(sems.cleared, 1)
            pool.memset(m.uT[:, :, 0:HIST], 0.0).then_inc(upad, 1)
            pool.wait_ge(idx_step, 7)
            pool.wait_ge(xn_turned, 2 * TILES)
            load_chunk(pool, m, sems, 0)

        @block.scalar
        def _(act):
            act.wait_ge(ss_clear, 1)
            for i in range(TILES):
                n = rows(i)
                act.wait_ge(x_in[i], 16)
                if i:
                    act.wait_ge(ss_ready, i)
                act.activation(m.junk[0:n, :], m.x[0:n, i, :], ACT.Square, accum_out=ss[0:n, i:i + 1])\
                   .then_inc(ss_ready, 1)
                for kk in range(2):
                    u = 2 * i + kk
                    act.wait_ge(raw_turned, u + 1)
                    act.activation(m.hT[:, 4 * kk:4 * kk + 4, P * i:P * i + n],
                                   pb[u % 4][:, :].rearrange("p (k t) -> p k t", k=4)[:, :, 0:n], ACT.Copy)\
                       .then_inc(xt_kept, 1)
            act.wait_ge(var_ready, 1)
            act.activation(rstd, var, ACT.Sqrt).then_inc(std_ready, 1)
            for u in range(2 * TILES):
                i, n = u // 2, rows(u // 2)
                act.wait_ge(rows_mm, u + 1)
                if u % 2 == 0:
                    act.activation(m.rowsT[0:n, i, 0:KV], pb[u % 4][0:n, 0:KV], ACT.Copy)
                    act.activation(m.rowsT[0:n, i, KV:2 * KV].rearrange("p (c g d) -> p g c d", c=2, g=NKV),
                                   pb[u % 4][0:n, KV:2 * KV].rearrange("p (g c d) -> p g c d", c=2, g=NKV), ACT.Copy)\
                       .then_inc(rows_kept, 1)
                else:
                    act.activation(m.rowsT[0:n, i, 2 * KV:3 * KV].rearrange("p (c g d) -> p g c d", c=2, g=NKV),
                                   pb[u % 4][0:n, 0:KV].rearrange("p (g c d) -> p g c d", c=2, g=NKV), ACT.Copy)
                    act.activation(m.rowsT[0:n, i, 3 * KV:ROWW], pb[u % 4][0:n, KV:ROWW - 2 * KV], ACT.Copy)\
                       .then_inc(rows_kept, 1)
            act.wait_ge(rows_kept, 2 * TILES)
            act.activation(m.gates[:, 0:PTILES, :], m.rowsT[:, 0:PTILES, 3 * KV:ROWW], ACT.Exp, scale=-1.0)\
               .then_inc(egate, 1)
            act.activation(m.gates[0:NS, PTILES, :], m.rowsT[0:NS, PTILES, 3 * KV:ROWW], ACT.Exp, scale=-1.0)\
               .then_inc(egate, 1)
            for u in range(HPG):
                act.wait_ge(tile_mm, HPG + u + 1)
                for hf in range(2):
                    last = act.activation(m.qT[:, u, HALF * hf:HALF * hf + HALF],
                                          pb[4 + 2 * (u % 2) + hf][:, 0:HALF], ACT.Copy, scale=SCALE)
                last.then_inc(q_kept, 1)
            for e, n in ((0, 4 * USAM), (1, 4 * USAM), (2, HIST)):
                act.wait_ge(ut_turned, e + 1)
                act.activation(m.utok[0:n, e, :], pb[1 + e][0:n, :], ACT.Copy).then_inc(ut_kept, 1)
            act.wait_ge(cols_kept, 1)
            for gi in range(4):
                act.wait_ge(pool_mm, gi + 1)
                for hf in range(2):
                    last = act.activation(m.mixT[:, 4 + gi, HALF * hf:HALF * hf + HALF],
                                          pb[4 + 2 * (gi % 2) + hf][:, 0:HALF], ACT.Identity, scale=psc[:, gi:gi + 1])
                last.then_inc(pool_kept, 1)

        @block.vector
        def _(dve):
            dve.memset(ss, 1.0).then_inc(ss_clear, 1)
            dve.wait_ge(ss_ready, TILES)
            dve.tensor_scalar(var, ss, 1.0 / D, EPS, ALU.mult, ALU.add).then_inc(var_ready, 1)
            dve.wait_ge(std_ready, 1)
            dve.reciprocal(rstd, rstd).then_inc(rstd_ready, 1)
            dve.wait_ge(rstd_ready, 1)
            for i in range(TILES):
                n = rows(i)
                dve.wait_ge(raw_turned, 2 * i + 2)
                dve.tensor_scalar(m.x[0:n, i, :], m.x[0:n, i, :], rstd[0:n, i:i + 1], None, ALU.mult)\
                   .then_inc(xn_ready, 1)
            dve.wait_ge(cols_turned, 1)
            dve.tensor_copy(m.cols[:, :], pb[7][:, 0:20]).then_inc(cols_kept, 1)
            dve.wait_ge(cols_kept, 1)
            for u in range(2 * TILES):
                i, kk, n = u // 2, u % 2, rows(u // 2)
                dve.wait_ge(xn_turned, u + 1)
                dve.tensor_tensor(m.xnT[:, 4 * kk:4 * kk + 4, P * i:P * i + n],
                                  pb[4 + u % 4][:, :].rearrange("p (k t) -> p k t", k=4)[:, :, 0:n],
                                  ga[:, 4 * kk:4 * kk + 4].unsqueeze(2).broadcast_to([P, 4, n]), ALU.mult)\
                   .then_inc(xnt_ready, 1)
            dve.wait_ge(table_in, 16)
            dve.wait_ge(sems.const_in, 16)
            tf, t2 = m.pa[:, 0:P], m.pbuf[:, 0:P]
            dve.tensor_copy(tf, m.tab[:, :]).then_inc(idx_step, 1)
            dve.wait_ge(idx_step, 1)
            dve.tensor_tensor(t2.rearrange("p (a k) -> p a k", k=4), tf.rearrange("p (a k) -> p a k", k=4),
                              const(m, "page4").unsqueeze(1).broadcast_to([P, 32, 4]), ALU.mult).then_inc(idx_step, 1)
            dve.wait_ge(idx_step, 2)
            dve.tensor_reduce(pgs, t2.rearrange("p (a k) -> p a k", k=4), AX.X, ALU.add).then_inc(idx_step, 1)
            dve.wait_ge(idx_step, 3)
            dve.tensor_scalar(m.idx_slc[:, :], pgs, 32.0, const(m, "quad"), ALU.mult, ALU.add).then_inc(idx_step, 1)
            dve.tensor_tensor(t2.rearrange("p (a k) -> p a k", k=64), tf.rearrange("p (a k) -> p a k", k=64),
                              const(m, "page64").unsqueeze(1).broadcast_to([P, 2, 64]), ALU.mult).then_inc(idx_step, 1)
            dve.wait_ge(idx_step, 5)
            dve.tensor_reduce(pgc, t2.rearrange("p (a k) -> p a k", k=64), AX.X, ALU.add).then_inc(idx_step, 1)
            dve.wait_ge(idx_step, 6)
            dve.scalar_tensor_tensor(out=m.idx_cmp[:, :, :], in0=pgc.unsqueeze(2).broadcast_to([P, 2, CHUNKS]),
                                     scalar=2.0 * CHUNKS,
                                     in1=const(m, "chunk").unsqueeze(1).broadcast_to([P, 2, CHUNKS]),
                                     op0=ALU.mult, op1=ALU.add).then_inc(idx_step, 1)
            dve.wait_ge(sp_turned, 1)
            dve.tensor_copy(m.uT[:, :, UEXT:UW].rearrange("p g (b r) -> p g b r", b=NB_SEQ)[:, :, :, 0:HIST],
                            pb[0][:, 0:480].rearrange("p (g b r) -> p g b r", g=4, b=NB_SEQ)).then_inc(sp_kept, 1)
            for u in range(4):
                dve.wait_ge(tile_mm, u + 1)
                a, b = pb[4 + 2 * (u % 2)], pb[5 + 2 * (u % 2)]
                dve.tensor_copy(m.uT[:, u, HIST:HIST + HALF], a[:, 0:HALF])
                dve.tensor_copy(m.uT[:, u, HIST + HALF:UEXT], b[:, 0:SEQ - HALF])
                dve.tensor_copy(m.uT[:, u, UEXT:UW].rearrange("p (b r) -> p b r", b=NB_SEQ)[:, :, HIST:USAM],
                                b[:, SEQ - HALF:HALF].rearrange("p (b t) -> p b t", b=NB_SEQ)).then_inc(tile_kept, 1)
            dve.wait_ge(upad, 1)
            dve.wait_ge(sp_kept, 1)
            dve.wait_ge(tile_kept, 4)
            steps = 0
            for gi, w in enumerate(POOLW):
                src, dst, other = m.uT[:, gi, :], m.pa, m.pbuf
                s = 1
                while s < w:
                    if steps:
                        dve.wait_ge(pool_step, steps)
                    dve.tensor_tensor(dst[:, 2 * s - 1:UW], src[:, 2 * s - 1:UW], src[:, s - 1:UW - s], ALU.add)\
                       .then_inc(pool_step, 1)
                    steps += 1
                    src, dst, other = dst, other, dst
                    s *= 2
                dve.wait_ge(pool_step, steps)
                dve.tensor_tensor(src[:, HIST:HIST + 16], src[:, HIST:HIST + 16],
                                  const(m, "corr")[:, 16 * gi:16 * gi + 16], ALU.mult).then_inc(pool_step, 1)
                steps += 1
                dve.wait_ge(pool_step, steps)
                sam = lambda v: v[:, UEXT:UW].rearrange("p (b r) -> p b r", b=NB_SEQ)[:, :, HIST:USAM]
                dve.scalar_tensor_tensor(out=m.dT[:, gi, 0:SEQ], in0=src[:, HIST:UEXT], scalar=1.0 / w,
                                         in1=m.uT[:, gi, HIST:UEXT], op0=ALU.mult, op1=ALU.subtract)\
                   .then_inc(pool_step, 1)
                dve.scalar_tensor_tensor(out=m.dT[:, gi, SEQ:TOK].rearrange("p (b t) -> p b t", b=NB_SEQ),
                                         in0=sam(src), scalar=1.0 / w, in1=sam(m.uT[:, gi, :]),
                                         op0=ALU.mult, op1=ALU.subtract).then_inc(pool_step, 1)
                steps += 2
                dve.wait_ge(pool_step, steps)
                dve.sem_inc(d_ready, 1)
            dve.wait_ge(egate, 2)
            dve.tensor_scalar(m.gates[:, 0:PTILES, :], m.gates[:, 0:PTILES, :], 1.0, None, ALU.add).then_inc(gate1, 1)
            dve.tensor_scalar(m.gates[0:NS, PTILES, :], m.gates[0:NS, PTILES, :], 1.0, None, ALU.add)\
               .then_inc(gate1, 1)
            dve.wait_ge(gate1, 2)
            dve.reciprocal(m.gates[:, 0:PTILES, :], m.gates[:, 0:PTILES, :])
            dve.reciprocal(m.gates[0:NS, PTILES, :], m.gates[0:NS, PTILES, :]).then_inc(gate1, 1)

        @block.tensor
        def _(pe):
            pe.wait_ge(sems.const_in, 16)
            for u in range(2 * TILES):
                i, kk, n = u // 2, u % 2, rows(u // 2)
                if kk == 0:
                    pe.wait_ge(x_in[i], 16)
                if u >= 4:
                    pe.wait_ge(xt_kept, u - 3)
                for k in range(4):
                    last = pe.transpose(pb[u % 4][:, P * k:P * k + n],
                                        m.x[0:n, i, P * (4 * kk + k):P * (4 * kk + k) + P], ident[0:n, 0:n])
                last.then_inc(raw_turned, 1)

            pe.wait_ge(cols_in, 48)
            pe.transpose(pb[7][:, 0:20], m.colrows, ident[0:20, 0:20]).then_inc(cols_turned, 1)

            def turn_normed(u):
                i, kk, n = u // 2, u % 2, rows(u // 2)
                pe.wait_ge(xn_ready, i + 1)
                if u == 3:
                    pe.wait_ge(cols_kept, 1)
                if u >= 4:
                    pe.wait_ge(xnt_ready, u - 3)
                for k in range(4):
                    last = pe.transpose(pb[4 + u % 4][:, P * k:P * k + n],
                                        m.x[0:n, i, P * (4 * kk + k):P * (4 * kk + k) + P], ident[0:n, 0:n])
                last.then_inc(xn_turned, 1)

            def project_rows(u):
                i, n = u // 2, rows(u // 2)
                if u == 0:
                    pe.wait_ge(rowsw_in, 32)
                if u % 2 == 0:
                    pe.wait_ge(xnt_ready, 2 * i + 2)
                if u < 4:
                    pe.wait_ge(xt_kept, 7 + u)
                else:
                    pe.wait_ge(rows_kept, u - 3)
                a, b = (0, 512) if u % 2 == 0 else (512, ROWW)
                for k in range(KT_D):
                    last = pe.matmul(pb[u % 4][0:n, 0:b - a], m.xnT[:, k, P * i:P * i + n], m.w_rows[:, k, a:b],
                                     start=(k == 0), stop=(k == KT_D - 1))
                last.then_inc(rows_mm, 1)

            for i in range(TILES):
                turn_normed(2 * i)
                turn_normed(2 * i + 1)
                if i:
                    project_rows(2 * i - 2)
                    project_rows(2 * i - 1)
            project_rows(2 * TILES - 2)
            project_rows(2 * TILES - 1)
            pe.wait_ge(spool_in, 16)
            pe.wait_ge(rows_kept, 9)
            for gi in range(4):
                last = pe.transpose(pb[0][:, 120 * gi:120 * gi + 120], m.spool[0:120, P * gi:P * gi + P],
                                    ident[0:120, 0:120])
            last.then_inc(sp_turned, 1)
            for u in range(8):
                if u == 0:
                    pe.wait_ge(xnt_ready, 2 * TILES)
                    pe.wait_ge(uw_in, 16)
                if u == 4:
                    pe.wait_ge(qw_in, 16 * NKV * KT_D)
                if 2 <= u < 6:
                    pe.wait_ge(tile_kept, u - 1)
                if u >= 6:
                    pe.wait_ge(q_kept, u - 5)
                for hf in range(2):
                    for k in range(KT_D):
                        w = m.w_u[:, k, PG * u:PG * u + PG] if u < 4 else m.w_q[:, k, P * (u - 4):P * (u - 3)]
                        last = pe.matmul(pb[4 + 2 * (u % 2) + hf][:, 0:HALF], w,
                                         m.xnT[:, k, HALF * hf:HALF * hf + HALF],
                                         start=(k == 0), stop=(k == KT_D - 1))
                last.then_inc(tile_mm, 1)
            pe.wait_ge(rows_kept, 2 * TILES)
            for e in range(2):
                for gi in range(4):
                    a = UEXT + 4 * USAM * e
                    last = pe.transpose(pb[1 + e][0:4 * USAM, P * gi:P * gi + P], m.uT[:, gi, a:a + 4 * USAM], ident)
                last.then_inc(ut_turned, 1)
            for gi in range(4):
                last = pe.transpose(pb[3][0:HIST, P * gi:P * gi + P], m.uT[:, gi, UEXT - HIST:UEXT], ident)
            last.then_inc(ut_turned, 1)
            pe.wait_ge(sems.wpool_in, 16)
            for gi in range(4):
                pe.wait_ge(d_ready, gi + 1)
                if gi < 2:
                    pe.wait_ge(q_kept, 3 + gi)
                else:
                    pe.wait_ge(pool_kept, gi - 1)
                for hf in range(2):
                    last = pe.matmul(pb[4 + 2 * (gi % 2) + hf][:, 0:HALF], m.wpool[:, gi, :],
                                     m.dT[:, gi, HALF * hf:HALF * hf + HALF], start=True, stop=True)
                last.then_inc(pool_mm, 1)


def load_chunk(eng, m, sems, ck):
    cache = m.cache_cmp.rearrange("l n (h k q) g c d -> (l n h k) (q g c d)", h=2, k=CHUNKS)
    for hf in range(2):
        eng.indirect_dma_start(m.raw[ck % 2][:, hf, :], None, cache,
                               bass.IndirectOffsetOnAxis(ap=m.idx_cmp[:, hf, ck:ck + 1], axis=0))\
           .then_inc(sems.raw_in[ck % 2], 16)


def compress(nc, m, sems, sem):
    pb = m.pb
    ident = const(m, "ident")
    pe_in, pe_turned, pe_kept = sem("pe_in"), sem("pe_turned"), sem("pe_kept")
    w1_in = [sem("w1_in0"), sem("w1_in1")]
    kt_turned, kt_kept, pblk_turned, pblk_kept = (
        sem("kt_turned"), sem("kt_kept"), sem("pblk_turned"), sem("pblk_kept"))
    blk_turned, blk_kept, hid_done = sem("blk_turned"), [sem("blk_kept_k"), sem("blk_kept_v")], sem("hid_done")
    hx_ready, gelu, gtanh, kc_mm, kc_kept = (
        sem("hx_ready"), sem("gelu"), sem("gtanh"), sem("kc_mm"), sem("kc_kept"))
    NBT = NB_SEQ * NBLK

    with nc.Block() as block:
        @block.sync
        def _(sp):
            sp.dma_start(m.pe_in[0:BLK, :], m.cmp_pe[0].rearrange("l c d -> l (c d)")).then_inc(pe_in, 16)
            for ck in range(CHUNKS):
                s = ck % 2
                if ck >= 2:
                    sp.wait_ge(hid_done, 2 * LP * (ck - 1))
                for c in range(2):
                    sp.dma_start(m.w1[s][:, c, :, :],
                                 m.cmp_w1[0, c].rearrange("(k a q) d h -> k (q d) a h", k=CHUNKS, q=2)[ck])\
                      .then_inc(w1_in[s], 16)
            for b in range(2):
                load_window(sp, m, b, b, sems)

        @block.gpsimd
        def _(pool):
            for ck in range(1, CHUNKS):
                if ck >= 2:
                    pool.wait_ge(blk_turned, CHUNK_L * (ck - 1))
                load_chunk(pool, m, sems, ck)
                if ck >= CHUNKS - 4:
                    for e in range(2):
                        load_pages(pool, m, 0, e, ck - (CHUNKS - 4), sems)

        @block.scalar
        def _(act):
            for br in range(2):
                act.wait_ge(kt_turned, br + 1)
                act.activation(m.kT[:, br, 0:SEQ], pb[4 + br][:, :], ACT.Copy).then_inc(kt_kept, 1)
            act.wait_ge(pe_turned, 1)
            act.activation(m.peT[:, :], pb[7][:, 0:BLK], ACT.Copy).then_inc(pe_kept, 1)
            act.wait_ge(kt_turned, 3)
            act.activation(m.kT[:, :, SEQ:TOK], pb[6][:, 0:2 * NS].rearrange("p (b t) -> p b t", b=2), ACT.Copy)\
               .then_inc(kt_kept, 1)
            act.wait_ge(pe_kept, 1)
            with act.Fori(0, CHUNKS // 2) as it:
                for v in range(2 * CHUNK_L):
                    lo = HD * (v % 2)
                    act.wait_ge(blk_turned, it * (2 * CHUNK_L) + v + 1)
                    act.activation(m.blkT[(v // 2) % 2][0][lo:lo + HD, :], pb[4 + v % 4][0:HD, :], ACT.Identity,
                                   bias=m.peT[0:HD, bass.ds(it * (2 * CHUNK_L) + v, 1)]).then_inc(blk_kept[0], 1)
            act.wait_ge(hid_done, BLK)
            act.activation(m.hx[:, :, :, NBT:NBT + PBLK],
                           pb[2][:, 0:32].rearrange("p (c g n) -> p c g n", c=2, g=2), ACT.Copy)
            for c in range(2):
                act.activation(m.hx[:, c, :, 0:NBT].rearrange("p g (h n) -> p h g n", h=2),
                               pb[c][:, :].rearrange("p (h g n) -> p h g n", h=2, g=2), ACT.Copy)\
                   .then_inc(hx_ready, 1)
            for c in range(2):
                act.wait_ge(gelu, 2 * c + 2)
                act.activation(m.ht[:, c], m.ht[:, c], ACT.Tanh, scale=GELU_C * GELU_K).then_inc(gtanh, 1)
            act.wait_ge(kc_mm, 1)
            act.activation(m.kcT[:, :], pb[0][:, 0:NBT + PBLK], ACT.Copy, scale=0.5).then_inc(kc_kept, 1)

        @block.vector
        def _(dve):
            dve.wait_ge(pe_kept, 1)
            for g in range(2):
                dve.wait_ge(pblk_turned, g + 1)
                for c in range(2):
                    for par in range(2):
                        lo, hi = HD * c, HD * par
                        src = pb[g][lo:lo + HD, :].rearrange("p (b l q) -> p b l q", b=PBLK, q=2)[:, :, :, par]
                        dst = m.blkT_p[hi:hi + HD, c, :, PBLK * g:PBLK * g + PBLK].rearrange("p l b -> p b l")
                        pe_b = m.peT[lo:lo + HD, :].rearrange("p (l q) -> p l q", q=2)[:, :, par]
                        last = dve.tensor_tensor(dst, src, pe_b.unsqueeze(1).broadcast_to([HD, PBLK, BLK // 2]),
                                                 ALU.add)
                last.then_inc(pblk_kept, 1)
            with dve.Fori(0, CHUNKS // 2) as it:
                for v in range(2 * CHUNK_L):
                    lo = HD * (v % 2)
                    dve.wait_ge(blk_turned, it * (2 * CHUNK_L) + v + 1)
                    dve.tensor_scalar(m.blkT[(v // 2) % 2][1][lo:lo + HD, :], pb[4 + v % 4][HD:P, :],
                                      m.peT[HD:P, bass.ds(it * (2 * CHUNK_L) + v, 1)], None, ALU.add)\
                       .then_inc(blk_kept[1], 1)
            for c in range(2):
                dve.wait_ge(hx_ready, c + 1)
                dve.tensor_tensor(m.ht[:, c], m.hx[:, c], m.hx[:, c], ALU.mult).then_inc(gelu, 1)
                dve.wait_ge(gelu, 2 * c + 1)
                dve.scalar_tensor_tensor(out=m.ht[:, c], in0=m.ht[:, c], scalar=1 / GELU_K, in1=m.hx[:, c],
                                         op0=ALU.add, op1=ALU.mult).then_inc(gelu, 1)
            for c in range(2):
                dve.wait_ge(gtanh, c + 1)
                dve.scalar_tensor_tensor(out=m.hx[:, c], in0=m.ht[:, c], scalar=1.0, in1=m.hx[:, c], op0=ALU.add,
                                         op1=ALU.mult).then_inc(gelu, 1)
            for n in range(3):
                dve.wait_ge(kc_mm, n + 2)
                if n < 2:
                    dve.tensor_scalar(m.vc[:, 4 * n:4 * n + 4, :],
                                      pb[1 + n][0:NBLK, :].rearrange("p (b d) -> p b d", b=4), 0.5, None, ALU.mult)\
                       .then_inc(kc_kept, 1)
                else:
                    dve.tensor_scalar(m.vc[0:PBLK, NB_SEQ, :], pb[3][0:PBLK, 0:P], 0.5, None, ALU.mult)\
                       .then_inc(kc_kept, 1)

        @block.tensor
        def _(pe):
            for br in range(2):
                for i in range(PTILES):
                    last = pe.transpose(pb[4 + br][:, P * i:P * i + P], keys(m, i, br), ident)
                last.then_inc(kt_turned, 1)
            pe.wait_ge(pe_in, 16)
            pe.transpose(pb[7][:, 0:BLK], m.pe_in[0:BLK, :], ident[0:BLK, 0:BLK]).then_inc(pe_turned, 1)
            for br in range(2):
                last = pe.transpose(pb[6][:, NS * br:NS * br + NS], keys(m, PTILES, br, NS), ident[0:NS, 0:NS])
            last.then_inc(kt_turned, 1)
            for g in range(2):
                for i in range(PTILES):
                    last = pe.transpose(pb[g][:, P * i:P * i + P], m.rowsT[:, i, P * g:P * g + P], ident)
                last.then_inc(pblk_turned, 1)
            pe.wait_ge(pblk_kept, 2)
            pe.wait_ge(pe_kept, 1)
            pe.wait_ge(kt_kept, 3)
            for n in range(3):
                pe.matmul(pb[n][:, :], m.zeros[0:1, 0:P], m.zeros[0:1, P:P + 512], start=True, stop=True)

            with pe.Fori(0, CHUNKS // 2) as it:
                def turn(v):
                    s, l = v // CHUNK_L, v % CHUNK_L
                    if l == 0:
                        pe.wait_ge(sems.raw_in[s], it * 32 + 32)
                    for hg in range(4):
                        a = KV * l + P * (hg % 2)
                        last = pe.transpose(pb[4 + v % 4][:, P * hg:P * hg + P], m.raw[s][:, hg // 2, a:a + P], ident)
                    last.then_inc(blk_turned, 1)

                def hidden(p):
                    s, a = p // LP, p % LP
                    if a == 0:
                        pe.wait_ge(w1_in[s], it * 32 + 32)
                    for c in range(2):
                        pe.wait_ge(blk_kept[c], it * (2 * CHUNK_L) + (2 * p + 2))
                        w = m.w1[s][:, c, a, :]
                        pe.matmul(pb[2][:, 16 * c:16 * c + 16], w,
                                  m.blkT_p[:, c, bass.ds(it * (2 * LP) + p, 1), :].rearrange("p a b -> p (a b)"),
                                  start=False, stop=False, skip_group_check=True)
                        pe.matmul(pb[c][:, :], w, m.blkT[p % 2][c], start=False, stop=False, skip_group_check=True)\
                          .then_inc(hid_done, 1)

                for p in range(2 * LP):
                    turn(2 * p)
                    turn(2 * p + 1)
                    if p >= 1:
                        hidden(p - 1)
                hidden(2 * LP - 1)

            pe.wait_ge(gelu, 5)
            pe.wait_ge(sems.w2_in, 16)
            for g in range(2):
                last = pe.matmul(pb[0][HD * g:HD * g + HD, 0:NBT + PBLK], m.w2[:, 0, :], m.hx[:, 0, g, :],
                                 start=True, stop=True)
            last.then_inc(kc_mm, 1)
            pe.wait_ge(gelu, 6)
            for b in range(NB_SEQ + 1):
                n = NBLK if b < NB_SEQ else PBLK
                for g in range(2):
                    last = pe.matmul(pb[1 + b // 4][0:n, P * (b % 4) + HD * g:P * (b % 4) + HD * g + HD],
                                     m.hx[:, 1, g, NBLK * b:NBLK * b + n], m.w2[:, 1, :], start=True, stop=True)
                if b in (3, 7, 8):
                    last.then_inc(kc_mm, 1)


def prompt(nc, m, sems, sem):
    pb = m.pb
    ident = const(m, "ident")
    q_staged, pre_ready, vst_staged = sem("q_staged"), sem("pre_ready"), sem("vst_staged")
    scored, summed, smax, exped, rec, scl_ready = (
        sem("scored"), sem("summed"), sem("smax"), sem("exped"), sem("rec"), sem("scl_ready"))
    scaled, p_turned, kept_act, kept_dve = sem("scaled"), sem("p_turned"), sem("kept_act"), sem("kept_dve")
    o_done, o_kept = sem("o_done"), sem("o_kept")
    kc_ready, c_scored, c_step, c_exp, c_ready, c_turned, ct_ready = (
        sem("kc_ready"), sem("c_scored"), sem("c_step"), sem("c_exp"), sem("c_ready"),
        sem("c_turned"), sem("ct_ready"))
    U = 2 * PTILES
    AHEAD = 4
    tile = lambda v: PTILES - 1 - (v % U) // 2
    width = lambda v: P * (tile(v) + 1)
    branch = lambda v: v % 2
    nm = lambda v: m.small[:, 2 * (v % 4):2 * (v % 4) + 2]
    su = lambda v: m.small[:, 8 + 2 * (v % 4):8 + 2 * (v % 4) + 2]
    cst, csum = m.small[:, 32:64], m.small[:, 64:96]
    heads = [P, PTILES, NH, PBLK]
    cc4 = m.cc.rearrange("p (i h n) -> p i h n", i=PTILES, h=NH)
    KC0 = NB_SEQ * NBLK

    def per_head(v):
        return v.rearrange("p (i h) -> p i h", h=NH)

    with nc.Block() as block:
        @block.sync
        def _(sp):
            for b in range(2, 4):
                load_window(sp, m, b, b, sems)

        @block.gpsimd
        def _(pool):
            pool.memset(m.kc2, 0.0).then_inc(sems.cleared, 1)
            for x in range(4):
                for e in range(2):
                    load_pages(pool, m, 1, e, x, sems)

            def scale(j, v):
                pool.wait_ge(scl_ready, j * U + (v + 1))
                pool.tensor_tensor(m.cp[v % 4][:, :, 0:width(v)], m.cp[v % 4][:, :, 0:width(v)],
                                   su(v).unsqueeze(2).broadcast_to([P, 2, width(v)]), ALU.mult).then_inc(scaled, 1)

            def body(j, last):
                for u in range(U):
                    if not last or u + AHEAD - 1 < U:
                        scale(j, u + AHEAD - 1)

            for v in range(AHEAD - 1):
                scale(0, v)
            with pool.Fori(0, HPG - 1) as j:
                body(j, False)
            body(HPG - 1, True)

        @block.scalar
        def _(act):
            def exponent(j, v):
                act.wait_ge(smax, j * U + (v + 1))
                for g in range(2):
                    last = act.activation(m.cp[v % 4][:, g, 0:width(v)], m.cp[v % 4][:, g, 0:width(v)], ACT.Exp,
                                          bias=nm(v)[:, g:g + 1], accum_out=su(v)[:, g:g + 1])
                last.then_inc(exped, 1)

            def keep_turned(j, v):
                act.wait_ge(p_turned, j * U + (v + 1))
                act.activation(m.cpT[v % 2][:, 1, 0:width(v)], pb[5][:, 0:width(v)], ACT.Copy).then_inc(kept_act, 1)

            def body(j, last):
                for u in range(U):
                    if not last or u + 1 < U:
                        keep_turned(j, u + 1)
                    if u == U - 1:
                        act.wait_ge(o_done, j + 1)
                        act.activation(m.mixT[:, bass.ds(j, 1), 0:SEQ].rearrange("p a t -> p (a t)"), pb[6][:, :],
                                       ACT.Copy).then_inc(o_kept, 1)
                    if not last or u + AHEAD < U:
                        exponent(j, u + AHEAD)

            exponent(0, 0)
            act.wait_ge(c_step, 3)
            act.activation(m.cc, m.cc, ACT.Exp).then_inc(c_exp, 1)
            act.wait_ge(c_scored, 2)
            act.activation(m.vrep[0:64, :], pb[6][0:64, 0:P], ACT.Copy).then_inc(ct_ready, 1)
            exponent(0, 1)
            for v in range(2, AHEAD):
                exponent(0, v)
            keep_turned(0, 0)
            with act.Fori(0, HPG - 1) as j:
                body(j, False)
            body(HPG - 1, True)

        @block.vector
        def _(dve):
            def stage_queries(j, part):
                a = SEQ // 2 * (1 - part)
                dve.tensor_copy(m.qst[:, a:a + SEQ // 2], m.qT[:, bass.ds(j, 1), a:a + SEQ // 2]
                                .rearrange("p a t -> p (a t)")).then_inc(q_staged, 1)

            def stage_penalties(j):
                for g in range(2):
                    last = dve.tensor_scalar(m.pre[:, g, :], const(m, "negd"),
                                             const(m, "slopes")[:, bass.ds(j + HPG * g, 1)], None, ALU.mult)
                last.then_inc(pre_ready, 1)

            def stage_values(j):
                for g in range(2):
                    last = dve.tensor_scalar(m.vst[0:64, HD * g:HD * g + HD], m.vrep[0:64, HD * g:HD * g + HD],
                                             const(m, "hmask")[0:64, bass.ds(j + HPG * g, 1)], None, ALU.mult)
                last.then_inc(vst_staged, 1)

            def sums(j, v):
                w = width(v)
                if v % U == 0:
                    dve.wait_ge(pre_ready, j + (v // U + 1))
                dve.wait_ge(scored, j * U + (v + 1))
                if v >= 4:
                    dve.wait_ge(p_turned, j * U + (v - 3))
                hold(dve, m, v % U)
                for g in range(2):
                    last = dve.tensor_tensor_reduce(m.cp[v % 4][:, g, 0:w], m.pre[:, g, SEQ - w:SEQ],
                                                    pb[2 * (v % 2) + g][:, 0:w], 1.0, -3e38, ALU.add, ALU.max,
                                                    nm(v)[:, g:g + 1])
                last.then_inc(summed, 1)
                dve.wait_ge(summed, j * U + (v + 1))
                dve.tensor_scalar(nm(v), nm(v), -1.0, None, ALU.mult).then_inc(smax, 1)

            def factors(j, v):
                dve.wait_ge(exped, j * U + (v + 1))
                dve.reciprocal(su(v), su(v)).then_inc(rec, 1)
                dve.wait_ge(rec, j * U + (v + 1))
                a = NH * (1 + branch(v))
                gt = m.gates[:, tile(v), a:a + NH].rearrange("p (g h) -> p g h", g=2)[:, :, bass.ds(j + v // U, 1)]
                dve.tensor_tensor(su(v), su(v), gt.rearrange("p g a -> p (g a)"), ALU.mult).then_inc(scl_ready, 1)

            def keep_turned(j, v):
                dve.wait_ge(p_turned, j * U + (v + 1))
                dve.tensor_copy(m.cpT[v % 2][:, 0, 0:width(v)], pb[4][:, 0:width(v)]).then_inc(kept_dve, 1)

            def body(j, last):
                for u in range(U):
                    if not last or u + 1 < U:
                        keep_turned(j, u + 1)
                    if not last or u + AHEAD < U:
                        sums(j, u + AHEAD)
                    if not last or u + AHEAD - 1 < U:
                        factors(j, u + AHEAD - 1)
                    if not last and u == AHEAD - 1:
                        stage_queries(j + 1, 0)
                        stage_penalties(j + 1)
                    if not last and u == AHEAD:
                        dve.wait_ge(scored, j * U + U)
                        stage_queries(j + 1, 1)
                if not last:
                    dve.wait_ge(o_done, j + 1)
                    stage_values(j + 1)

            dve.wait_ge(sems.cleared, 3)
            for g in range(2):
                a = HD * g
                last = dve.tensor_copy(m.kc2[a:a + HD, PBLK * g:PBLK * g + PBLK], m.kcT[a:a + HD, KC0:KC0 + PBLK])
            last.then_inc(kc_ready, 1)
            for part in range(2):
                stage_queries(0, part)
            dve.tensor_tensor(cc4, const(m, "cmpd").rearrange("p (i n) -> p i n", n=PBLK).unsqueeze(2)
                              .broadcast_to(heads), const(m, "slopes").unsqueeze(1).unsqueeze(3).broadcast_to(heads),
                              ALU.mult).then_inc(c_ready, 1)
            stage_penalties(0)
            sums(0, 0)
            dve.wait_ge(c_ready, 1)
            dve.wait_ge(c_scored, 1)
            for g in range(2):
                c = cc4[:, :, HPG * g:HPG * g + HPG, :]
                last = dve.tensor_tensor(c, c, pb[7][:, 0:256].rearrange("p (i j g n) -> p g i j n", i=PTILES, j=HPG,
                                                                         g=2)[:, g], ALU.add)
            last.then_inc(c_step, 1)
            dve.wait_ge(c_step, 1)
            dve.tensor_reduce(per_head(cst), cc4, AX.X, ALU.max).then_inc(c_step, 1)
            dve.wait_ge(c_step, 2)
            dve.tensor_tensor(cc4, cc4, per_head(cst).unsqueeze(3).broadcast_to(heads), ALU.subtract)\
               .then_inc(c_step, 1)
            sums(0, 1)
            dve.wait_ge(c_exp, 1)
            dve.tensor_tensor(cc4, cc4, const(m, "cmpm").rearrange("p (i n) -> p i n", n=PBLK).unsqueeze(2)
                              .broadcast_to(heads), ALU.mult).then_inc(c_step, 1)
            dve.wait_ge(c_step, 4)
            dve.tensor_reduce(per_head(csum), cc4, AX.X, ALU.add).then_inc(c_step, 1)
            dve.wait_ge(c_step, 5)
            dve.tensor_scalar(csum, csum, 1e-30, None, ALU.max).then_inc(c_step, 1)
            factors(0, 0)
            dve.wait_ge(c_step, 6)
            dve.reciprocal(csum, csum).then_inc(c_step, 1)
            sums(0, 2)
            dve.wait_ge(c_step, 7)
            dve.tensor_tensor(per_head(csum), per_head(csum), m.gates[:, 0:PTILES, 0:NH], ALU.mult)\
               .then_inc(c_step, 1)
            factors(0, 1)
            dve.wait_ge(c_step, 8)
            dve.tensor_tensor(cc4, cc4, per_head(csum).unsqueeze(3).broadcast_to(heads), ALU.mult)\
               .then_inc(c_ready, 1)
            sums(0, 3)
            factors(0, 2)
            dve.wait_ge(c_turned, 1)
            dve.tensor_copy(m.ccT[0:64, :], pb[7][0:64, :]).then_inc(ct_ready, 1)
            keep_turned(0, 0)
            dve.wait_ge(ct_ready, 2)
            stage_values(0)
            with dve.Fori(0, HPG - 1) as j:
                body(j, False)
            body(HPG - 1, True)

        @block.tensor
        def _(pe):
            def scores(j, v):
                i, w = tile(v), width(v)
                if v % U in (0, 4):
                    pe.wait_ge(q_staged, (j + v // U) * 2 + (1 + (v % U) // 4))
                if v >= 2:
                    pe.wait_ge(summed, j * U + (v - 1))
                for g in range(2):
                    a = HD * g
                    last = pe.matmul(pb[2 * (v % 2) + g][:, 0:w], m.qst[a:a + HD, P * i:P * i + P],
                                     m.kT[a:a + HD, branch(v), 0:w], start=True, stop=True)
                last.then_inc(scored, 1)

            def turn(j, v):
                pe.wait_ge(scaled, j * U + (v + 1))
                if v >= 1:
                    pe.wait_ge(kept_dve, j * U + v)
                    pe.wait_ge(kept_act, j * U + v)
                for g in range(2):
                    for k in range(tile(v) + 1):
                        last = pe.transpose(pb[4 + g][:, P * k:P * k + P], m.cp[v % 4][:, g, P * k:P * k + P], ident)
                last.then_inc(p_turned, 1)

            def values(j, u):
                i, br = tile(u), branch(u)
                pe.wait_ge(kept_dve, j * U + (u + 1))
                pe.wait_ge(kept_act, j * U + (u + 1))
                if u == 0:
                    pe.wait_ge(o_kept, j + 1)
                if u == 1:
                    pe.wait_ge(vst_staged, j + 1)
                out = lambda g: pb[6][HD * g:HD * g + HD, P * i:P * i + P]
                for k in range(i + 1):
                    for g in range(2):
                        last = pe.matmul(out(g), values_at(m, k, br)[:, HD * g:HD * g + HD],
                                         m.cpT[u % 2][:, g, P * k:P * k + P], start=(br == 0 and k == 0), stop=False,
                                         skip_group_check=True)
                if br == 1:
                    for g in range(2):
                        last = pe.matmul(out(g), m.vst[0:64, HD * g:HD * g + HD], m.ccT[0:64, P * i:P * i + P],
                                         start=False, stop=True, skip_group_check=True)
                if u == U - 1:
                    last.then_inc(o_done, 1)

            def body(j, last):
                for u in range(U):
                    values(j, u)
                    if not last or u + 1 < U:
                        turn(j, u + 1)
                    if not last or u + AHEAD < U:
                        scores(j, u + AHEAD)

            scores(0, 0)
            scores(0, 1)
            pe.wait_ge(kc_ready, 1)
            for i in range(PTILES):
                for j in range(HPG):
                    a = 64 * i + 16 * j
                    last = pe.matmul(pb[7][:, a:a + 16], m.qT[:, j, P * i:P * i + P], m.kc2, start=True, stop=True)
            last.then_inc(c_scored, 1)
            pe.matmul(pb[6][0:64, 0:P], const(m, "spread8")[0:PBLK, :], m.vc[0:PBLK, NB_SEQ, :], start=True, stop=True)\
              .then_inc(c_scored, 1)
            for v in range(2, AHEAD):
                scores(0, v)
            pe.wait_ge(c_ready, 2)
            for i in range(PTILES):
                last = pe.transpose(pb[7][0:64, P * i:P * i + P], m.cc[:, 64 * i:64 * i + 64], ident)
            last.then_inc(c_turned, 1)
            pe.sem_inc(o_kept, 1)
            turn(0, 0)
            pe.wait_ge(vst_staged, 1)
            with pe.Fori(0, HPG - 1) as j:
                body(j, False)
            body(HPG - 1, True)


def sample(nc, m, sems, sem):
    pb = m.pb
    ident = const(m, "ident")
    NPAIR = NB_SEQ // 2
    big_in, g_mm, g_step, gates_kept, qs_ready = (
        sem("big_in"), sem("g_mm"), sem("g_step"), sem("gates_kept"), sem("qs_ready"))
    n_scored, scored = sem("sn_scored"), sem("s_scored")
    packed = {e: sem(f"packed_{e}") for e in ("act", "dve", "pool")}
    k_turned, k_kept = sem("k_turned"), sem("k_kept")
    c_step, c_exp, p_cmp, imp_mm, sel_step, selb_ready, pre_ready = (
        sem("sc_step"), sem("sc_exp"), sem("p_cmp"), sem("imp_mm"), sem("sel_step"), sem("selb_ready"),
        sem("s_pre_ready"))
    rank, win_summed, summed, mx_ready, exped = sem("rank"), sem("win_summed"), sem("s_summed"), sem("mx_ready"), sem("s_exped")
    p_turned, pt_act, pt_dve, v_done = sem("s_p_turned"), sem("pt_act"), sem("pt_dve"), sem("v_done")
    f_step, o_step, merged, o_turned, o_kept = (
        sem("f_step"), sem("o_step"), sem("merged"), sem("so_turned"), sem("so_kept"))
    sm = m.small
    cmax, cneg, csum = sm[:, 0:1], sm[:, 1:2], sm[:, 2:3]
    mx = lambda n: sm[:, 8 + 8 * (n % 2):16 + 8 * (n % 2)]
    nmx = lambda n: sm[:, 24 + 2 * (n % 2):26 + 2 * (n % 2)]
    ssum = lambda n: sm[:, 28 + 2 * (n % 2):30 + 2 * (n % 2)]
    NSL = PAST + NS
    WIN0 = NSL
    CMP0 = NSL + WINDOW + NS
    ORDER = (0, 4, 1, 2, 3)
    X = len(ORDER)
    UN = 2 * X
    VN = X + 1
    PACKER = ("act", "act", "act", "dve", "pool", "dve", "act", "pool", "dve", "act")
    SMALL, IMP, OT = 0, 160, 192
    C_STEPS, SEL_STEPS, F_STEPS, O_STEPS = 3, 5, 2, 2

    def pack(eng, n, u):
        x, e = ORDER[u // 2], u % 2
        if e == 0 or PACKER[u - 1] != PACKER[u]:
            if x < 4:
                eng.wait_ge(sems.slc_in[n % 2][x], 32 * (n // 2 + 1))
            else:
                eng.wait_ge(sems.win_in[n % 2], 32 * (n // 2 + 1))
        if UN * n + u >= 3:
            eng.wait_ge(k_turned, UN * n + u - 2)
        dst = m.kst[(UN * n + u) % 3].rearrange("p (a d) -> p a d", d=HD)
        src = m.slot[2 * (n % 2) + e][:, x].rearrange("p q (g k) -> p (q g) k", g=NKV)[:, :, 0:HD]
        if PACKER[u] == "act":
            eng.activation(dst, src, ACT.Copy).then_inc(packed["act"], 1)
        else:
            eng.tensor_copy(dst, src).then_inc(packed[PACKER[u]], 1)

    def count_packed(n, u):
        return n * PACKER.count(PACKER[u]) + PACKER[:u + 1].count(PACKER[u])

    with nc.Block() as block:
        @block.sync
        def _(sp):
            sp.dma_start(m.big, m.c_big).then_inc(big_in, 16)
            for n in range(2, NPAIR):
                sp.wait_ge(v_done, VN * (n - 2) + 2)
                for e in range(2):
                    load_window(sp, m, 2 * (n % 2) + e, 2 * n + e, sems)
            sp.wait_ge(v_done, VN * (NPAIR - 2) + X)
            for s in range(2):
                load_w_out(sp, m, sems, s)

        @block.gpsimd
        def _(pool):
            pool.memset(m.qs, 0.0).then_inc(sems.cleared, 1)
            for n in range(NPAIR):
                for u in range(UN):
                    if PACKER[u] == "pool":
                        pack(pool, n, u)
                pool.wait_ge(big_in, 16)
                pool.wait_ge(selb_ready, n + 1)
                if n >= 2:
                    pool.wait_ge(p_turned, VN * (n - 1))
                for x in range(4):
                    pool.tensor_tensor(
                        m.sp[n % 2][:, 512 * x:512 * x + 512].rearrange("p (m b q) -> p m b q", m=4, b=8),
                        bigconst(m, "s_slc")[:, 512 * x:512 * x + 512].rearrange("p (m b q) -> p m b q", m=4, b=8),
                        m.selb[:, 8 * x:8 * x + 8].unsqueeze(1).unsqueeze(3).broadcast_to([P, 4, 8, 16]),
                        ALU.add).then_inc(pre_ready, 1)
                if 1 <= n < NPAIR - 1:
                    for i, x in enumerate(ORDER):
                        if x < 4:
                            pool.wait_ge(v_done, VN * (n - 1) + i + 1)
                            for e in range(2):
                                load_pages(pool, m, n + 1, e, x, sems)

        @block.scalar
        def _(act):
            act.wait_ge(g_mm, 1)
            act.activation(m.imp_g, pb[0][:, 0:96], ACT.Copy).then_inc(gates_kept, 1)

            def keep_keys(n, u):
                act.wait_ge(k_turned, n * UN + u + 1)
                act.activation(m.skT[(UN * n + u) % 4], pb[6 + u % 2][:, :], ACT.Copy).then_inc(k_kept, 1)

            def keep_output(n):
                act.wait_ge(o_turned, n + 1)
                for g in range(2):
                    a = HD * g
                    last = act.activation(
                        m.mixT[a:a + HD, 0:HPG, SEQ + 2 * DEC * n:SEQ + 2 * DEC * (n + 1)]
                        .rearrange("p h (e t) -> p e h t", e=2),
                        pb[5][a:a + HD, OT:OT + P].rearrange("p (e g h t) -> p e g h t", e=2, g=2, h=HPG)[:, :, g],
                        ACT.Copy)
                last.then_inc(o_kept, 1)

            def exponents(n):
                act.wait_ge(mx_ready, n + 1)
                act.activation(m.sp[n % 2][:, 0:NSL], m.sp[n % 2][:, 0:NSL], ACT.Exp, bias=nmx(n)[:, 0:1],
                               accum_out=ssum(n)[:, 0:1])
                act.activation(m.sp[n % 2][:, WIN0:CMP0], m.sp[n % 2][:, WIN0:CMP0], ACT.Exp, bias=nmx(n)[:, 1:2],
                               accum_out=ssum(n)[:, 1:2]).then_inc(exped, 1)

            for n in range(NPAIR + 1):
                if n < NPAIR:
                    for u in range(3 if n != 1 else 0):
                        pack(act, n, u)
                    for u in range(UN):
                        if u == 1:
                            act.wait_ge(c_step, n * C_STEPS + 2)
                            act.activation(m.sp[n % 2][:, CMP0:CMP0 + NBLK], m.sp[n % 2][:, CMP0:CMP0 + NBLK], ACT.Exp,
                                           bias=cneg, accum_out=csum).then_inc(c_exp, 1)
                        if n != 1 or u >= 2:
                            keep_keys(n, u)
                        if u + 3 < UN and PACKER[u + 3] == "act":
                            pack(act, n, u + 3)
                    if n >= 2:
                        keep_output(n - 2)
                if n >= 1:
                    for i in range(3):
                        act.wait_ge(p_turned, VN * (n - 1) + i + 1)
                        if VN * (n - 1) + i >= 3:
                            act.wait_ge(v_done, VN * (n - 1) + i - 2)
                        act.activation(m.spT[i % 3], pb[6 + i % 2][:, :], ACT.Copy).then_inc(pt_act, 1)
                if n < NPAIR:
                    if n == 0:
                        for u in range(3):
                            pack(act, 1, u)
                        for u in range(2):
                            keep_keys(1, u)
                    exponents(n)
            for n in range(NPAIR - 2, NPAIR):
                keep_output(n)

        @block.vector
        def _(dve):
            dve.wait_ge(sems.cleared, 4)
            for g in range(NKV):
                a = HD * g
                last = dve.tensor_copy(
                    m.qs[a:a + HD, :].rearrange("p (b g h t) -> p b g h t", b=NB_SEQ, g=NKV, h=HPG)[:, :, g],
                    m.qT[a:a + HD, :, SEQ:TOK].rearrange("p h (b t) -> p b h t", b=NB_SEQ))
            last.then_inc(qs_ready, 1)
            dve.wait_ge(gates_kept, 1)
            gt12 = m.imp_g.rearrange("p (a r h) -> p (a r) h", a=NPAIR, r=3)
            dve.tensor_tensor(gt12, gt12, const(m, "headrow").unsqueeze(1).broadcast_to([P, 12, NH]), ALU.mult)\
               .then_inc(g_step, 1)
            dve.wait_ge(g_step, 1)
            dve.tensor_reduce(m.grow[:, :], gt12, AX.X, ALU.add).then_inc(g_step, 1)
            dve.wait_ge(g_step, 2)

            def small_scores(n):
                cmpp, s_new = m.sp[n % 2][:, CMP0:CMP0 + NBLK], const(m, "s_new")[:, NS * n:NS * n + NS]
                dve.wait_ge(n_scored, n + 1)
                dve.tensor_tensor_reduce(cmpp, const(m, "s_cmp"), pb[5][:, 128:160], 1.0, -3e38, ALU.add, ALU.max,
                                         cmax).then_inc(c_step, 1)
                dve.wait_ge(c_step, n * C_STEPS + 1)
                dve.tensor_scalar(cneg, cmax, -1.0, None, ALU.mult).then_inc(c_step, 1)
                dve.tensor_tensor_reduce(m.sp[n % 2][:, PAST:NSL], s_new, pb[5][:, 0:NS], 1.0, -3e38, ALU.add,
                                         ALU.max, mx(n)[:, 4:5])
                dve.tensor_tensor_reduce(m.sp[n % 2][:, WIN0 + WINDOW:CMP0], s_new, pb[5][:, NS:2 * NS], 1.0, -3e38,
                                         ALU.add, ALU.max, mx(n)[:, 6:7])

            def compressed(n):
                cmpp = m.sp[n % 2][:, CMP0:CMP0 + NBLK]
                dve.wait_ge(c_exp, n + 1)
                dve.reciprocal(csum, csum).then_inc(c_step, 1)
                dve.wait_ge(c_step, n * C_STEPS + 3)
                dve.tensor_scalar(cmpp, cmpp, csum, None, ALU.mult).then_inc(p_cmp, 1)

            def select(n):
                dve.wait_ge(imp_mm, n + 1)
                dve.tensor_copy(m.imp, pb[5][:, IMP:IMP + NBLK]).then_inc(sel_step, 1)
                dve.wait_ge(sel_step, n * SEL_STEPS + 1)
                dve.memset(m.imp[:, 0:NBLK:NBLK - 1], FORCE).then_inc(sel_step, 1)
                dve.wait_ge(sel_step, n * SEL_STEPS + 2)
                shape = [P, 2, NBLK // 2, NBLK]
                ib = m.imp.unsqueeze(1).unsqueeze(1).broadcast_to(shape)
                ia = m.imp.rearrange("p (c a) -> p c a", c=2).unsqueeze(3).broadcast_to(shape)
                if n:
                    dve.wait_ge(rank, n)
                dve.tensor_tensor(m.gt, ib, ia, ALU.is_gt)
                dve.tensor_tensor(m.eq, ib, ia, ALU.is_equal).then_inc(sel_step, 1)
                pack(dve, n, 8)
                dve.wait_ge(big_in, 16)
                dve.wait_ge(sel_step, n * SEL_STEPS + 3)
                dve.tensor_tensor(m.eq, m.eq, bigconst(m, "before").rearrange("p (c a b) -> p c a b", c=2, b=NBLK),
                                  ALU.mult).then_inc(sel_step, 1)
                dve.wait_ge(sel_step, n * SEL_STEPS + 4)
                dve.tensor_tensor(m.gt, m.gt, m.eq, ALU.add).then_inc(sel_step, 1)
                dve.wait_ge(sel_step, n * SEL_STEPS + 5)
                if n:
                    dve.wait_ge(pre_ready, 4 * n)
                dve.tensor_reduce(m.selb.rearrange("p (c a) -> p c a", c=2), m.gt, AX.X, ALU.add)\
                   .then_inc(rank, 1)
                dve.wait_ge(rank, n + 1)
                dve.tensor_scalar(m.selb, m.selb, N_SELECT - 1.5, NEG, ALU.is_ge, ALU.mult).then_inc(selb_ready, 1)

            def merge(n):
                dve.wait_ge(exped, n + 1)
                dve.reciprocal(ssum(n), ssum(n)).then_inc(f_step, 1)
                dve.wait_ge(f_step, n * F_STEPS + 1)
                dve.tensor_tensor(ssum(n), ssum(n), m.grow[:, 3 * n + 1:3 * n + 3], ALU.mult).then_inc(f_step, 1)
                dve.wait_ge(f_step, n * F_STEPS + 2)
                dve.wait_ge(v_done, VN * (n + 1))
                if n:
                    dve.wait_ge(o_turned, n)
                dve.tensor_scalar(m.o_sb, pb[4][:, 0:P], ssum(n)[:, 0:1], None, ALU.mult).then_inc(o_step, 1)
                for k, f in enumerate((ssum(n)[:, 1:2], m.grow[:, 3 * n:3 * n + 1])):
                    dve.wait_ge(o_step, n * O_STEPS + k + 1)
                    dve.scalar_tensor_tensor(out=m.o_sb, in0=pb[4][:, P * (k + 1):P * (k + 2)], scalar=f,
                                             in1=m.o_sb, op0=ALU.mult, op1=ALU.add)\
                       .then_inc(o_step if k == 0 else merged, 1)

            for n in range(NPAIR + 1):
                if n < NPAIR:
                    small_scores(n)
                    pack(dve, n, 3)
                    compressed(n)
                    pack(dve, n, 5)
                    select(n)
                    dve.wait_ge(scored, X * n + 2)
                    dve.tensor_tensor_reduce(m.sp[n % 2][:, WIN0:WIN0 + WINDOW], bigconst(m, "s_win"), pb[4][:, :],
                                             1.0, -3e38, ALU.add, ALU.max, mx(n)[:, 5:6]).then_inc(win_summed, 1)
                    for x in range(4):
                        dve.wait_ge(pre_ready, n * 4 + x + 1)
                        dve.wait_ge(scored, X * n + ORDER.index(x) + 1)
                        a = 512 * x
                        dve.tensor_tensor_reduce(m.sp[n % 2][:, a:a + 512], m.sp[n % 2][:, a:a + 512], pb[x][:, :],
                                                 1.0, -3e38, ALU.add, ALU.max, mx(n)[:, x:x + 1]).then_inc(summed, 1)
                    dve.wait_ge(win_summed, n + 1)
                    dve.wait_ge(summed, 4 * n + 4)
                    dve.tensor_reduce(nmx(n)[:, 0:1], mx(n)[:, 0:5], AX.X, ALU.max, negate=True)
                    dve.tensor_reduce(nmx(n)[:, 1:2], mx(n)[:, 5:7], AX.X, ALU.max, negate=True).then_inc(mx_ready, 1)
                if n >= 1:
                    for i in range(3, VN):
                        dve.wait_ge(p_turned, VN * (n - 1) + i + 1)
                        dve.wait_ge(v_done, VN * (n - 1) + i - 2)
                        if i < X:
                            dve.tensor_copy(m.spT[i % 3], pb[6 + i % 2][:, :]).then_inc(pt_dve, 1)
                        else:
                            dve.tensor_copy(m.spX[0:NS, 0:256], pb[6 + i % 2][0:NS, 0:256])
                            dve.tensor_copy(m.spX[0:NBLK, 256:384], pb[6 + i % 2][0:NBLK, 256:384])\
                               .then_inc(pt_dve, 1)
                    merge(n - 1)

        @block.tensor
        def _(pe):
            for n in range(NPAIR):
                last = pe.matmul(pb[0][:, 24 * n:24 * n + 24], const(m, "tokrow")[0:NS, P * n:P * n + P],
                                 m.gates[0:NS, PTILES, :], start=True, stop=True)
            last.then_inc(g_mm, 1)
            pe.wait_ge(qs_ready, 1)

            def queries(n, e):
                return m.qs[:, HD * (2 * n + e):HD * (2 * n + e + 1)]

            def small_scores(n):
                if n:
                    pe.wait_ge(sel_step, (n - 1) * SEL_STEPS + 1)
                if n >= 3:
                    pe.wait_ge(o_kept, n - 2)
                for e in range(2):
                    b, rows_e = 2 * n + e, slice(HD * e, HD * e + HD)
                    pe.matmul(pb[5][rows_e, 128:160], queries(n, e), m.kcT[:, NBLK * b:NBLK * (b + 1)],
                              start=True, stop=True)
                    for br in range(2):
                        last = pe.matmul(pb[5][rows_e, NS * br:NS * br + NS], queries(n, e), m.kT[:, br, SEQ:TOK],
                                         start=True, stop=True)
                last.then_inc(n_scored, 1)

            def turn_keys(n, u):
                pe.wait_ge(packed[PACKER[u]], count_packed(n, u))
                if UN * n + u >= 2:
                    pe.wait_ge(k_kept, n * UN + u - 1)
                if n >= 2 and u < 2:
                    pe.wait_ge(pt_dve, 3 * (n - 1))
                for mm in range(QUAD):
                    last = pe.transpose(pb[6 + u % 2][:, P * mm:P * mm + P],
                                        m.kst[(UN * n + u) % 3][:, P * mm:P * mm + P], ident)
                last.then_inc(k_turned, 1)

            def scores(n, i):
                x = ORDER[i]
                pe.wait_ge(k_kept, n * UN + 2 * i + 2)
                if n == 0 and i == 0:
                    pe.wait_ge(gates_kept, 1)
                if x < 4 and n:
                    pe.wait_ge(summed, 4 * (n - 1) + x + 1)
                if x == 4 and n:
                    pe.wait_ge(win_summed, n)
                if x == 4 and n >= 2:
                    pe.wait_ge(merged, n - 1)
                for e in range(2):
                    last = pe.matmul(pb[x][64 * e:64 * e + 64, :], queries(n, e), m.skT[(UN * n + 2 * i + e) % 4],
                                     start=True, stop=True)
                last.then_inc(scored, 1)

            def turn_output(n):
                pe.wait_ge(merged, n + 1)
                if n:
                    pe.wait_ge(o_kept, n)
                pe.transpose(pb[5][:, OT:OT + P], m.o_sb, ident).then_inc(o_turned, 1)

            def turn_probs(n, i):
                if i == 0:
                    pe.wait_ge(exped, n + 1)
                    pe.wait_ge(k_kept, UN * min(n + 2, NPAIR))
                if i in (2, 3, 4):
                    pe.wait_ge(pt_act, 3 * n + i - 1)
                if i == 5:
                    pe.wait_ge(pt_dve, 3 * n + 1)
                if i < X:
                    a = 512 * ORDER[i] if ORDER[i] < 4 else WIN0
                    for mm in range(QUAD):
                        last = pe.transpose(pb[6 + i % 2][:, P * mm:P * mm + P],
                                            m.sp[n % 2][:, a + P * mm:a + P * mm + P], ident)
                else:
                    pe.transpose(pb[6 + i % 2][0:NBLK, 2 * P:3 * P], m.sp[n % 2][:, CMP0:CMP0 + NBLK], ident)
                    pe.transpose(pb[6 + i % 2][0:NS, 0:P], m.sp[n % 2][:, PAST:NSL], ident)
                    last = pe.transpose(pb[6 + i % 2][0:NS, P:2 * P], m.sp[n % 2][:, WIN0 + WINDOW:CMP0], ident)
                last.then_inc(p_turned, 1)

            def values(n, i):
                if i < 3:
                    pe.wait_ge(pt_act, 3 * n + i + 1)
                else:
                    pe.wait_ge(pt_dve, 3 * n + i - 2)
                if i == 0:
                    pe.wait_ge(win_summed, min(n + 2, NPAIR))
                    if n:
                        pe.wait_ge(merged, n)
                out = lambda e, r: pb[4][64 * e:64 * e + 64, P * r:P * r + P]
                for mm in range(QUAD if i < X else 0):
                    for e in range(2):
                        last = pe.matmul(out(e, int(ORDER[i] == 4)).rearrange("p (g d) -> p g d", g=NKV),
                                         m.spT[i % 3][:, P * mm + 64 * e:P * mm + 64 * e + 64],
                                         m.slot[2 * (n % 2) + e][:, ORDER[i], mm, :]
                                         .rearrange("p (g k) -> p g k", g=NKV)[:, :, HD:2 * HD],
                                         start=(i == 0 and mm == 0), stop=False, skip_group_check=True)
                if i == X:
                    for e in range(2):
                        pe.matmul(out(e, 2), m.spX[0:NBLK, 2 * P + 64 * e:2 * P + 64 * e + 64], m.vc[:, 2 * n + e, :],
                                  start=False, stop=False, skip_group_check=True)
                        for br in range(2):
                            last = pe.matmul(out(e, br), m.spX[0:NS, P * br + 64 * e:P * br + 64 * e + 64],
                                             values_at(m, PTILES, br, NS), start=False, stop=(br == 1),
                                             skip_group_check=True)
                last.then_inc(v_done, 1)

            for n in range(NPAIR + 1):
                if n < NPAIR:
                    small_scores(n)
                    for i in range(X + 1):
                        if i < X:
                            turn_keys(n, 2 * i)
                            turn_keys(n, 2 * i + 1)
                        if i == 1:
                            pe.wait_ge(p_cmp, n + 1)
                            pe.matmul(pb[5][:, IMP:IMP + NBLK], const(m, "headsum"),
                                      m.sp[n % 2][:, CMP0:CMP0 + NBLK], start=True, stop=True).then_inc(imp_mm, 1)
                        if i >= 1:
                            scores(n, i - 1)
                    if n >= 2:
                        pe.wait_ge(sel_step, n * SEL_STEPS + 1)
                        turn_output(n - 2)
                if n >= 1:
                    for i in range(VN + 1):
                        if i < VN:
                            turn_probs(n - 1, i)
                        if i >= 1:
                            values(n - 1, i - 1)
                        if i == 1 and n == NPAIR:
                            turn_output(n - 2)
            turn_output(NPAIR - 1)


def load_w_out(eng, m, sems, s):
    dst = m.raw_w[s]
    src = m.w_out[0][:, 512 * s:512 * s + 512]
    for g in range(2):
        eng.dma_start(dst[HD * g:HD * g + HD, 0:HPG, :],
                      src[256 * g:256 * g + 256, :].rearrange("(j d) n -> d j n", d=HD)).then_inc(sems.ring_in[s], 16)
    eng.dma_start(dst[:, HPG:KT_D, :], src[512:D, :].rearrange("(k p) n -> p k n", p=P)).then_inc(sems.ring_in[s], 16)


def mlp(nc, m, sems, sem):
    pb = m.pb
    ident = const(m, "ident")
    gf_in = sem("gf_in")
    xh_ready, xl_ready, wh_ready, wl_ready = sem("xh_ready"), sem("xl_ready"), sem("wh_ready"), sem("wl_ready")
    unit_mm, kept = sem("unit_mm"), sem("kept")
    sq_ready, sq_added, ssq_mm, var_ready, std_ready, rb_ready = (
        sem("sq_ready"), sem("sq_added"), sem("ssq_mm"), sem("m_var"), sem("m_std"), sem("rb_ready"))
    a_ready, ah_ready, al_ready = sem("a_ready"), sem("ah_ready"), sem("al_ready")
    y_turned, y_sq, y_var, y_std, y_part, y_done = (
        sem("y_turned"), sem("y_sq"), sem("y_var"), sem("y_std"), sem("y_part"), sem("y_done"))
    y_out = sem("y_out")
    g_mlp = m.cols[:, 8:16]
    ysum = lambda i: m.small[:, 16 + 2 * i:18 + 2 * i]
    yv = lambda i: m.small[:, 32 + i:33 + i]
    W0 = 48
    NQ, UQ = 4, 16
    FIRST = KT_D
    UNITS = FIRST + NQ * UQ
    MIX_ORDER = [4, 5, 6, 7, 0, 1, 2, 3]
    out = lambda r, hf: pb[2 * (r % 2) + hf][:, 0:HALF]
    half = lambda v, hf: v[:, HALF * hf:HALF * hf + HALF]
    sqsum = m.relu[0]

    with nc.Block() as block:
        @block.sync
        def _(sp):
            sp.dma_start(m.gfin, m.g_final.rearrange("(o d) -> o d", o=1).broadcast_to([P, D])).then_inc(gf_in, 16)
            for q in range(NQ):
                for down in range(2):
                    for s in range(2):
                        t = 2 + 4 * q + 2 * down + s
                        sp.wait_ge(wl_ready, 4 * (t - 1))
                        if down:
                            src = m.w_down[0][1024 * q:1024 * q + 1024, 512 * s:512 * s + 512]
                        else:
                            src = m.w_up[0][:, 1024 * q + 512 * s:1024 * q + 512 * s + 512]
                        sp.dma_start(m.raw_w[s], src.rearrange("(k p) n -> p k n", p=P)).then_inc(sems.ring_in[s], 16)
            for i in range(TILES):
                sp.wait_ge(y_done, i + 1)
                if i < PTILES:
                    sp.dma_start(m.o_yp[0, P * i:P * i + P, :], m.yo[i]).then_inc(y_out, 16)
                else:
                    sp.dma_start(m.o_ys.rearrange("b t d -> (b t) d"), m.yo[i][0:NS, :]).then_inc(y_out, 16)
            sp.wait_ge(y_out, 16 * TILES)

        @block.gpsimd
        def _(pool):
            for n in range(1, KT_D - 1):
                pool.wait_ge(sq_ready, n + 1)
                if n > 1:
                    pool.wait_ge(sq_added, n - 1)
                pool.tensor_tensor(sqsum, sqsum, m.sq[n % 2], ALU.add).then_inc(sq_added, 1)

        def wcols(t, k):
            return t[:, k % 4, :].rearrange("p (k n) -> p k n", k=KT_D)

        def raw_cols(n):
            return m.raw_w[(n // 4) % 2][:, :, P * (n % 4):P * (n % 4) + P]

        @block.scalar
        def _(act):
            def split(i, base=0, loaded=W0):
                if i % 4 == 0:
                    act.wait_ge(sems.ring_in[(i // 4) % 2], loaded + 16 * (i // 8))
                act.activation(wcols(m.wh, i), raw_cols(i), ACT.Copy).then_inc(wh_ready, 1)

            split(0)
            for k in MIX_ORDER:
                act.activation(m.xh[:, k, :], m.mixT[:, k, :], ACT.Copy).then_inc(xh_ready, 1)
            split(1)
            split(2)
            for n in range(FIRST):
                if n:
                    act.wait_ge(unit_mm, n)
                split(n + 3)
                act.wait_ge(kept, n + 1)
                if n >= 3:
                    act.wait_ge(sq_added, n - 2)
                act.activation(m.sq[n % 2] if n else sqsum, m.hT[:, n, :], ACT.Square).then_inc(sq_ready, 1)
            for k in range(KT_D):
                act.activation(m.xh[:, k, :], m.hT[:, k, :], ACT.Identity, scale=g_mlp[:, k:k + 1])\
                   .then_inc(xh_ready, 1)
            act.wait_ge(var_ready, 1)
            act.activation(m.rb, m.var, ACT.Sqrt).then_inc(std_ready, 1)

            def quarter(q, last):
                for i in range(UQ):
                    n = q * UQ + (FIRST + i)
                    if i < 8:
                        f = q * 8 + i
                        act.wait_ge(kept, n + 1)
                        act.activation(m.act[i % 2], m.relu[i % 2], ACT.Square).then_inc(a_ready, 1)
                        act.wait_ge(a_ready, f + 1)
                        act.activation(m.ah[:, i, :], m.act[i % 2], ACT.Copy).then_inc(ah_ready, 1)
                    if not (last and i + 3 >= UQ):
                        act.wait_ge(unit_mm, n)
                        split(i + 3, q * UQ + FIRST, q * 32 + (W0 + 16))

            with act.Fori(0, NQ - 1) as q:
                quarter(q, False)
            quarter(NQ - 1, True)
            for i in range(TILES + 1):
                if i < TILES:
                    n = rows(i)
                    act.wait_ge(y_turned, i + 1)
                    if i:
                        act.wait_ge(y_sq, i)
                    for hf in range(2):
                        last = act.activation(m.sq[hf][0:n, 0:512], pb[2 * (i % 4) + hf][0:n, :], ACT.Square,
                                              accum_out=ysum(i)[0:n, hf:hf + 1])
                    last.then_inc(y_sq, 1)
                if i:
                    n = rows(i - 1)
                    act.wait_ge(y_var, i)
                    act.activation(yv(i - 1)[0:n, :], yv(i - 1)[0:n, :], ACT.Sqrt).then_inc(y_std, 1)

        @block.vector
        def _(dve):
            def split(i, base=0):
                dve.wait_ge(wh_ready, base + (i + 1))
                dve.tensor_tensor(wcols(m.wl, i), raw_cols(i), wcols(m.wh, i).bitcast(F32), ALU.subtract)\
                   .then_inc(wl_ready, 1)

            split(0)
            for c, k in enumerate(MIX_ORDER):
                dve.wait_ge(xh_ready, c + 1)
                dve.tensor_tensor(m.xl[:, k, :], m.mixT[:, k, :], m.xh[:, k, :].bitcast(F32), ALU.subtract)\
                   .then_inc(xl_ready, 1)
            split(1)
            for n in range(FIRST):
                split(n + 2)
                dve.wait_ge(unit_mm, n + 1)
                for hf in range(2):
                    last = dve.tensor_tensor(half(m.hT[:, n, :], hf), out(n, hf), half(m.hT[:, n, :], hf), ALU.add)
                last.then_inc(kept, 1)
            for n in range(FIRST):
                dve.wait_ge(xh_ready, KT_D + n + 1)
                dve.scalar_tensor_tensor(out=m.xl[:, n, :], in0=m.hT[:, n, :], scalar=g_mlp[:, n:n + 1],
                                         in1=m.xh[:, n, :].bitcast(F32), op0=ALU.mult, op1=ALU.subtract)\
                   .then_inc(xl_ready, 1)
            dve.wait_ge(ssq_mm, 1)
            for hf in range(2):
                last = dve.tensor_scalar(half(m.var, hf), pb[6 + hf][:, 0:HALF], 1.0 / D, EPS, ALU.mult, ALU.add)
            last.then_inc(var_ready, 1)
            dve.wait_ge(std_ready, 1)
            dve.reciprocal(m.rb, m.rb).then_inc(rb_ready, 1)
            dve.wait_ge(rb_ready, 1)

            def quarter(q, last):
                for i in range(UQ):
                    n = q * UQ + (FIRST + i)
                    dve.wait_ge(unit_mm, n + 1)
                    for hf in range(2):
                        if i < 8:
                            op = dve.scalar_tensor_tensor(out=half(m.relu[i % 2], hf), in0=out(i, hf), scalar=0.0,
                                                          in1=half(m.rb, hf), op0=ALU.max, op1=ALU.mult)
                        else:
                            h = half(m.hT[:, i - 8, :], hf)
                            op = dve.tensor_tensor(h, out(i, hf), h, ALU.add)
                    op.then_inc(kept, 1)
                    if not (last and i + 2 >= UQ):
                        split(i + 2, q * UQ + FIRST)
                    if i < 8:
                        dve.wait_ge(ah_ready, q * 8 + (i + 1))
                        dve.tensor_tensor(m.al[:, i, :], m.act[i % 2], m.ah[:, i, :].bitcast(F32), ALU.subtract)\
                           .then_inc(al_ready, 1)

            with dve.Fori(0, NQ - 1) as q:
                quarter(q, False)
            quarter(NQ - 1, True)
            dve.wait_ge(gf_in, 16)
            for i in range(TILES):
                n = rows(i)
                dve.wait_ge(y_sq, i + 1)
                dve.tensor_tensor(yv(i)[0:n, :], ysum(i)[0:n, 0:1], ysum(i)[0:n, 1:2], ALU.add).then_inc(y_part, 1)
                dve.wait_ge(y_part, 2 * i + 1)
                dve.tensor_scalar(yv(i)[0:n, :], yv(i)[0:n, :], 1.0 / D, EPS, ALU.mult, ALU.add).then_inc(y_var, 1)
                dve.wait_ge(y_std, i + 1)
                dve.reciprocal(yv(i)[0:n, :], yv(i)[0:n, :]).then_inc(y_part, 1)
                dve.wait_ge(y_part, 2 * i + 2)
                for hf in range(2):
                    last = dve.scalar_tensor_tensor(out=m.yo[i][0:n, 512 * hf:512 * hf + 512],
                                                    in0=pb[2 * (i % 4) + hf][0:n, :], scalar=yv(i)[0:n, :],
                                                    in1=m.gfin[0:n, 512 * hf:512 * hf + 512], op0=ALU.mult,
                                                    op1=ALU.mult)
                last.then_inc(y_done, 1)

        @block.tensor
        def _(pe):
            def product(i, k, xh, xl, first, end):
                w = (wcols(m.wh, i)[:, k, :], wcols(m.wl, i)[:, k, :])
                for part, (wi, x) in enumerate(((0, xh), (0, xl), (1, xh))):
                    for hf in range(2):
                        last = pe.matmul(out(i, hf), w[wi], half(x[:, k, :], hf), start=first and part == 0,
                                         stop=end and part == 2)
                return last

            for n in range(FIRST):
                pe.wait_ge(wl_ready, n + 1)
                if n >= 2:
                    pe.wait_ge(kept, n - 1)
                for c, k in enumerate(MIX_ORDER):
                    if n == 0:
                        pe.wait_ge(xl_ready, c + 1)
                    last = product(n, k, m.xh, m.xl, c == 0, c == KT_D - 1)
                last.then_inc(unit_mm, 1)
            pe.wait_ge(sq_added, KT_D - 2)
            for hf in range(2):
                pe.matmul(pb[6 + hf][:, 0:HALF], m.ones[:, :], half(sqsum, hf), start=True, stop=False)
            pe.wait_ge(sq_ready, KT_D)
            for hf in range(2):
                last = pe.matmul(pb[6 + hf][:, 0:HALF], m.ones[:, :], half(m.sq[(KT_D - 1) % 2], hf), start=False,
                                 stop=True)
            last.then_inc(ssq_mm, 1)
            with pe.Fori(0, NQ) as q:
                for down in range(2):
                    with pe.Fori(0, 2) as s:
                        for r in range(4):
                            n = q * UQ + s * 4 + (FIRST + 8 * down + r)
                            pe.wait_ge(wl_ready, n + 1)
                            pe.wait_ge(kept, n - 1)
                            for k in range(KT_D):
                                if r == 0 and not down:
                                    pe.wait_ge(xl_ready, KT_D + k + 1)
                                if r == 0 and down:
                                    pe.wait_ge(al_ready, q * 8 + (k + 1))
                                last = product(r, k, m.ah if down else m.xh, m.al if down else m.xl, k == 0,
                                               k == KT_D - 1)
                            last.then_inc(unit_mm, 1)
            pe.wait_ge(kept, UNITS)
            for i in range(TILES):
                n = rows(i)
                if i >= 4:
                    pe.wait_ge(y_done, i - 3)
                for k in range(KT_D):
                    last = pe.transpose(pb[2 * (i % 4) + k // 4][0:n, P * (k % 4):P * (k % 4) + P],
                                        m.hT[:, k, P * i:P * i + n], ident)
                last.then_inc(y_turned, 1)


INPUTS = ["x_prompt", "x_sample", "cache_cmp", "cache_slc", "state_win", "state_pool", "page_table", "g_attn", "w_in",
          "cmp_pe", "cmp_w1", "cmp_w2", "w_pool", "pool_scale", "w_out", "g_mlp", "w_up", "w_down", "g_final"]
OUTPUTS = [("o_yp", (1, SEQ, D)), ("o_ys", (NB_SEQ, DEC, D)),
           ("o_pcmp", (1, 1, SEQ, NKV, 2, HD)), ("o_pslc", (1, 1, SEQ, NKV, 2, HD)),
           ("o_pwin", (1, 1, SEQ, NKV, 2, HD)), ("o_ppool", (1, 1, HIST, 512)),
           ("o_scmp", (1, NB_SEQ, DEC, NKV, 2, HD)), ("o_sslc", (1, NB_SEQ, DEC, NKV, 2, HD)),
           ("o_swin", (1, NB_SEQ, WINDOW, NKV, 2, HD)), ("o_spool", (1, NB_SEQ, HIST, 512))]


def build(nc, m):
    with ExitStack() as ctx:
        place(nc, ctx, m)

        def sem(name):
            return ctx.enter_context(nc.semaphore(name))

        sems = Mem()
        sems.const_in, sems.wpool_in, sems.w2_in = sem("const_in"), sem("wpool_in"), sem("w2_in")
        sems.cleared = sem("cleared")
        sems.raw_in = [sem("raw_in0"), sem("raw_in1")]
        sems.slc_in = [[sem(f"slc_in{q}_{x}") for x in range(4)] for q in range(2)]
        sems.win_in = [sem("win_in0"), sem("win_in1")]
        sems.ring_in = [sem("ring_in0"), sem("ring_in1")]
        with ExitStack() as attention:
            place_attention(nc, attention, m)
            m.imp_g = m.spX[:, 0:96]
            project(nc, m, sems, sem)
            compress(nc, m, sems, sem)
            prompt(nc, m, sems, sem)
            sample(nc, m, sems, sem)
        with ExitStack() as last:
            place_mlp(nc, last, m)
            mlp(nc, m, sems, sem)


def kernel(**inputs):
    import concourse.bacc as _bacc
    from concourse.bass_utils import run_bass_kernel_spmd as _run

    nc = _bacc.Bacc("TRN2", target_bir_lowering=False, num_devices=1)
    arrays, m = {}, Mem()
    for name in INPUTS:
        a = np.ascontiguousarray(inputs[name])
        arrays[f"in_{name}"] = a
        ap = nc.dram_tensor(f"in_{name}", a.shape, mybir.dt.from_np(a.dtype), kind="ExternalInput").ap()
        m.__dict__["w_in_d" if name == "w_in" else name] = ap
    for name, group in zip(("c_small", "c_big"), tables()):
        a = np.ascontiguousarray(np.concatenate(list(group.values()), axis=1))
        arrays[name] = a
        m.__dict__[name] = nc.dram_tensor(name, a.shape, F32, kind="ExternalInput").ap()
    for name, shape in OUTPUTS:
        m.__dict__[name] = nc.dram_tensor(name, shape, F32, kind="ExternalOutput").ap()
    build(nc, m)
    r = _run(nc, [arrays], core_ids=[0])
    return tuple(r.results[0][name] for name, _ in OUTPUTS)
```
